# Optimizing a Trainium2 kernel written in Bass

```python
import math
import jax, jax.numpy as jnp
from jax import lax
import numpy as np

D_MODEL = 1024
BATCH = 1
SEQ = 512
DEPTH = 2

N_MIXERS = 2
N_HEADS = 4
QK_DIM = D_MODEL // (2 * N_HEADS)
V_DIM = D_MODEL // N_HEADS
CHUNK = 128
GATE_CAP = 15.0
CONV_WIDTH = 3
D_FF = 4 * D_MODEL
EPS = 1e-6
N_MLSTM_LAYERS = (DEPTH + 1) // 2
N_CONV_LAYERS = DEPTH // 2
QK_COLS = N_HEADS * QK_DIM
MLSTM_IN = 2 * QK_COLS + 2 * D_MODEL + 2 * N_HEADS
CONV_IN = 3 * D_MODEL


def rms_norm(x, g):
    xf = x.astype(jnp.float32)
    y = xf * lax.rsqrt(jnp.mean(xf * xf, axis=-1, keepdims=True) + EPS)
    return (y * g.astype(jnp.float32)).astype(x.dtype)

def mlstm_mixer(x, w_in, b_gates, g_hnorm, w_out):
    B_, S, _ = x.shape
    nc = S // CHUNK
    proj = x @ w_in
    q, k, v, o, gates = jnp.split(
        proj, [QK_COLS, 2 * QK_COLS, 2 * QK_COLS + D_MODEL, 2 * QK_COLS + 2 * D_MODEL], axis=-1)
    f32 = jnp.float32
    q = q.astype(f32).reshape(B_, S, N_HEADS, QK_DIM).transpose(0, 2, 1, 3)
    k = (k.astype(f32) * (QK_DIM ** -0.5)).reshape(B_, S, N_HEADS, QK_DIM).transpose(0, 2, 1, 3)
    v = v.astype(f32).reshape(B_, S, N_HEADS, V_DIM).transpose(0, 2, 1, 3)
    gates = gates.astype(f32) + b_gates.astype(f32)
    gates = GATE_CAP * jnp.tanh(gates / GATE_CAP)
    ig = gates[..., :N_HEADS].transpose(0, 2, 1)
    logf = jax.nn.log_sigmoid(gates[..., N_HEADS:]).transpose(0, 2, 1)

    qc = q.reshape(B_, N_HEADS, nc, CHUNK, QK_DIM)
    kc = k.reshape(B_, N_HEADS, nc, CHUNK, QK_DIM)
    vc = v.reshape(B_, N_HEADS, nc, CHUNK, V_DIM)
    igc = ig.reshape(B_, N_HEADS, nc, CHUNK)
    bcum = jnp.cumsum(logf.reshape(B_, N_HEADS, nc, CHUNK), axis=-1)
    b_last = bcum[..., -1]

    log_w = b_last[..., None] - bcum + igc
    m_loc = jnp.max(log_w, axis=-1)
    w = jnp.exp(log_w - m_loc[..., None])
    kv_loc = jnp.einsum('bhcl,bhcld,bhcle->bhcde', w, kc, vc)
    n_loc = jnp.einsum('bhcl,bhcld->bhcd', w, kc)

    def step(carry, inp):
        C, n, m = carry
        bl, ml, kvl, nl = inp
        m_new = jnp.maximum(bl + m, ml)
        a = jnp.exp(bl + m - m_new)
        s = jnp.exp(ml - m_new)
        C_new = a[..., None, None] * C + s[..., None, None] * kvl
        n_new = a[..., None] * n + s[..., None] * nl
        return (C_new, n_new, m_new), (C, n, m)

    init = (jnp.zeros((B_, N_HEADS, QK_DIM, V_DIM), f32),
            jnp.zeros((B_, N_HEADS, QK_DIM), f32),
            jnp.zeros((B_, N_HEADS), f32))
    xs = (jnp.moveaxis(b_last, 2, 0), jnp.moveaxis(m_loc, 2, 0),
          jnp.moveaxis(kv_loc, 2, 0), jnp.moveaxis(n_loc, 2, 0))
    _, (C_prev, n_prev, m_prev) = lax.scan(step, init, xs)
    C_prev = jnp.moveaxis(C_prev, 0, 2)
    n_prev = jnp.moveaxis(n_prev, 0, 2)
    m_prev = jnp.moveaxis(m_prev, 0, 2)

    causal = jnp.tril(jnp.ones((CHUNK, CHUNK), dtype=bool))
    logD = bcum[..., :, None] - bcum[..., None, :] + igc[..., None, :]
    logD = jnp.where(causal, logD, -jnp.inf)
    log_inter = bcum + m_prev[..., None]
    m_t = jnp.maximum(jnp.max(logD, axis=-1), log_inter)
    Dm = jnp.exp(logD - m_t[..., None])
    scores = jnp.einsum('bhcld,bhcsd->bhcls', qc, kc) * Dm
    inter = jnp.exp(log_inter - m_t)
    num = (jnp.einsum('bhcls,bhcse->bhcle', scores, vc)
           + inter[..., None] * jnp.einsum('bhcld,bhcde->bhcle', qc, C_prev))
    den = jnp.sum(scores, axis=-1) + inter * jnp.einsum('bhcld,bhcd->bhcl', qc, n_prev)
    h = num / jnp.maximum(jnp.abs(den), jnp.exp(-m_t))[..., None]

    h = h.reshape(B_, N_HEADS, S, V_DIM).transpose(0, 2, 1, 3)
    h = h * lax.rsqrt(jnp.mean(h * h, axis=-1, keepdims=True) + EPS)
    h = h * g_hnorm.astype(f32).reshape(N_HEADS, V_DIM)
    h = jax.nn.sigmoid(o.astype(f32)) * h.reshape(B_, S, D_MODEL)
    return h.astype(x.dtype) @ w_out

def short_conv_mixer(x, w_in, w_conv, w_out):
    proj = x @ w_in
    bgate, cgate, xh = jnp.split(proj, 3, axis=-1)
    u = cgate * xh
    conv = lax.conv_general_dilated(
        u, w_conv[:, None, :].astype(u.dtype), window_strides=(1,),
        padding=[(CONV_WIDTH - 1, 0)],
        dimension_numbers=('NWC', 'WIO', 'NWC'),
        feature_group_count=D_MODEL)
    return (bgate * conv) @ w_out

def sqrelu_mlp(x, w_up, w_down):
    h = jax.nn.relu(x @ w_up)
    return (h * h) @ w_down

def first_inputs(seed: int = 0) -> dict:
    key = jax.random.key(seed)
    ks = jax.random.split(key, 12)
    f32 = jnp.float32
    x = jax.random.normal(ks[0], (BATCH, SEQ, D_MODEL), f32)
    norm_g = 1.0 + 0.05 * jax.random.normal(ks[1], (DEPTH, 4, D_MODEL), f32)
    w_in_mlstm = jax.random.normal(ks[2], (N_MLSTM_LAYERS, D_MODEL, MLSTM_IN), f32) * D_MODEL ** -0.5
    i_bias = -3.0 + 0.1 * jax.random.normal(ks[3], (N_MLSTM_LAYERS, N_HEADS), f32)
    f_bias = (jnp.linspace(3.0, 6.0, N_HEADS, dtype=f32)[None, :]
              + 0.1 * jax.random.normal(ks[4], (N_MLSTM_LAYERS, N_HEADS), f32))
    b_gates_mlstm = jnp.concatenate([i_bias, f_bias], axis=-1)
    g_hnorm = 1.0 + 0.05 * jax.random.normal(ks[5], (N_MLSTM_LAYERS, D_MODEL), f32)
    w_out_mlstm = jax.random.normal(ks[6], (N_MLSTM_LAYERS, D_MODEL, D_MODEL), f32) * D_MODEL ** -0.5
    w_in_conv = jax.random.normal(ks[7], (N_CONV_LAYERS, D_MODEL, CONV_IN), f32) * D_MODEL ** -0.5
    w_conv = jax.random.normal(ks[8], (N_CONV_LAYERS, CONV_WIDTH, D_MODEL), f32) * CONV_WIDTH ** -0.5
    w_out_conv = jax.random.normal(ks[9], (N_CONV_LAYERS, D_MODEL, D_MODEL), f32) * D_MODEL ** -0.5
    w_mlp_up = jax.random.normal(ks[10], (DEPTH, D_MODEL, D_FF), f32) * D_MODEL ** -0.5
    w_mlp_down = jax.random.normal(ks[11], (DEPTH, D_FF, D_MODEL), f32) * D_FF ** -0.5
    return {"x": x, "norm_g": norm_g, "w_in_mlstm": w_in_mlstm, "b_gates_mlstm": b_gates_mlstm,
            "g_hnorm": g_hnorm, "w_out_mlstm": w_out_mlstm, "w_in_conv": w_in_conv,
            "w_conv": w_conv, "w_out_conv": w_out_conv, "w_mlp_up": w_mlp_up,
            "w_mlp_down": w_mlp_down}

def first_block(x, norm_g, w_in_mlstm, b_gates_mlstm, g_hnorm, w_out_mlstm, w_in_conv,
              w_conv, w_out_conv, w_mlp_up, w_mlp_down):
    for i in range(DEPTH):
        g = norm_g[i]
        j = i // N_MIXERS
        h = rms_norm(x, g[0])
        if i % N_MIXERS == 0:
            h = mlstm_mixer(h, w_in_mlstm[j], b_gates_mlstm[j], g_hnorm[j], w_out_mlstm[j])
        else:
            h = short_conv_mixer(h, w_in_conv[j], w_conv[j], w_out_conv[j])
        x = x + rms_norm(h, g[1])
        h = sqrelu_mlp(rms_norm(x, g[2]), w_mlp_up[i], w_mlp_down[i])
        x = x + rms_norm(h, g[3])
    return x


DEPTH_2 = 1

GRID_W = 64
CTX_LEN = 256

H_A = 8
KV_A = 2
G_A = H_A // KV_A
DH_A = 64
WINDOW = 128
BLOCK = 128
BAND = BLOCK + 2 * WINDOW

H_B = 8
NOPE_B = 64
ROPE_B = 32
V_B = 64
Q_RANK = 384
KV_RANK = 256
MLA_SCALE = (NOPE_B + ROPE_B) ** -0.5

W_QA = H_A * DH_A
W_KA = KV_A * DH_A
W_VA = KV_A * DH_A
IN_WIDTHS = (W_QA, W_KA, W_VA, Q_RANK, KV_RANK, ROPE_B)
IN_DIM = sum(IN_WIDTHS)
SPLIT_POINTS = tuple(int(v) for v in np.cumsum(IN_WIDTHS)[:-1])
MIX_DIM = H_A * DH_A + H_B * V_B

N_EXPERTS = 16
CAP_FACTOR = 2
D_FF_2 = 512

ROPE_BASE = 10000.0


def rmsnorm(x, w):
    xf = x.astype(jnp.float32)
    y = xf * lax.rsqrt(jnp.mean(xf * xf, axis=-1, keepdims=True) + EPS)
    return (y * w.astype(jnp.float32)).astype(x.dtype)

def modulate(h, shift, scale):
    return h * (1 + scale) + shift

def axial_rope(x, rows, cols):
    d = x.shape[-1]
    da = d // 2
    nf = da // 2
    inv = ROPE_BASE ** (-jnp.arange(nf, dtype=jnp.float32) / nf)

    def rot(xa, pos):
        ang = pos.astype(jnp.float32)[:, None] * inv[None, :]
        cos = jnp.cos(ang)[None, :, None, :]
        sin = jnp.sin(ang)[None, :, None, :]
        x1, x2 = xa[..., :nf], xa[..., nf:]
        return jnp.concatenate([x1 * cos - x2 * sin, x1 * sin + x2 * cos], axis=-1)

    xf = x.astype(jnp.float32)
    out = jnp.concatenate([rot(xf[..., :da], rows), rot(xf[..., da:], cols)], axis=-1)
    return out.astype(x.dtype)

def gqa_sink_attend(qb, keys, vals, bias, sink_g):
    s = jnp.einsum('bqkgd,bskd->bkgqs', qb, keys, preferred_element_type=jnp.float32) * (DH_A ** -0.5)
    if bias is not None:
        s = s + bias
    b, q = qb.shape[0], qb.shape[1]
    s_sink = jnp.broadcast_to(sink_g.astype(jnp.float32)[None, :, :, None, None], (b, KV_A, G_A, q, 1))
    p = jax.nn.softmax(jnp.concatenate([s, s_sink], axis=-1), axis=-1)[..., :-1]
    o = jnp.einsum('bkgqs,bskd->bqkgd', p.astype(vals.dtype), vals)
    return o.reshape(b, q, H_A * DH_A)

def window_attention_latent(q, k, v, kc, vc, sink_g):
    b, s_len = q.shape[:2]
    lc = kc.shape[1]
    nb = s_len // BLOCK
    qg = q.reshape(b, s_len, KV_A, G_A, DH_A)
    pad = ((0, 0), (WINDOW, WINDOW), (0, 0), (0, 0))
    kp = jnp.pad(k, pad)
    vp = jnp.pad(v, pad)
    ctx_bias = jnp.zeros((BLOCK, lc), jnp.float32)

    def block(i):
        start = i * BLOCK
        qb = lax.dynamic_slice_in_dim(qg, start, BLOCK, axis=1)
        kb = lax.dynamic_slice_in_dim(kp, start, BAND, axis=1)
        vb = lax.dynamic_slice_in_dim(vp, start, BAND, axis=1)
        tq = start + jnp.arange(BLOCK)
        ts = start - WINDOW + jnp.arange(BAND)
        valid = (jnp.abs(tq[:, None] - ts[None, :]) <= WINDOW) & (ts[None, :] >= 0) & (ts[None, :] < s_len)
        band_bias = jnp.where(valid, 0.0, -jnp.inf).astype(jnp.float32)
        keys = jnp.concatenate([kc, kb], axis=1)
        vals = jnp.concatenate([vc, vb], axis=1)
        bias = jnp.concatenate([ctx_bias, band_bias], axis=1)
        return gqa_sink_attend(qb, keys, vals, bias, sink_g)

    out = lax.map(block, jnp.arange(nb))
    return jnp.transpose(out, (1, 0, 2, 3)).reshape(b, s_len, H_A * DH_A)

def mla_attend(qn, qr, kn, kr, v):
    s = (jnp.einsum('bqhd,bkhd->bhqk', qn, kn, preferred_element_type=jnp.float32)
         + jnp.einsum('bqhr,bkr->bhqk', qr, kr, preferred_element_type=jnp.float32)) * MLA_SCALE
    p = jax.nn.softmax(s, axis=-1)
    o = jnp.einsum('bhqk,bkhd->bqhd', p.astype(v.dtype), v)
    return o.reshape(qn.shape[0], qn.shape[1], H_B * V_B)

def mla_latent(qn, qr, kn, kr, v):
    b, s_len = qn.shape[:2]
    nb = s_len // BLOCK

    def block(i):
        start = i * BLOCK
        qnb = lax.dynamic_slice_in_dim(qn, start, BLOCK, axis=1)
        qrb = lax.dynamic_slice_in_dim(qr, start, BLOCK, axis=1)
        return mla_attend(qnb, qrb, kn, kr, v)

    out = lax.map(block, jnp.arange(nb))
    return jnp.transpose(out, (1, 0, 2, 3)).reshape(b, s_len, H_B * V_B)

def project_groups(t, w_in, q_norm, kv_norm, w_q_up, w_kv_up):
    bt, n = t.shape[:2]
    p = jnp.einsum('bsd,de->bse', t, w_in)
    qa, ka, va, cq, ckv, kr = jnp.split(p, SPLIT_POINTS, axis=-1)
    qa = qa.reshape(bt, n, H_A, DH_A)
    ka = ka.reshape(bt, n, KV_A, DH_A)
    va = va.reshape(bt, n, KV_A, DH_A)
    qb = jnp.einsum('bsr,re->bse', rmsnorm(cq, q_norm), w_q_up).reshape(bt, n, H_B, NOPE_B + ROPE_B)
    kvb = jnp.einsum('bsr,re->bse', rmsnorm(ckv, kv_norm), w_kv_up).reshape(bt, n, H_B, NOPE_B + V_B)
    return (qa, ka, va, qb[..., :NOPE_B], qb[..., NOPE_B:], kr,
            kvb[..., :NOPE_B], kvb[..., NOPE_B:])

def token_mixers(h, hc, rows, cols, w_in, sink, q_norm, kv_norm, w_q_up, w_kv_up, w_out, with_ctx_out):
    sink_g = sink.reshape(KV_A, G_A)
    qa, ka, va, qbn, qbr, kr, kbn, vb = project_groups(h, w_in, q_norm, kv_norm, w_q_up, w_kv_up)
    qa_c, ka_c, va_c, qbn_c, qbr_c, kr_c, kbn_c, vb_c = project_groups(hc, w_in, q_norm, kv_norm, w_q_up, w_kv_up)
    qa = axial_rope(qa, rows, cols)
    ka = axial_rope(ka, rows, cols)
    qbr = axial_rope(qbr, rows, cols)
    kr = axial_rope(kr[:, :, None, :], rows, cols)[:, :, 0, :]
    o_a = window_attention_latent(qa, ka, va, ka_c, va_c, sink_g)
    o_b = mla_latent(qbn, qbr,
                     jnp.concatenate([kbn_c, kbn], axis=1),
                     jnp.concatenate([kr_c, kr], axis=1),
                     jnp.concatenate([vb_c, vb], axis=1))
    out = jnp.einsum('bse,ed->bsd', jnp.concatenate([o_a, o_b], axis=-1), w_out)
    if not with_ctx_out:
        return out, None
    lc = hc.shape[1]
    o_a_c = gqa_sink_attend(qa_c.reshape(hc.shape[0], lc, KV_A, G_A, DH_A), ka_c, va_c, None, sink_g)
    o_b_c = mla_attend(qbn_c, qbr_c, kbn_c, kr_c, vb_c)
    out_c = jnp.einsum('bse,ed->bsd', jnp.concatenate([o_a_c, o_b_c], axis=-1), w_out)
    return out, out_c

def ec_moe(h, w_router, w_gate, w_up, w_down):
    n = h.shape[1]
    cap = CAP_FACTOR * n // N_EXPERTS
    aff = jax.nn.softmax(jnp.einsum('bnd,de->bne', h, w_router, preferred_element_type=jnp.float32), axis=-1)
    vals, idx = lax.top_k(jnp.swapaxes(aff, 1, 2), cap)

    def per_sample(hs, idx_s, val_s):
        xs = hs[idx_s]
        a = jnp.einsum('ecd,edf->ecf', xs, w_gate)
        u = jnp.einsum('ecd,edf->ecf', xs, w_up)
        y = jnp.einsum('ecf,efd->ecd', jax.nn.silu(a) * u, w_down) * val_s[..., None].astype(hs.dtype)
        return jnp.zeros_like(hs).at[idx_s.reshape(-1)].add(y.reshape(-1, hs.shape[-1]).astype(hs.dtype))

    return jax.vmap(per_sample)(h, idx, vals)

def second_inputs(seed: int = 0) -> dict:
    key = jax.random.key(seed)
    ks = jax.random.split(key, 20)
    f32 = jnp.float32
    L = DEPTH_2

    def nrm(k, shape, scale):
        return jax.random.normal(k, shape, f32) * scale

    return {
        "x": nrm(ks[0], (BATCH, SEQ, D_MODEL), 1.0),
        "c": nrm(ks[1], (BATCH, D_MODEL), 1.0),
        "ctx": nrm(ks[2], (BATCH, CTX_LEN, D_MODEL), 1.0),
        "c_ctx": nrm(ks[3], (D_MODEL,), 1.0),
        "w_mod": nrm(ks[4], (L, D_MODEL, 6 * D_MODEL), 0.5 * D_MODEL ** -0.5),
        "b_mod": nrm(ks[5], (L, 6 * D_MODEL), 0.01),
        "norm_attn": 1.0 + nrm(ks[6], (L, D_MODEL), 0.02),
        "norm_ffn": 1.0 + nrm(ks[7], (L, D_MODEL), 0.02),
        "w_in": nrm(ks[8], (L, D_MODEL, IN_DIM), D_MODEL ** -0.5),
        "sink": nrm(ks[9], (L, H_A), 0.5),
        "q_norm": 1.0 + nrm(ks[10], (L, Q_RANK), 0.02),
        "kv_norm": 1.0 + nrm(ks[11], (L, KV_RANK), 0.02),
        "w_q_up": nrm(ks[12], (L, Q_RANK, H_B * (NOPE_B + ROPE_B)), Q_RANK ** -0.5),
        "w_kv_up": nrm(ks[13], (L, KV_RANK, H_B * (NOPE_B + V_B)), KV_RANK ** -0.5),
        "w_out": nrm(ks[14], (L, MIX_DIM, D_MODEL), MIX_DIM ** -0.5),
        "w_router": nrm(ks[15], (L, D_MODEL, N_EXPERTS), D_MODEL ** -0.5),
        "w_gate": nrm(ks[16], (L, N_EXPERTS, D_MODEL, D_FF_2), D_MODEL ** -0.5),
        "w_up": nrm(ks[17], (L, N_EXPERTS, D_MODEL, D_FF_2), D_MODEL ** -0.5),
        "w_down": nrm(ks[18], (L, N_EXPERTS, D_FF_2, D_MODEL), D_FF_2 ** -0.5),
        "norm_final": 1.0 + nrm(ks[19], (D_MODEL,), 0.02),
    }

def second_block(x, c, ctx, c_ctx, w_mod, b_mod, norm_attn, norm_ffn, w_in, sink, q_norm, kv_norm,
              w_q_up, w_kv_up, w_out, w_router, w_gate, w_up, w_down, norm_final):
    n_lat = x.shape[1]
    ROWS = n_lat // GRID_W
    rows = jnp.repeat(jnp.arange(ROWS, dtype=jnp.int32), GRID_W)
    cols = jnp.tile(jnp.arange(GRID_W, dtype=jnp.int32), ROWS)
    xc = ctx
    for l in range(DEPTH_2):
        last = l == DEPTH_2 - 1
        mod = jnp.einsum('bd,de->be', jax.nn.silu(c), w_mod[l]) + b_mod[l]
        mod_c = jnp.einsum('d,de->e', jax.nn.silu(c_ctx), w_mod[l]) + b_mod[l]
        sh_a, sc_a, g_a, sh_f, sc_f, g_f = [m[:, None, :] for m in jnp.split(mod, 6, axis=-1)]
        csh_a, csc_a, cg_a, csh_f, csc_f, cg_f = jnp.split(mod_c, 6, axis=-1)

        h = modulate(rmsnorm(x, norm_attn[l]), sh_a, sc_a)
        hc = modulate(rmsnorm(xc, norm_attn[l]), csh_a, csc_a)
        mix, mix_c = token_mixers(h, hc, rows, cols, w_in[l], sink[l], q_norm[l], kv_norm[l],
                                  w_q_up[l], w_kv_up[l], w_out[l], not last)
        x = x + g_a * mix
        h2 = modulate(rmsnorm(x, norm_ffn[l]), sh_f, sc_f)
        x = x + g_f * ec_moe(h2, w_router[l], w_gate[l], w_up[l], w_down[l])

        if not last:
            xc = xc + cg_a * mix_c
            h2c = modulate(rmsnorm(xc, norm_ffn[l]), csh_f, csc_f)
            xc = xc + cg_f * ec_moe(h2c, w_router[l], w_gate[l], w_up[l], w_down[l])
    return rmsnorm(x, norm_final)


def setup_inputs(seed=0):
    out = dict(first_inputs(seed))
    for name, value in second_inputs(seed + 1).items():
        if name != "x":
            out[name + "_2"] = value
    return out


def reference(
    x, norm_g, w_in_mlstm, b_gates_mlstm, g_hnorm, w_out_mlstm, w_in_conv, w_conv, w_out_conv,
    w_mlp_up, w_mlp_down, c_2, ctx_2, c_ctx_2, w_mod_2, b_mod_2, norm_attn_2, norm_ffn_2,
    w_in_2, sink_2, q_norm_2, kv_norm_2, w_q_up_2, w_kv_up_2, w_out_2, w_router_2, w_gate_2,
    w_up_2, w_down_2, norm_final_2,
):
    x = first_block(
        x, norm_g, w_in_mlstm, b_gates_mlstm, g_hnorm, w_out_mlstm, w_in_conv, w_conv,
        w_out_conv, w_mlp_up, w_mlp_down,
    )
    return second_block(
        x, c_2, ctx_2, c_ctx_2, w_mod_2, b_mod_2, norm_attn_2, norm_ffn_2, w_in_2, sink_2,
        q_norm_2, kv_norm_2, w_q_up_2, w_kv_up_2, w_out_2, w_router_2, w_gate_2, w_up_2,
        w_down_2, norm_final_2,
    )


_drawn_inputs = setup_inputs


def setup_inputs(seed=0):
    import zlib

    import numpy as np

    out = dict(_drawn_inputs(seed))
    spreads = {}
    factors = {'ctx_2': 7.424,
     'c_ctx_2': 3.073,
     'b_mod_2': 8.0,
     'norm_attn_2': 8.0,
     'norm_ffn_2': 8.0,
     'sink_2': 8.0,
     'q_norm_2': 8.0,
     'kv_norm_2': 8.0,
     'w_q_up_2': 6.826}
    for name, (base, spread) in spreads.items():
        noise = np.random.default_rng([zlib.crc32(name.encode()), seed]).standard_normal(out[name].shape)
        drawn = base * np.exp(spread * noise) if base else spread * noise
        out[name] = __import__('jax').numpy.asarray(drawn.astype(out[name].dtype))
    for name, factor in factors.items():
        out[name] = (out[name] * factor).astype(out[name].dtype)
    return out
```

```python
import contextlib

import numpy as np

import concourse.bass as bass
from concourse import mybir

F32 = mybir.dt.float32
F32R = mybir.dt.float32r
BF16 = mybir.dt.bfloat16
ALU = mybir.AluOpType
ACT = mybir.ActivationFunctionType
AX = mybir.AxisListType

P = 128
TOK = 512
NQ = TOK // P
CTX = 256
D = 1024
KT = D // P
HEADS = 4
VT = D // HEADS // P
EPS = 1e-6
GATE_CAP = 15.0
KSCALE = float(P) ** -0.5
RANK_Q, RANK_KV = 3, 2
KEYS = CTX + TOK
NE, CAP = 16, 64
PAIRS = NE // 2
FT = 4
BIG = 1e30

SLOT = KT * P
RING, SPLIT_RING, BANKS = 4, 2, 4

N_MOD = 48
G_GATES, G_QK, G_V, G_O = 0, 1, 9, 17
G_OUT0 = 25
G_MLP0 = 33
G_CONV = 97
G_OUT1 = 121
G_MLP1 = 129
G_IN2 = 193
G_VUP = 205
G_MLA = 206
G_OUT2 = 214
N_SPLIT = 222
N_MOE = 12 * NE
G_AHEAD = G_OUT0 + SPLIT_RING
T_MOD, T_MOE = G_AHEAD, N_MOD + N_SPLIT
N_TILES = T_MOE + N_MOE

COL = {}
_n = 0
for _name, _w in (("norm_g", 8 * KT), ("g_hnorm", KT), ("conv", 3 * KT), ("b_mod", 48), ("norm_attn", KT),
                  ("norm_ffn", KT), ("norm_final", KT), ("q_norm", RANK_Q), ("kv_norm", RANK_KV), ("c", 2 * KT),
                  ("sink", 8), ("b_i", 1), ("b_f", 1), ("eps", 1)):
    COL[_name] = _n
    _n += _w
NCOL = _n

NORMS = []


def _norm(tiles, width):
    base = NORMS[-1][0] + NORMS[-1][1] if NORMS else 0
    NORMS.append((base, tiles, width))
    return len(NORMS) - 1


N_PRE = {}
N_POST = {}
N_PRE["mix0"] = _norm(KT, TOK)
N_POST["mix0"] = _norm(KT, TOK)
N_PRE["mlp0"] = _norm(KT, TOK)
N_POST["mlp0"] = _norm(KT, TOK)
N_PRE["mix1"] = _norm(KT, TOK)
N_POST["mix1"] = _norm(KT, TOK)
N_PRE["mlp1"] = _norm(KT, TOK)
N_POST["mlp1"] = _norm(KT, TOK)
N_ATT = _norm(KT, TOK)
N_CTX = _norm(KT, CTX)
N_CKV_C = _norm(RANK_KV, CTX)
N_CKV = _norm(RANK_KV, TOK)
N_CQ = _norm(RANK_Q, TOK)
N_FFN = _norm(KT, TOK)
N_FINAL = _norm(KT, TOK)

PREP = {n: i for i, n in enumerate(("mix0", "out0", "mlp0", "mix1", "mlp1", "att", "out2"))}
HID = {"mlp0": 0, "mix1": 32, "mlp1": 40, "ctx": 72, "ckv_c": 80, "ckv": 82, "cq": 84}
POST_G = {"mix0": G_OUT0, "mlp0": G_MLP0 + 56, "mix1": G_OUT1, "mlp1": G_MLP1 + 56}
ROPE_A = [(i + 16) % 32 for i in range(32)]
ROPE_B = [i ^ 8 for i in range(32)]
SCALE_A, SCALE_B = 64 ** -0.5, 96 ** -0.5
WIN = CTX + 3 * P
MOE_STEP = 24


class At:

    def __init__(self, base, i=None, per=0):
        self.base, self.i, self.per = base, i, per

    def __add__(self, k):
        return At(self.base + k, self.i, self.per)

    def n(self, k=0):
        return self.base + k if self.i is None else self.i * self.per + (self.base + k)

    def place(self):
        return self.base + (N_MOD if self.base >= G_AHEAD else 0)

    def rounds(self):
        r = self.place() // RING + 1
        return r if self.i is None else self.i * (self.per // RING) + r


class Chain:

    def __init__(self, eng, sem):
        self.eng, self.sem, self.n, self.i, self.per = eng, sem, 0, None, 0

    def do(self, ins):
        ins.then_inc(self.sem, 1)
        self.n += 1
        return ins

    def sync(self):
        if self.i is None:
            if self.n:
                self.eng.wait_ge(self.sem, self.n)
        else:
            self.eng.wait_ge(self.sem, self.i * self.per + self.n)

    def link(self, ins):
        self.do(ins)
        self.sync()

    @contextlib.contextmanager
    def fori(self, count, per):
        start = self.n
        with self.eng.Fori(0, count) as i:
            self.i, self.per = i, per
            yield i
            assert self.n - start == per, f"{self.n - start} steps an iteration"
        self.i, self.per, self.n = None, 0, start + count * per

    @contextlib.contextmanager
    def inside(self, i, per):
        self.i, self.per, self.start = i, per, self.n
        yield
        assert self.n - self.start == per, f"{self.n - self.start} steps an iteration"

    def after(self, count):
        self.n, self.i = self.start + count * self.per, None


def build(nc, x, ctx_in, cols, ident_in, ones_in, sel_in, rope_in, mask_in, iota_in, tri_in, router_in, stream,
          out):
    with contextlib.ExitStack() as keep:
        def sb(name, shape, dt=F32):
            return keep.enter_context(nc.sbuf_tensor(name, shape, dt))

        res = sb("residual", [P, KT, TOK])
        raw = sb("raw_tiles", [P, RING, SLOT])
        w_hi = sb("w_hi", [P, SPLIT_RING, SLOT], F32R)
        w_lo = sb("w_lo", [P, SPLIT_RING, SLOT], F32R)
        act_hi = sb("act_hi", [P, KT, TOK], F32R)
        act_lo = sb("act_lo", [P, KT, TOK], F32R)
        hid_hi = sb("hid_hi", [P, KT, TOK], F32R)
        hid_lo = sb("hid_lo", [P, KT, TOK], F32R)
        ident = sb("ident", [P, P])
        ones = sb("ones", [P, P])
        sel = sb("sel", [HEADS, HEADS, P])
        col = sb("columns", [P, NCOL])
        row = sb("norm_row", [P, TOK])
        diag = sb("norm_diag", [P, NQ, P])
        small = sb("norm_small", [P, 2, NQ])
        sq = sb("squares", [P, 2, TOK])
        ssum = sb("square_sum", [P, TOK])
        tmp = sb("tmp", [P, 2, TOK])
        silu_c = sb("silu_c", [P, KT, 2])
        mod = sb("mod", [P, N_MOD, 2])
        gain = sb("gains", [P, 3, KT])
        ARENA = 19500
        arena = sb("arena", [P, ARENA])

        psum = keep.enter_context(nc.psum_tensor("banks", [P, 8, 512], F32))

        def view(at, *dims):
            n = int(np.prod(dims))
            assert at + n <= ARENA, (at, dims)
            v = arena[:, at:at + n]
            if len(dims) == 2:
                return v.rearrange("p (a b) -> p a b", b=dims[1])
            if len(dims) == 3:
                return v.rearrange("p (a b c) -> p a b c", b=dims[1], c=dims[2])
            return v

        qT, kT = view(0, HEADS, TOK), view(2048, HEADS, TOK)
        v_tok, o_sig, vT = view(4096, NQ, D), view(8192, KT, TOK), view(12288, KT, TOK)
        dec, wk, q_in, inter_s = (view(12288 + 512 * i, NQ, P) for i in range(4))
        num, num2 = view(14336, VT, TOK), view(15360, VT, TOK)
        rows_at = [16384 + 512 * i for i in range(6)]
        grow = [arena[0:HEADS, a:a + 512].rearrange("p (c l) -> p c l", l=P) for a in rows_at]
        state = view(16384, 3, 2 * P + 1)
        gcol = sb("gate_cols", [P, 2, NQ, HEADS])
        hsm = sb("head_small", [P, 6, NQ])
        gsm = sb("gate_small", [HEADS, 8])
        y = view(0, KT, TOK)
        halo = view(4096, 2, TOK + 2)
        cbuf = view(5200, 4, TOK)
        sqt = view(7400, 2, TOK)

        rope = view(0, 4, TOK)
        mask = view(2048, 3 * 3 * P // 2).bitcast(BF16).rearrange("p (a b) -> p a b", b=3 * P)
        ident_b = sb("ident_bf16", [P, P], BF16)
        qa, ka, va = view(3200, 4, TOK), view(5248, CTX + TOK + 2 * P), view(6272, 8, P)
        cq, ckv, kr = view(7296, RANK_Q, TOK), view(8832, RANK_KV, KEYS), view(10368, KEYS)
        o_tok = view(11136, NQ, D)
        ctx_x = view(15232, KT, CTX)
        turn_raw, turn_sh, va_t = view(17280, TOK), view(17792, TOK), view(18304, KEYS)
        prob, prob_t, q_stage = view(15232, 2, KEYS), view(16768, 2, KEYS), view(18304, TOK)
        vb, qh, kh = view(7296, 6, TOK), view(2048, 2, TOK), view(3072, 2, KEYS)
        soft = sb("softmax_small", [P, 6, 2])
        sink_neg = sb("sink_neg", [P, 8])
        xs, ye, h2 = view(0, KT, NE * CAP), view(8192, PAIRS, D), view(8192, KT, TOK)
        gate_s, h_e = view(16384, 2, FT * CAP), view(16896, 2, FT * CAP)
        aff_t = [arena[0:NE, 17408 + 512 * i:17920 + 512 * i] for i in range(2)]
        aff, aff_p, msk = view(18432, NQ, NE), view(18496, NQ, NE), view(18560, NQ, NE)
        val, e_small, iota, tri = view(18624, PAIRS), view(18640, 2, NQ), view(18656, CAP), view(18720, P)
        router = view(18848, KT, NE)
        top8 = sb("top8", [NE, 8])
        sel_t, sel_s = hid_lo, hid_hi
        latent_hi = hid_hi.rearrange("p a b -> p (a b)")[:, 3 * TOK:3 * TOK + 2 * KEYS].rearrange("p (a b) -> p a b", b=KEYS)
        latent_lo = hid_lo.rearrange("p a b -> p (a b)")[:, 3 * TOK:3 * TOK + 2 * KEYS].rearrange("p (a b) -> p a b", b=KEYS)

        def mine(bank, e):
            return psum[:, bank, :].rearrange("p (f e c) -> p f e c", e=2, c=CAP)[:, :, e, :]

        sems = {}

        def sem(name):
            if name not in sems:
                sems[name] = keep.enter_context(nc.semaphore(name))
            return sems[name]

        raw_in = [sem(f"raw_in_{s}") for s in range(RING)]
        mod_done, moe_done = sem("mod_done"), sem("moe_done")
        hi_done, lo_done, mm_done, tile_out = sem("hi_done"), sem("lo_done"), sem("mm_done"), sem("tile_out")
        sq_done, sq_added, msq_done, std_done = sem("sq_done"), sem("sq_added"), sem("msq_done"), sem("std_done")
        diag_ready, bc_done = sem("diag_ready"), sem("bc_done")
        a_hi, a_ready, h_hi, h_ready = sem("a_hi"), sem("a_ready"), sem("h_hi"), sem("h_ready")
        y_ready, x_ready = sem("y_ready"), sem("x_ready")
        const_in, x_in = sem("const_in"), [sem(f"x_in_{i}") for i in range(2)]
        out_in = [sem(f"out_{i}") for i in range(2)]

        def c(name, j=0):
            return col[:, COL[name] + j:COL[name] + j + 1]

        def normg(layer, which, j):
            return c("norm_g", (4 * layer + which) * KT + j)

        block = keep.enter_context(nc.Block())

        @block.sync
        def _(sp):
            n_const = 0
            for dst, src in ((col[:], cols), (ident[:], ident_in), (ones[:], ones_in), (sel[:], sel_in)):
                sp.dma_start(dst, src).then_inc(const_in, 16)
                n_const += 1
            for h in range(2):
                sp.dma_start(res[:, 4 * h:4 * h + 4, :], x[:, 4 * h:4 * h + 4, :]).then_inc(x_in[h], 16)

            def load(t, slot):
                sp.dma_start(raw[:, slot, :], stream[t]).then_inc(raw_in[slot], 16)

            for t in range(RING):
                load(t, t % RING)
            with sp.Fori(0, G_AHEAD // RING - 1) as i:
                for s in range(RING):
                    sp.wait_ge(lo_done, i * RING + (s + 1))
                    load(i * RING + (RING + s), s)
            for t in range(G_AHEAD // RING * RING, G_AHEAD + RING):
                sp.wait_ge(lo_done, t - RING + 1)
                load(t, t % RING)
            with sp.Fori(0, N_MOD // RING - 1) as i:
                for s in range(RING):
                    sp.wait_ge(mod_done, i * RING + (s + 1))
                    load(i * RING + (T_MOD + RING + s), (T_MOD + s) % RING)
            for s in range(RING):
                sp.wait_ge(mod_done, N_MOD - RING + s + 1)
                load(T_MOD + N_MOD + s, (T_MOD + s) % RING)
            rest = (N_SPLIT - G_AHEAD - RING) // RING
            with sp.Fori(0, rest) as i:
                for s in range(RING):
                    sp.wait_ge(lo_done, i * RING + (G_AHEAD + s + 1))
                    load(i * RING + (T_MOD + N_MOD + RING + s), (T_MOD + s) % RING)
            for g in range(G_AHEAD + RING * (rest + 1), N_SPLIT):
                sp.wait_ge(lo_done, g - RING + 1)
                load(N_MOD + g, (N_MOD + g) % RING)
            for t in range(RING):
                sp.wait_ge(lo_done, N_SPLIT - RING + t + 1)
                load(T_MOE + t, (T_MOE + t) % RING)
            with sp.Fori(0, N_MOE // RING - 1) as i:
                for s in range(RING):
                    sp.wait_ge(moe_done, i * RING + (s + 1))
                    load(i * RING + (T_MOE + RING + s), (T_MOE + s) % RING)

            for h in range(2):
                sp.wait_ge(sem("final"), 4 * h + 4)
                sp.dma_start(out[:, 4 * h:4 * h + 4, :], res[:, 4 * h:4 * h + 4, :]).then_inc(out_in[h], 16)
            for h in range(2):
                sp.wait_ge(out_in[h], 16)

        @block.gpsimd
        def _(pool):
            def sums(n):
                base, tiles, width = NORMS[n]
                for j in range(tiles):
                    pool.wait_ge(sq_done, base + j + 1)
                    if j == 0:
                        if n:
                            pool.wait_ge(msq_done, n)
                        nc.gpsimd.tensor_copy(ssum[:, :width], sq[:, (base + j) % 2, :width]).then_inc(sq_added, 1)
                    else:
                        pool.wait_ge(sq_added, base + j)
                        nc.gpsimd.tensor_tensor(ssum[:, :width], ssum[:, :width], sq[:, (base + j) % 2, :width],
                                                ALU.add).then_inc(sq_added, 1)

            sums(N_PRE["mix0"])
            for h in range(HEADS):
                pool.wait_ge(sem("dec_exp"), h + 1)
                nc.gpsimd.affine_select(out=dec, in_=dec, compare_op=ALU.is_ge, fill=0.0, base=0,
                                        pattern=[[0, NQ], [1, P]], channel_multiplier=-1).then_inc(sem("dec_masked"), 1)
            for k, name in enumerate(("mix0", "mlp0", "mix1", "mlp1")):
                sums(N_POST[name])
                sums(N_PRE[("mlp0", "mix1", "mlp1")[k]] if k < 3 else N_ATT)

            for n in (N_CTX, N_CKV_C, N_CKV, N_CQ):
                sums(n)
            sums(N_FFN)
            sums(N_FINAL)

        @block.tensor
        def _(pe):
            chain = Chain(pe, sem("pe_chain"))

            def norm_sum(n):
                base, tiles, width = NORMS[n]
                pe.wait_ge(sq_added, base + tiles)
                if n:
                    pe.wait_ge(std_done, n)
                for q in range(width // P):
                    mm = pe.matmul(psum[:, 7, q:q + 1], ssum[:, q * P:(q + 1) * P], ones[:, 0:1], start=True, stop=True)
                mm.then_inc(msq_done, 1)

            def norm_bcast(n):
                pe.wait_ge(diag_ready, n + 1)
                pe.matmul(psum[:, 6, :NORMS[n][2]], ones[:, :], diag[:, :NORMS[n][2] // P, :],
                          start=True, stop=True).then_inc(bc_done, 1)

            def product(out_ap, slot, terms):
                for k, (a, b, hi, lo, wait) in enumerate(terms):
                    if wait:
                        pe.wait_ge(*wait)
                    for m, (w, v) in enumerate(((w_hi, hi), (w_lo, hi), (w_hi, lo))):
                        mm = pe.matmul(out_ap, w[:, slot, a:b], v, start=(k == 0 and m == 0),
                                       stop=(k == len(terms) - 1 and m == 2))
                return mm

            def gemm(g, hi, lo, ready=None, done=0):
                pe.wait_ge(lo_done, g.n(1))
                if g.base - done >= BANKS:
                    pe.wait_ge(tile_out, g.n(1 - done - BANKS))
                terms = [(k * P, (k + 1) * P, hi[:, k, :], lo[:, k, :], ready and (ready[0], ready[1] + k))
                         for k in range(KT)]
                product(psum[:, (g.base - done) % BANKS, :], g.base % SPLIT_RING, terms).then_inc(mm_done, 1)

            pe.wait_ge(const_in, 64)
            n_mod = 0

            def modulation(count):
                nonlocal n_mod
                for n in range(n_mod, n_mod + count):
                    t = T_MOD + n
                    pe.wait_ge(raw_in[t % RING], 16 * (t // RING + 1))
                    for k in range(KT):
                        mm = pe.matmul(psum[:, 3, 2 * n:2 * n + P], raw[:, t % RING, k * P:(k + 1) * P],
                                       silu_c[:, k, :].unsqueeze(1).broadcast_to([P, P // 2, 2]),
                                       start=(k == 0), stop=(k == KT - 1))
                    mm.then_inc(mod_done, 1)
                n_mod += count

            def a_wait(prep):
                return (a_ready, 8 * PREP[prep] + 1)

            for j in range(5):
                gemm(At(j), act_hi, act_lo, a_wait("mix0") if j == 0 else None)
                if j == 1:
                    norm_sum(N_PRE["mix0"])
                if j == 2:
                    norm_bcast(N_PRE["mix0"])
            with pe.Fori(0, 3) as i:
                for j in range(4):
                    gemm(At(5 + j, i, 4), act_hi, act_lo)
            for j in range(8):
                gemm(At(G_O + j), act_hi, act_lo)
                if j >= 2:
                    pe.wait_ge(sem("v_tok_done"), j - 1)
                for q in range(NQ):
                    mm = pe.transpose(psum[:, 4 + j % 2, q * P:(q + 1) * P], vT[:, j, q * P:(q + 1) * P], ident[:, :])
                mm.then_inc(sem("v_turned"), 1)
            pe.wait_ge(sem("inter_done"), 1)
            for q in range(NQ):
                pe.transpose(psum[:, 7, 16 + 4 * q:20 + 4 * q], grow[4][:, q, :], ident[0:4, 0:4])
                mm = pe.transpose(psum[:, 7, 32 + 4 * q:36 + 4 * q], grow[5][:, q, :], ident[0:4, 0:4])
            mm.then_inc(sem("gate_turned"), 1)
            for h in range(HEADS):
                if h:
                    pe.wait_ge(a_ready, 8 + VT * h)
                if h == 0:
                    pe.wait_ge(sem("gate_cols_done"), 1)
                    pe.wait_ge(sem("v_tok_done"), 8)
                    pe.wait_ge(tile_out, 25)
                mm = pe.matmul(psum[:, 6, :], sel[:, h, :], grow[2].rearrange("p c l -> p (c l)"), start=True, stop=True)
                mm.then_inc(sem("u_bc"), 1)
                mm = pe.matmul(psum[:, 7, :], sel[:, h, :], grow[3].rearrange("p c l -> p (c l)"), start=True, stop=True)
                mm.then_inc(sem("i_bc"), 1)
                for q in range(NQ):
                    mm = pe.matmul(psum[:, 4, q * P:(q + 1) * P], kT[:, h, q * P:(q + 1) * P],
                                   qT[:, h, q * P:(q + 1) * P], start=True, stop=True)
                mm.then_inc(sem("scores"), 1)
                for q in range(NQ):
                    mm = pe.transpose(psum[:, 0, q * P:(q + 1) * P], kT[:, h, q * P:(q + 1) * P], ident[:, :])
                mm.then_inc(sem("k_turned"), 1)
                if h == 0:
                    pe.wait_ge(sem("silu_done"), 1)
                modulation(3)
                pe.wait_ge(sem("wk_done"), h + 1)
                for q in range(NQ - 1):
                    if q:
                        modulation(1)
                        pe.wait_ge(sem("state_done"), 3 * h + q)
                    pe.matmul(psum[:, 5, 0:2 * P], wk[:, q, :], v_tok[:, q, h * 2 * P:(h + 1) * 2 * P],
                              start=True, stop=True)
                    pe.matmul(psum[:, 5, 2 * P:2 * P + 1], wk[:, q, :], ones[:, 0:1],
                              start=True, stop=True).then_inc(sem("kv_done"), 1)
                modulation(1)
                pe.wait_ge(sem("p_done"), h + 1)
                pe.wait_ge(sem("state_done"), 3 * h + 3)
                for q in range(NQ):
                    for t in range(VT):
                        at = (h * VT + t) * P
                        pe.matmul(psum[:, 1 + t, q * P:(q + 1) * P], v_tok[:, q, at:at + P], dec[:, q, :],
                                  start=True, stop=(q == 0))
                        if q:
                            pe.matmul(psum[:, 1 + t, q * P:(q + 1) * P], state[:, q - 1, t * P:(t + 1) * P],
                                      q_in[:, q, :], start=False, stop=True)
                    mm = pe.matmul(psum[:, 7, q:q + 1], dec[:, q, :], ones[:, 0:1], start=True, stop=(q == 0))
                    if q:
                        mm = pe.matmul(psum[:, 7, q:q + 1], q_in[:, q, :], state[:, q - 1, 2 * P:2 * P + 1],
                                       start=False, stop=True)
                mm.then_inc(sem("num_done"), 1)
                modulation(2)
                pe.wait_ge(sem("num_sq"), h + 1)
                for q in range(NQ):
                    for t in range(VT):
                        mm = pe.matmul(psum[:, 6, 8 + q:9 + q], num2[:, t, q * P:(q + 1) * P], ones[:, 0:1],
                                       start=(t == 0), stop=(t == VT - 1))
                mm.then_inc(sem("num_msq"), 1)
                modulation(2)
                pe.wait_ge(sem("head_diag"), h + 1)
                pe.matmul(psum[:, 0, :], ones[:, :], diag[:, :, :], start=True, stop=True).then_inc(sem("head_bc"), 1)
                modulation(2)

            def out_proj(g0, hi, lo, ready, n):
                for j in range(8):
                    gemm(At(g0 + j), hi, lo, ready if j == 0 else None)
                norm_sum(n)
                norm_bcast(n)

            def mlp_pe(g0, name, layer):
                hb = HID[name]

                def quarter(g, first, ready, after=None):
                    for j in range(8):
                        gemm(g + j, act_hi, act_lo, first if j == 0 else None)
                        if after and j == 1:
                            norm_sum(after)
                        if after and j == 2:
                            norm_bcast(after)
                    for j in range(8):
                        gemm(g + (8 + j), hid_hi, hid_lo, ready if j == 0 else None)

                quarter(At(g0), a_wait(name), (h_ready, hb + 1), N_PRE[name])
                with pe.Fori(0, 2) as i:
                    quarter(At(g0 + 16, i, 16), None, (h_ready, i * 8 + (hb + 9)))
                quarter(At(g0 + 48), None, (h_ready, hb + 25))
                norm_sum(N_POST[name])
                norm_bcast(N_POST[name])

            out_proj(G_OUT0, act_hi, act_lo, a_wait("out0"), N_POST["mix0"])
            mlp_pe(G_MLP0, "mlp0", 0)
            for j in range(4):
                gemm(At(G_CONV + j), act_hi, act_lo, a_wait("mix1") if j == 0 else None)
                if j == 1:
                    norm_sum(N_PRE["mix1"])
                if j == 2:
                    norm_bcast(N_PRE["mix1"])
            with pe.Fori(0, 5) as i:
                for j in range(4):
                    gemm(At(G_CONV + 4 + j, i, 4), act_hi, act_lo)
            out_proj(G_OUT1, hid_hi, hid_lo, (h_ready, HID["mix1"] + 1), N_POST["mix1"])
            mlp_pe(G_MLP1, "mlp1", 1)

            norm_sum(N_ATT)
            norm_bcast(N_ATT)
            norm_sum(N_CTX)
            for i in range(12):
                g = G_IN2 + i
                if i >= 5:
                    gemm(At(g), act_hi, act_lo)
                    continue
                pe.wait_ge(lo_done, g + 1)
                pe.wait_ge(tile_out, g - BANKS + 1)
                product(psum[:, g % BANKS, :], g % SPLIT_RING,
                        [(k * P, k * P + P, act_hi[:, k, :], act_lo[:, k, :],
                          (a_ready, 8 * PREP["att"] + k + 1) if i == 0 else None) for k in range(KT)])
                if i == 0:
                    norm_bcast(N_CTX)
                if i >= 2:
                    pe.wait_ge(tile_out, g - 1)
                product(psum[:, 4 + i % 2, 0:CTX], g % SPLIT_RING,
                        [(k * P, k * P + P, hid_hi[:, k, 0:CTX], hid_lo[:, k, 0:CTX],
                          (h_ready, HID["ctx"] + k + 1) if i == 0 else None) for k in range(KT)])\
                    .then_inc(mm_done, 1)
            pe.wait_ge(tile_out, G_IN2 + 12)
            for q in range(KEYS // P):
                mm = pe.transpose(psum[:, 4 + q // 4, (q % 4) * P:(q % 4 + 1) * P], va_t[:, q * P:(q + 1) * P], ident[:, :])
            mm.then_inc(sem("va_turned"), 1)
            for n in (N_CKV_C, N_CKV, N_CQ):
                norm_sum(n)
                norm_bcast(n)
            g = G_VUP
            pe.wait_ge(lo_done, g + 1)
            pe.wait_ge(h_ready, HID["cq"])
            for q in range(KEYS // P):
                if q >= BANKS:
                    pe.wait_ge(sem("vb_out"), q - BANKS + 1)
                for k in range(RANK_KV):
                    for m, (w, v) in enumerate(((w_hi, latent_hi), (w_lo, latent_hi), (w_hi, latent_lo))):
                        mm = pe.matmul(psum[:, q % BANKS, :], v[:, k, q * P:(q + 1) * P],
                                       w[:, g % SPLIT_RING, k * TOK:(k + 1) * TOK],
                                       start=(k == 0 and m == 0), stop=(k == 1 and m == 2))
                mm.then_inc(mm_done if q == KEYS // P - 1 else sem("vb_mm"), 1)

            def attend(pre, steps, first, i, scores, tiles, value, parts=()):
                n = lambda k: i * steps + k

                def turn(s):
                    pe.wait_ge(sem(pre + "_exp"), n(s + 1))
                    pe.wait_ge(sem(pre + "_pt"), n(s + 1))
                    for t in range(tiles):
                        mm = pe.transpose(psum[:, 4 + t // 4, (t % 4) * P:(t % 4 + 1) * P],
                                          prob[:, s % 2, t * P:(t + 1) * P], ident[:, :])
                    mm.then_inc(sem(pre + "_turned"), 1)

                def values(s):
                    pe.wait_ge(sem(pre + "_pt"), n(s + 2))
                    pe.wait_ge(sem(pre + "_o"), n(s + 1))
                    for t in range(tiles):
                        mm = pe.matmul(psum[:, 6, 0:P], prob_t[:, s % 2, t * P:(t + 1) * P], value(s, t),
                                       start=(t == 0), stop=(t == tiles - 1))
                    mm.then_inc(sem(pre + "_pv"), 1)

                for s in range(steps):
                    if s >= 2:
                        pe.wait_ge(sem(pre + "_exp"), n(s - 1))
                    scores(s).then_inc(sem(pre + "_s"), 1)
                    for p in (parts(s) if parts else ()):
                        p()
                    if s >= 1:
                        turn(s - 1)
                    if s >= 2:
                        values(s - 2)
                turn(steps - 1)
                values(steps - 2)
                values(steps - 1)

            pe.wait_ge(sem("va_done"), 1)
            pe.wait_ge(sem("rope_in"), 32)
            with pe.Fori(0, 4) as i:
                pe.wait_ge(sem("q_staged"), i + 1)

                def win_scores(s):
                    lane, q, b = 64 * (s // 4), s % 4, 2 * (s % 2)
                    pe.matmul(psum[:, b, 256:512], q_stage[lane:lane + 64, q * P:(q + 1) * P], ka[lane:lane + 64, 0:CTX],
                              start=True, stop=True)
                    pe.matmul(psum[:, b + 1, 0:3 * P], q_stage[lane:lane + 64, q * P:(q + 1) * P],
                              ka[lane:lane + 64, CTX + q * P:CTX + (q + 3) * P], start=True, stop=False)
                    kind = 0 if q == 0 else 2 if q == NQ - 1 else 1
                    return pe.matmul(psum[:, b + 1, 0:3 * P], ident_b[:, :], mask[:, kind, :], start=False, stop=True)

                def win_value(s, t):
                    return va[:, t if t < 2 else t + s % 4, :]

                attend("win", 8, 0, i, win_scores, WIN // P, win_value)
            pe.wait_ge(tile_out, G_VUP + 1)
            pe.wait_ge(sem("win_o"), 33)
            pe.wait_ge(sem("kr_copied"), 1)
            with pe.Fori(0, 2) as i:
                def part(hh, k):
                    g = At(G_MLA + hh, i, 4)
                    s = g.base % SPLIT_RING
                    if k == 0:
                        pe.wait_ge(lo_done, g.n(1))
                    if k:
                        pe.wait_ge(sem("part_out"), i * 8 + (2 * hh + k))
                    else:
                        pe.wait_ge(tile_out, g.n())
                    if k == 0:
                        terms = [(m * P, m * P + P, hid_hi[:, m, :], hid_lo[:, m, :], None) for m in range(RANK_Q)]
                        product(psum[:, 7, :], s, terms).then_inc(sem("part_mm"), 1)
                    else:
                        a, b = ((0, TOK), (TOK, KEYS))[k - 1]
                        terms = [((3 + m) * P, (4 + m) * P, latent_hi[:, m, a:b], latent_lo[:, m, a:b], None)
                                 for m in range(RANK_KV)]
                        product(psum[:, 7, 0:b - a], s, terms).then_inc(mm_done if k == 2 else sem("part_mm"), 1)

                for k in range(3):
                    part(0, k)

                def mla_scores(s):
                    hh, q, b = s // 4, s % 4, 2 * (s % 2)
                    if q == 0:
                        pe.wait_ge(tile_out, At(G_MLA + hh, i, 4).n(1))
                    lhs = qh[:, hh % 2, q * P:(q + 1) * P]
                    pe.matmul(psum[:, b, :], lhs, kh[:, hh % 2, 0:TOK], start=True, stop=True)
                    return pe.matmul(psum[:, b + 1, 0:KEYS - TOK], lhs, kh[:, hh % 2, TOK:KEYS], start=True, stop=True)

                def mla_value(s, t):
                    return vb[:, t, bass.ds(i * 256 + P * (s // 8), P)]

                def mla_parts(s):
                    hh, q = s // 4 + 1, s % 4
                    return [lambda: part(hh, q)] if q < 3 and hh < 4 else []

                attend("mla", 16, 0, i, mla_scores, KEYS // P, mla_value, mla_parts)
            pe.wait_ge(sem("mla_o"), 33)
            for j in range(KT):
                if j >= BANKS:
                    pe.wait_ge(a_ready, 8 * PREP["out2"] + j - BANKS + 1)
                for q in range(NQ):
                    mm = pe.transpose(psum[:, j % BANKS, q * P:(q + 1) * P], o_tok[:, q, j * P:(j + 1) * P], ident[:, :])
                mm.then_inc(sem("mix_turned"), 1)
            pe.wait_ge(a_ready, 8 * PREP["out2"] + KT)
            for j in range(KT):
                gemm(At(G_OUT2 + j), act_hi, act_lo)
            norm_sum(N_FFN)
            norm_bcast(N_FFN)
            pe.wait_ge(sem("moe_in"), 48)
            pe.wait_ge(sem("h2_done"), KT)
            for q in range(NQ):
                for k in range(KT):
                    mm = pe.matmul(psum[:, 7, q * NE:(q + 1) * NE], h2[:, k, q * P:(q + 1) * P], router[:, k, :],
                                   start=(k == 0), stop=(k == KT - 1))
            mm.then_inc(sem("logits"), 1)
            for m in range(8):
                if m >= BANKS:
                    pe.wait_ge(sem("tok_lo"), m - BANKS + 1)
                q, half = m // 2, m % 2
                for k in range(4):
                    mm = pe.transpose(psum[:, m % BANKS, k * P:(k + 1) * P], h2[:, 4 * half + k, q * P:(q + 1) * P], ident[:, :])
                mm.then_inc(sem("tok_turned"), 1)
            pe.wait_ge(sem("aff_done"), 1)
            for q in range(NQ):
                mm = pe.transpose(psum[0:NE, 4, q * P:(q + 1) * P], aff[:, q, :], ident[:, :])
            mm.then_inc(sem("aff_turned"), 1)
            pe.wait_ge(sem("chosen"), 1)
            for q in range(NQ):
                mm = pe.transpose(psum[:, 5, q * NE:(q + 1) * NE], aff_t[1][:, q * P:(q + 1) * P], ident[0:NE, 0:NE])
            mm.then_inc(sem("msk_turned"), 1)
            pe.wait_ge(sem("msk_done"), 1)
            for q in range(NQ):
                for b in range(q + 1):
                    mm = pe.matmul(psum[:, 6, q * NE:(q + 1) * NE], tri if b == q else ones[:, :], msk[:, b, :],
                                   start=(b == 0), stop=(b == q))
            mm.then_inc(sem("counted"), 1)
            pe.wait_ge(sem("sel_done"), 1)
            pe.wait_ge(sem("tok_lo"), 8)
            for m in range(16):
                d, half = m // 2, m % 2
                if m >= BANKS:
                    pe.wait_ge(sem("xs_done"), m - BANKS + 1)
                for q in range(NQ):
                    f = 2 * q + d // 4
                    for k, v in enumerate((act_hi, act_lo)):
                        mm = pe.matmul(psum[:, m % BANKS, :], v[:, f, (d % 4) * P:(d % 4 + 1) * P], sel_s[:, 2 * q + half, :],
                                       start=(q == 0 and k == 0), stop=(q == NQ - 1 and k == 1))
                mm.then_inc(sem("gathered"), 1)
            for p in range(PAIRS):
                if p >= 2:
                    pe.wait_ge(sem("sel_t_done"), p - 1)
                for q in range(NQ):
                    part_ = sel_s[:, 2 * q + p // 4, (p % 4) * P:(p % 4 + 1) * P].bitcast(F32)
                    mm = pe.transpose(psum[:, 4 + p % 2, q * P:(q + 1) * P], part_, ident[:, :])
                mm.then_inc(sem("sel_turned"), 1)
            for p in range(PAIRS):
                for q in range(NQ):
                    part_ = sel_s[:, 2 * q + p // 4, (p % 4) * P:(p % 4 + 1) * P].bitcast(F32)
                    mm = pe.matmul(psum[:, 7, p * NE:(p + 1) * NE], part_, aff[:, q, :], start=(q == 0), stop=(q == NQ - 1))
            mm.then_inc(sem("val_mm"), 1)
            pe.wait_ge(sem("xs_done"), 16)
            pe.wait_ge(sem("val_done"), 1)
            pe.wait_ge(sem("sel_t_done"), PAIRS)

            def arrived(i, t):
                pe.wait_ge(raw_in[(T_MOE + t) % RING], i * (16 * MOE_STEP // RING) + 16 * ((T_MOE + t) // RING + 1))
                return raw[:, (T_MOE + t) % RING, :]

            with pe.Fori(0, PAIRS) as i:
                pe.wait_ge(sem("moe_h"), i * 2 + 1)
                for t in range(16):
                    e, kind, f = t // 8, t % 8 // 4, t % 4
                    w = arrived(i, t)
                    for k in range(KT):
                        mm = pe.matmul(psum[:, 2 * e + kind, f * P:(f + 1) * P], w[:, k * P:(k + 1) * P],
                                       xs[:, k, bass.ds(i * P, P)], start=(k == 0), stop=(k == KT - 1))
                    mm.then_inc(moe_done, 1)
                pe.wait_ge(sem("moe_y"), i * 2 + 1)
                for t in range(16, 24):
                    e, f = (t - 16) // FT, t % FT
                    w = arrived(i, t)
                    if f == 0:
                        pe.wait_ge(sem("moe_h"), i * 2 + (e + 2))
                    for half in range(2):
                        mm = pe.matmul(psum[e * CAP:(e + 1) * CAP, 4 + half, :], h_e[:, e, f * CAP:(f + 1) * CAP],
                                       w[:, half * 512:(half + 1) * 512], start=(f == 0), stop=(f == FT - 1))
                    mm.then_inc(moe_done, 1)
            pe.wait_ge(sem("moe_y"), 2 * PAIRS + 1)
            for j in range(KT):
                if j >= BANKS:
                    pe.wait_ge(sem("x_out"), j - BANKS + 1)
                for p in range(PAIRS):
                    mm = pe.matmul(psum[:, j % BANKS, :], ye[:, p, j * P:(j + 1) * P], sel_t[:, p, :].bitcast(F32),
                                   start=(p == 0), stop=(p == PAIRS - 1))
                mm.then_inc(sem("scattered"), 1)
            norm_sum(N_FINAL)
            norm_bcast(N_FINAL)

        @block.scalar
        def _(act):
            chain = Chain(act, sem("act_chain"))

            def split(g):
                if g.base >= N_SPLIT:
                    return
                slot = g.place() % RING
                act.wait_ge(raw_in[slot], g.rounds() * 16)
                if g.base >= SPLIT_RING:
                    act.wait_ge(mm_done, g.n(1 - SPLIT_RING))
                nc.scalar.copy(w_hi[:, g.base % SPLIT_RING, :], raw[:, slot, :]).then_inc(hi_done, 1)

            def square(n, j, src):
                base, _, width = NORMS[n]
                if base + j >= 2:
                    act.wait_ge(sq_added, base + j - 1)
                nc.scalar.activation(sq[:, (base + j) % 2, :width], src, ACT.Square).then_inc(sq_done, 1)

            def root(n, feats):
                act.wait_ge(msq_done, n + 1)
                if n:
                    act.wait_ge(diag_ready, n)
                w = NORMS[n][2] // P
                nc.scalar.activation(small[:, 0, :w], psum[:, 7, 0:w], ACT.Sqrt, bias=c("eps"),
                                     scale=1.0 / feats).then_inc(std_done, 1)

            act.wait_ge(const_in, 64)
            nc.scalar.activation(silu_c.rearrange("p a b -> p (a b)"), col[:, COL["c"]:COL["c"] + 2 * KT],
                                 ACT.Silu).then_inc(sem("silu_done"), 1)
            for j in range(KT):
                act.wait_ge(x_in[j // 4], 16)
                nc.scalar.activation(act_hi[:, j, :], res[:, j, :], ACT.Copy, scale=normg(0, 0, j)).then_inc(a_hi, 1)
                square(N_PRE["mix0"], j, res[:, j, :])
            split(At(0))
            split(At(1))
            split(At(2))
            root(N_PRE["mix0"], D)
            act.wait_ge(tile_out, 1)
            r0, r1 = grow[0], grow[1]
            for k in range(2):
                nc.scalar.activation(grow[k], grow[k], ACT.Tanh, bias=gsm[:, k:k + 1],
                                     scale=1.0 / GATE_CAP).then_inc(sem("gate_tanh"), 1)
            act.wait_ge(sem("gate_tanh"), 2)
            chain.link(nc.scalar.activation(grow[2], grow[1], ACT.Exp, scale=-GATE_CAP))
            nc.scalar.activation(grow[1], grow[2], ACT.Ln, bias=1.0).then_inc(sem("gate_ln"), 1)
            for j in range(1, 5):
                split(At(j + 2))
            with act.Fori(0, 3) as i:
                for j in range(4):
                    split(At(7 + j, i, 4))
            act.wait_ge(sem("gate_u"), 1)
            for q in range(NQ):
                last = nc.scalar.activation(grow[3][:, q, :], grow[2][:, q, :], ACT.Exp, bias=gsm[:, 2 + q:3 + q], scale=-1.0)
            last.then_inc(sem("inter_done"), 1)
            for j in range(8):
                split(At(G_O + j + 2))
                act.wait_ge(sem("v_turned"), j + 1)
                nc.scalar.activation(v_tok[:, :, j * P:(j + 1) * P],
                                     psum[:, 4 + j % 2, :].rearrange("p (a b) -> p a b", b=P), ACT.Copy)\
                    .then_inc(sem("v_tok_done"), 1)
                act.wait_ge(tile_out, G_O + j + 1)
                nc.scalar.activation(o_sig[:, j, :], o_sig[:, j, :], ACT.Sigmoid).then_inc(sem("o_done"), 1)
            act.wait_ge(sem("gate_cols_done"), 1)
            nc.scalar.activation(gcol[:, 1], gcol[:, 1], ACT.Exp, scale=-1.0).then_inc(sem("floor_done"), 1)
            for h in range(HEADS):
                act.wait_ge(sem("gap_done"), h + 1)
                nc.scalar.activation(dec, dec, ACT.Exp, scale=-1.0).then_inc(sem("dec_exp"), 1)
                act.wait_ge(sem("num_copied"), h + 1)
                nc.scalar.activation(num2, num, ACT.Square).then_inc(sem("num_sq"), 1)
                act.wait_ge(sem("head_var"), h + 1)
                nc.scalar.activation(hsm[:, 3, :], hsm[:, 2, :], ACT.Sqrt).then_inc(sem("head_root"), 1)
                for t in range(VT):
                    act.wait_ge(sem("h_full"), VT * h + t + 1)
                    nc.scalar.copy(act_hi[:, VT * h + t, :], tmp[:, t, :]).then_inc(a_hi, 1)

            def post(name, j):
                act.wait_ge(tile_out, POST_G[name] + j + 1)
                square(N_POST[name], j, y[:, j, :])

            def prep(name, nxt, layer, which):
                root(N_POST[name], D)
                for j in range(KT):
                    act.wait_ge(x_ready, 8 * ("mix0", "mlp0", "mix1", "mlp1").index(name) + j + 1)
                    if nxt:
                        nc.scalar.activation(act_hi[:, j, :], res[:, j, :], ACT.Copy,
                                             scale=normg(layer, which, j)).then_inc(a_hi, 1)
                        square(N_PRE[nxt], j, res[:, j, :])
                    else:
                        square(N_ATT, j, res[:, j, :])

            def mlp_act(g0, name):
                def up(g, j, nroot=None):
                    split(g + (j + 2))
                    if nroot is not None and j == 0:
                        root(nroot, D)
                    act.wait_ge(tile_out, g.n(j + 1))
                    chain.do(nc.scalar.activation(sqt[:, j % 2, :], tmp[:, j % 2, :], ACT.Square))
                    chain.sync()
                    nc.scalar.copy(hid_hi[:, j, :], sqt[:, j % 2, :]).then_inc(h_hi, 1)

                for j in range(8):
                    up(At(g0), j, N_PRE[name])
                for j in range(8):
                    split(At(g0 + 8 + j + 2))
                with chain.fori(2, 8) as i:
                    g = At(g0 + 16, i, 16)
                    for j in range(8):
                        up(g, j)
                    for j in range(8):
                        split(g + (8 + j + 2))
                for j in range(8):
                    up(At(g0 + 48), j)
                for j in range(8):
                    split(At(g0 + 48 + 8 + j + 2))
                    post(name, j)

            for j in range(8):
                split(At(G_OUT0 + j + 2))
                post("mix0", j)
            prep("mix0", "mlp0", 0, 2)
            mlp_act(G_MLP0, "mlp0")
            prep("mlp0", "mix1", 1, 0)
            split(At(G_CONV + 2))
            root(N_PRE["mix1"], D)

            def conv_hi(f, k):
                act.wait_ge(sem("conv_full"), f)
                nc.scalar.copy(hid_hi[:, k, :], cbuf[:, 3, :]).then_inc(h_hi, 1)

            split(At(G_CONV + 3))
            split(At(G_CONV + 4))
            conv_hi(1, 0)
            for j in range(1, 8):
                for s in range(3):
                    split(At(G_CONV + 3 * j + s + 2))
                conv_hi(j + 1, j)
            for j in range(8):
                split(At(G_OUT1 + j + 2))
                post("mix1", j)
            prep("mix1", "mlp1", 1, 2)
            mlp_act(G_MLP1, "mlp1")
            prep("mlp1", None, 0, 0)

            def rounded(dst, width, base, done, t0, tiles, shift=None):
                for j in range(tiles):
                    act.wait_ge(sem("t_ready"), t0 + j + 1)
                    src = tmp[:, j % 2, :width]
                    if shift is None:
                        ins = nc.scalar.copy(dst(j), src)
                    else:
                        ins = nc.scalar.activation(dst(j), src, ACT.Identity, bias=shift(j))
                    ins.then_inc(done, 1)

            def softmax(pre, steps, i, scale, keys, tiles, sink=None, begin=None):
                n = lambda k: i * steps + k

                def move(s):
                    act.wait_ge(sem(pre + "_turned"), n(s + 1))
                    if s >= 2:
                        act.wait_ge(sem(pre + "_pv"), n(s - 1))
                    src = psum[:, 4:6, :].rearrange("p a b -> p (a b)")[:, 0:tiles * P]
                    nc.scalar.copy(prob_t[:, s % 2, 0:tiles * P], src).then_inc(sem(pre + "_pt"), 1)

                for s in range(steps):
                    act.wait_ge(sem(pre + "_max"), n(s + 1))
                    if s >= 2:
                        act.wait_ge(sem(pre + "_turned"), n(s - 1))
                    src = psum[:, 2 * (s % 2):2 * (s % 2) + 2, :].rearrange("p a b -> p (a b)")
                    a = 256 if sink else 0
                    nc.scalar.activation(prob[:, s % 2, 0:keys], src[:, a:a + keys], ACT.Exp, bias=soft[:, 1, s % 2:s % 2 + 1],
                                         scale=scale, accum_out=soft[:, 2, s % 2:s % 2 + 1]).then_inc(sem(pre + "_exp"), 1)
                    if sink:
                        nc.scalar.activation(soft[:, 3, s % 2:s % 2 + 1], sink(s), ACT.Exp,
                                             bias=soft[:, 1, s % 2:s % 2 + 1]).then_inc(sem(pre + "_sink"), 1)
                    if s >= 1:
                        move(s - 1)
                    if begin:
                        begin(s)
                move(steps - 1)

            act.dma_start(rope, rope_in).then_inc(sem("rope_in"), 16)
            act.dma_start(mask, mask_in).then_inc(sem("rope_in"), 16)
            root(N_ATT, D)
            act.dma_start(ctx_x, ctx_in).then_inc(sem("ctx_in"), 16)
            act.wait_ge(sem("ctx_in"), 16)
            for j in range(KT):
                square(N_CTX, j, ctx_x[:, j, :])
            rounded(lambda j: act_hi[:, j, :], TOK, None, a_hi, 0, KT, lambda j: mod[:, j, 0:1])
            root(N_CTX, D)
            rounded(lambda j: hid_hi[:, j, 0:CTX], CTX, None, h_hi, KT, KT, lambda j: mod[:, j, 1:2])
            for i in range(12):
                split(At(G_IN2 + i + 2))
            act.wait_ge(sem("va_turned"), 1)
            nc.scalar.copy(va[:, 0:2, :], psum[:, 4, 0:256].rearrange("p (a b) -> p a b", b=P))
            nc.scalar.copy(va[:, 3:5, :], psum[:, 4, 256:512].rearrange("p (a b) -> p a b", b=P))
            nc.scalar.copy(va[:, 5:7, :], psum[:, 5, 0:256].rearrange("p (a b) -> p a b", b=P)).then_inc(sem("va_done"), 1)
            act.wait_ge(tile_out, G_IN2 + 12)
            for j in range(RANK_KV):
                square(N_CKV_C, j, ckv[:, j, 0:CTX])
            root(N_CKV_C, RANK_KV * P)
            for j in range(RANK_KV):
                square(N_CKV, j, ckv[:, j, CTX:KEYS])
            rounded(lambda j: latent_hi[:, j, 0:CTX], CTX, None, h_hi, 2 * KT, RANK_KV)
            root(N_CKV, RANK_KV * P)
            for j in range(RANK_Q):
                square(N_CQ, j, cq[:, j, :])
            rounded(lambda j: latent_hi[:, j, CTX:KEYS], TOK, None, h_hi, 2 * KT + 2, RANK_KV)
            root(N_CQ, RANK_Q * P)
            rounded(lambda j: hid_hi[:, j, :], TOK, None, h_hi, 2 * KT + 4, RANK_Q)
            split(At(G_VUP + 2))
            act.sem_inc(sem("win_pt"), 1)
            with act.Fori(0, 4) as i:
                softmax("win", 8, i, SCALE_A, WIN, WIN // P,
                        sink=lambda s: col[:, bass.ds(i + (COL["sink"] + 4 * (s // 4)), 1)])
            act.sem_inc(sem("mla_pt"), 1)
            with act.Fori(0, 2) as i:
                split(At(G_MLA + 2, i, 4))

                def begin(s):
                    if s % 4 == 2 and s < 12:
                        split(At(G_MLA + s // 4 + 3, i, 4))
                softmax("mla", 16, i, SCALE_B, KEYS, KEYS // P, begin=begin)
            for j in range(KT):
                act.wait_ge(sem("mix_turned"), j + 1)
                nc.scalar.copy(act_hi[:, j, :], psum[:, j % BANKS, :]).then_inc(a_hi, 1)
            for j in range(KT):
                split(At(G_OUT2 + j + 2))
                act.wait_ge(tile_out, G_OUT2 + j + 1)
                square(N_FFN, j, res[:, j, :])
            act.dma_start(router, router_in).then_inc(sem("moe_in"), 16)
            act.dma_start(iota, iota_in).then_inc(sem("moe_in"), 16)
            act.dma_start(tri, tri_in).then_inc(sem("moe_in"), 16)
            root(N_FFN, D)
            for j in range(KT):
                act.wait_ge(sem("h2_gain"), j + 1)
                nc.scalar.activation(h2[:, j, :], h2[:, j, :], ACT.Identity, bias=mod[:, 24 + j, 0:1]).then_inc(sem("h2_done"), 1)
            act.wait_ge(sem("aff_sub"), 1)
            nc.scalar.activation(aff_p, aff_p, ACT.Exp).then_inc(sem("aff_exp"), 1)
            for m in range(8):
                act.wait_ge(sem("tok_turned"), m + 1)
                nc.scalar.copy(act_hi[:, m, :], psum[:, m % BANKS, :]).then_inc(sem("tok_hi"), 1)
            for m in range(16):
                d, half = m // 2, m % 2
                act.wait_ge(sem("gathered"), m + 1)
                nc.scalar.copy(xs[:, d, half * 512:(half + 1) * 512], psum[:, m % BANKS, :]).then_inc(sem("xs_done"), 1)
            for p in range(PAIRS):
                act.wait_ge(sem("sel_turned"), p + 1)
                nc.scalar.copy(sel_t[:, p, :], psum[:, 4 + p % 2, :]).then_inc(sem("sel_t_done"), 1)
            act.wait_ge(sem("val_done"), 1)
            act.sem_inc(sem("moe_y"), 1)
            with act.Fori(0, PAIRS) as i:
                for e in range(2):
                    act.wait_ge(moe_done, i * MOE_STEP + 8 * (e + 1))
                    nc.scalar.activation(gate_s[:, e, :].rearrange("p (f c) -> p f c", c=CAP), mine(2 * e, e), ACT.Silu).then_inc(sem("moe_silu"), 1)
                act.wait_ge(moe_done, i * MOE_STEP + MOE_STEP)
                for half in range(2):
                    nc.scalar.activation(ye.rearrange("p a b -> p (a b)")[:, bass.ds(i * D + half * 512, 512)],
                                         psum[:, 4 + half, :], ACT.Copy,
                                         scale=val[:, bass.ds(i, 1)]).then_inc(sem("moe_y"), 1)
            for j in range(KT):
                act.wait_ge(sem("x_out"), j + 1)
                square(N_FINAL, j, res[:, j, :])
            root(N_FINAL, D)

        @block.vector
        def _(dve):
            chain = Chain(dve, sem("dve_chain"))
            V = nc.vector

            def split(g):
                if g.base >= N_SPLIT:
                    return
                s = g.base % SPLIT_RING
                dve.wait_ge(hi_done, g.n(1))
                V.tensor_tensor(w_lo[:, s, :], raw[:, g.place() % RING, :], w_hi[:, s, :].bitcast(F32),
                                ALU.subtract).then_inc(lo_done, 1)

            def norm_diag(n):
                w = NORMS[n][2] // P
                dve.wait_ge(std_done, n + 1)
                chain.link(V.reciprocal(small[:, 1, :w], small[:, 0, :w]))
                if n:
                    dve.wait_ge(bc_done, n)
                V.tensor_tensor(diag[:, :w, :], ident[:, :].unsqueeze(1).broadcast_to([P, w, P]),
                                small[:, 1, :w].unsqueeze(2).broadcast_to([P, w, P]), ALU.mult).then_inc(diag_ready, 1)

            def norm_row(n):
                dve.wait_ge(bc_done, n + 1)
                w = NORMS[n][2]
                chain.link(V.tensor_copy(row[:, :w], psum[:, 6, :w]))

            def acc(g, done=0):
                return psum[:, (g.base - done) % BANKS, :]

            def evac_wait(g):
                dve.wait_ge(mm_done, g.n(1))

            dve.wait_ge(const_in, 64)
            chain.link(V.memset(gsm[:, 2:8], 0.0))
            for k, name in enumerate(("b_i", "b_f")):
                chain.link(V.tensor_scalar(gsm[:, k:k + 1], c(name)[0:HEADS], 1.0 / GATE_CAP, None, ALU.mult))
            for j in range(KT):
                dve.wait_ge(a_hi, j + 1)
                V.scalar_tensor_tensor(out=act_lo[:, j, :], in0=res[:, j, :], scalar=normg(0, 0, j),
                                       in1=act_hi[:, j, :].bitcast(F32), op0=ALU.mult,
                                       op1=ALU.subtract).then_inc(a_ready, 1)
            split(At(0))
            split(At(1))
            split(At(2))
            norm_diag(0)
            norm_row(0)
            evac_wait(At(0))
            chain.do(V.tensor_tensor(grow[0].rearrange("p c l -> p (c l)"), psum[0:4, 0, :], row[0:4, :], ALU.mult))
            V.tensor_tensor(grow[1].rearrange("p c l -> p (c l)"), psum[32:36, 0, :], row[32:36, :],
                            ALU.mult).then_inc(tile_out, 1)

            def evac_qk(g, dst, scale):
                split(g + 2)
                evac_wait(g)
                if scale is None:
                    V.tensor_tensor(dst, acc(g), row[:, :], ALU.mult).then_inc(tile_out, 1)
                else:
                    V.scalar_tensor_tensor(out=dst, in0=acc(g), scalar=scale, in1=row[:, :], op0=ALU.mult,
                                           op1=ALU.mult).then_inc(tile_out, 1)

            for j in range(4):
                evac_qk(At(1 + j), qT[:, j, :], None)
            for j in range(4):
                evac_qk(At(5 + j), kT[:, j, :], KSCALE)
            dve.wait_ge(sem("gate_ln"), 1)

            def scan(src, a, b, op):
                s = 1
                while s < P:
                    chain.do(V.tensor_copy(a[:, :, 0:s], src[:, :, 0:s]))
                    chain.link(V.tensor_tensor(a[:, :, s:P], src[:, :, s:P], src[:, :, 0:P - s], op))
                    src, a, b = a, b, a
                    s *= 2
                return src

            nb = scan(grow[1], grow[3], grow[2], ALU.add)
            at = [r for r in (grow[1], grow[2], grow[3]) if r is not nb][0]
            assert nb is grow[3]
            chain.link(V.scalar_tensor_tensor(out=grow[4], in0=grow[0], scalar=GATE_CAP, in1=nb,
                                              op0=ALU.mult, op1=ALU.add))
            pm = scan(grow[4], grow[0], grow[1], ALU.max)
            assert pm is grow[0]
            for q in range(NQ):
                m = gsm[:, 2 + q:3 + q]
                chain.link(V.tensor_scalar(grow[2][:, q, :], pm[:, q, :], m, None, ALU.max))
                if q < NQ - 1:
                    chain.link(V.tensor_tensor(gsm[:, 3 + q:4 + q], grow[2][:, q, P - 1:P], nb[:, q, P - 1:P],
                                               ALU.subtract))
            V.tensor_tensor(grow[5], grow[2], nb, ALU.subtract).then_inc(sem("gate_u"), 1)
            for j in range(8):
                g = At(G_V + j)
                split(g + 2)
                evac_wait(g)
                V.tensor_tensor(vT[:, j, :], acc(g), row[:, :], ALU.mult).then_inc(tile_out, 1)
            for j in range(8):
                g = At(G_O + j)
                split(g + 2)
                evac_wait(g)
                V.tensor_tensor(o_sig[:, j, :], acc(g), row[:, :], ALU.mult).then_inc(tile_out, 1)
            dve.wait_ge(sem("gate_turned"), 1)
            V.tensor_copy(gcol.rearrange("p a q h -> p (a q h)"), psum[:, 7, 16:48]).then_inc(sem("gate_cols_done"), 1)
            dve.wait_ge(sem("gate_cols_done"), 1)

            for h in range(HEADS):
                dve.wait_ge(sem("u_bc"), h + 1)
                for q in range(NQ):
                    last = V.tensor_scalar(dec[:, q, :], psum[:, 6, q * P:(q + 1) * P], gcol[:, 0, q, h:h + 1],
                                           0.0, ALU.subtract, ALU.max)
                last.then_inc(sem("gap_done"), 1)
                dve.wait_ge(sem("i_bc"), h + 1)
                i_bc = psum[:, 7, :].rearrange("p (a b) -> p a b", b=P)
                chain.do(V.tensor_copy(inter_s, i_bc))
                chain.do(V.tensor_tensor(q_in, qT[:, h, :].rearrange("p (a b) -> p a b", b=P), i_bc, ALU.mult))
                dve.wait_ge(sem("dec_masked"), h + 1)
                dve.wait_ge(sem("k_turned"), h + 1)
                for q in range(NQ - 1):
                    last = V.tensor_scalar(wk[:, q, :], psum[:, 0, q * P:(q + 1) * P], dec[:, q, P - 1:P], None,
                                           ALU.mult)
                last.then_inc(sem("wk_done"), 1)
                dve.wait_ge(sem("wk_done"), h + 1)
                dve.wait_ge(sem("scores"), h + 1)
                V.tensor_tensor(dec, psum[:, 4, :].rearrange("p (a b) -> p a b", b=P), dec,
                                ALU.mult).then_inc(sem("p_done"), 1)
                chain.sync()
                for q in range(NQ - 1):
                    dve.wait_ge(sem("kv_done"), 3 * h + q + 1)
                    if q == 0:
                        V.tensor_copy(state[:, 0, :], psum[:, 5, :2 * P + 1]).then_inc(sem("state_done"), 1)
                    else:
                        dve.wait_ge(sem("state_done"), 3 * h + q)
                        V.scalar_tensor_tensor(out=state[:, q, :], in0=state[:, q - 1, :],
                                               scalar=inter_s[:, q, P - 1:P], in1=psum[:, 5, :2 * P + 1],
                                               op0=ALU.mult, op1=ALU.add).then_inc(sem("state_done"), 1)
                dve.wait_ge(sem("num_done"), h + 1)
                V.tensor_copy(num, psum[:, 1:1 + VT, :]).then_inc(sem("num_copied"), 1)
                if h == 0:
                    dve.wait_ge(sem("floor_done"), 1)
                chain.link(V.scalar_tensor_tensor(out=hsm[:, 0, :], in0=psum[:, 7, 0:NQ], scalar=-1.0,
                                                  in1=gcol[:, 1, :, h], op0=ALU.mult, op1=ALU.max))
                chain.link(V.tensor_tensor(hsm[:, 0, :], psum[:, 7, 0:NQ], hsm[:, 0, :], ALU.max))
                chain.link(V.scalar_tensor_tensor(out=hsm[:, 1, :], in0=hsm[:, 0, :], scalar=EPS, in1=hsm[:, 0, :],
                                                  op0=ALU.mult, op1=ALU.mult))
                dve.wait_ge(sem("num_msq"), h + 1)
                chain.link(V.scalar_tensor_tensor(out=hsm[:, 2, :], in0=psum[:, 6, 8:8 + NQ],
                                                  scalar=1.0 / (VT * P), in1=hsm[:, 1, :],
                                                  op0=ALU.mult, op1=ALU.add))
                V.tensor_scalar(hsm[:, 2, :], hsm[:, 2, :], 1e35, None, ALU.min).then_inc(sem("head_var"), 1)
                dve.wait_ge(sem("head_root"), h + 1)
                chain.link(V.reciprocal(hsm[:, 4, :], hsm[:, 3, :]))
                V.tensor_tensor(diag[:, :, :], ident[:, :].unsqueeze(1).broadcast_to([P, NQ, P]),
                                hsm[:, 4, :].unsqueeze(2).broadcast_to([P, NQ, P]), ALU.mult)\
                    .then_inc(sem("head_diag"), 1)
                dve.wait_ge(sem("head_bc"), h + 1)
                dve.wait_ge(sem("num_copied"), h + 1)
                for t in range(VT):
                    chain.do(V.tensor_tensor(tmp[:, t, :], num[:, t, :], psum[:, 0, :], ALU.mult))
                chain.sync()
                for t in range(VT):
                    V.scalar_tensor_tensor(out=tmp[:, t, :], in0=tmp[:, t, :], scalar=c("g_hnorm", VT * h + t),
                                           in1=o_sig[:, VT * h + t, :], op0=ALU.mult,
                                           op1=ALU.mult).then_inc(sem("h_full"), 1)
                for t in range(VT):
                    dve.wait_ge(a_hi, 8 + VT * h + t + 1)
                    V.tensor_tensor(act_lo[:, VT * h + t, :], tmp[:, t, :],
                                    act_hi[:, VT * h + t, :].bitcast(F32), ALU.subtract).then_inc(a_ready, 1)

            dve.wait_ge(mod_done, N_MOD)
            chain.link(V.tensor_tensor(mod[:, :, :], psum[:, 3, 0:2 * N_MOD].rearrange("p (a b) -> p a b", b=2),
                                       col[:, COL["b_mod"]:COL["b_mod"] + N_MOD].unsqueeze(2).broadcast_to([P, N_MOD, 2]),
                                       ALU.add))
            for k, (first, which, name) in enumerate(((8, 0, "norm_attn"), (8, 1, "norm_attn"), (32, 0, "norm_ffn"))):
                chain.link(V.scalar_tensor_tensor(out=gain[:, k, :], in0=mod[:, first:first + 8, which], scalar=1.0,
                                                  in1=col[:, COL[name]:COL[name] + KT], op0=ALU.add, op1=ALU.mult))
            chain.link(V.tensor_scalar(sink_neg[:, :], col[:, COL["sink"]:COL["sink"] + 8], -1.0, None, ALU.mult))

            def prep(name, nxt, layer, which, glayer, gwhich):
                norm_diag(N_POST[name])
                norm_row(N_POST[name])
                xb = 8 * ("mix0", "mlp0", "mix1", "mlp1").index(name)

                def lo(j):
                    dve.wait_ge(a_hi, 8 * PREP[nxt] + j + 1)
                    V.scalar_tensor_tensor(out=act_lo[:, j, :], in0=res[:, j, :], scalar=normg(layer, which, j),
                                           in1=act_hi[:, j, :].bitcast(F32), op0=ALU.mult,
                                           op1=ALU.subtract).then_inc(a_ready, 1)

                for j in range(KT):
                    chain.link(V.scalar_tensor_tensor(out=tmp[:, j % 2, :], in0=y[:, j, :], scalar=normg(glayer, gwhich, j),
                                                      in1=row[:, :], op0=ALU.mult, op1=ALU.mult))
                    V.tensor_tensor(res[:, j, :], res[:, j, :], tmp[:, j % 2, :], ALU.add).then_inc(x_ready, 1)
                    if nxt and j:
                        lo(j - 1)
                if nxt:
                    lo(KT - 1)

            def evac_y(g, j, add=False):
                split(g + 2)
                evac_wait(g)
                if add:
                    V.tensor_tensor(y[:, j, :], y[:, j, :], acc(g), ALU.add).then_inc(tile_out, 1)
                else:
                    V.tensor_copy(y[:, j, :], acc(g)).then_inc(tile_out, 1)

            def mlp_dve(g0, name):
                hb = HID[name]

                def lo(g, j, i, r):
                    n = hb + j + 1 + r
                    dve.wait_ge(h_hi, n if i is None else i * 8 + n)
                    V.tensor_tensor(hid_lo[:, j, :], sqt[:, j % 2, :], hid_hi[:, j, :].bitcast(F32),
                                    ALU.subtract).then_inc(h_ready, 1)

                def quarter(g, r, i=None, pre=None, add=True):
                    for j in range(8):
                        gj = g + j
                        split(gj + 2)
                        if pre is not None and j == 0:
                            norm_diag(pre)
                            norm_row(pre)
                        evac_wait(gj)
                        V.scalar_tensor_tensor(out=tmp[:, j % 2, :], in0=acc(gj), scalar=0.0, in1=row[:, :],
                                               op0=ALU.max, op1=ALU.mult).then_inc(tile_out, 1)
                        if j:
                            lo(g, j - 1, i, r)
                    lo(g, 7, i, r)
                    for j in range(8):
                        evac_y(g + (8 + j), j, add)

                quarter(At(g0), 0, pre=N_PRE[name], add=False)
                with dve.Fori(0, 2) as i:
                    quarter(At(g0 + 16, i, 16), 8, i)
                quarter(At(g0 + 48), 24)

            for j in range(8):
                evac_y(At(G_OUT0 + j), j)
            prep("mix0", "mlp0", 0, 2, 0, 1)
            mlp_dve(G_MLP0, "mlp0")
            prep("mlp0", "mix1", 1, 0, 0, 3)
            chain.link(V.memset(halo[:, :, 0:2], 0.0))
            for j in range(8):
                g = At(G_CONV + 3 * j)
                split(g + 2)
                if j == 0:
                    norm_diag(N_PRE["mix1"])
                    norm_row(N_PRE["mix1"])
                evac_wait(g)
                V.tensor_tensor(cbuf[:, 0, :], acc(g), row[:, :], ALU.mult).then_inc(tile_out, 1)
                g = g + 1
                split(g + 2)
                evac_wait(g)
                V.tensor_tensor(cbuf[:, 1, :], acc(g), row[:, :], ALU.mult).then_inc(tile_out, 1)
                dve.wait_ge(tile_out, g.n(1))
                u = halo[:, j % 2, :]
                chain.link(V.tensor_tensor(u[:, 2:], cbuf[:, 0, :], cbuf[:, 1, :], ALU.mult))
                chain.link(V.tensor_scalar(cbuf[:, 2, :], u[:, 2:], c("conv", 2 * KT + j), None, ALU.mult))
                for k in (1, 0):
                    chain.link(V.scalar_tensor_tensor(out=cbuf[:, 2, :], in0=u[:, k:k + TOK], scalar=c("conv", k * KT + j),
                                                      in1=cbuf[:, 2, :], op0=ALU.mult, op1=ALU.add))
                g = g + 1
                split(g + 2)
                evac_wait(g)
                V.tensor_tensor(cbuf[:, 1, :], acc(g), row[:, :], ALU.mult).then_inc(tile_out, 1)
                dve.wait_ge(tile_out, g.n(1))
                V.tensor_tensor(cbuf[:, 3, :], cbuf[:, 2, :], cbuf[:, 1, :], ALU.mult).then_inc(sem("conv_full"), 1)
                dve.wait_ge(h_hi, HID["mix1"] + j + 1)
                V.tensor_tensor(hid_lo[:, j, :], cbuf[:, 3, :], hid_hi[:, j, :].bitcast(F32),
                                ALU.subtract).then_inc(h_ready, 1)
            for j in range(8):
                evac_y(At(G_OUT1 + j), j)
            prep("mix1", "mlp1", 1, 2, 1, 1)
            mlp_dve(G_MLP1, "mlp1")
            prep("mlp1", None, 0, 0, 1, 3)

            def modulated(t0, tiles, width, src, g, dst, done_hi, base, ready, shift=None):
                def lo(j):
                    dve.wait_ge(done_hi, base + j + 1)
                    hi, lo_ = dst(j)
                    if shift is None:
                        V.tensor_tensor(lo_, tmp[:, j % 2, :width], hi.bitcast(F32), ALU.subtract).then_inc(ready, 1)
                    else:
                        V.scalar_tensor_tensor(out=lo_, in0=tmp[:, j % 2, :width], scalar=shift(j), in1=hi.bitcast(F32),
                                               op0=ALU.add, op1=ALU.subtract).then_inc(ready, 1)

                for j in range(tiles):
                    if j >= 2:
                        dve.wait_ge(ready, base + j - 1)
                    V.scalar_tensor_tensor(out=tmp[:, j % 2, :width], in0=src(j), scalar=g(j), in1=row[:, :width],
                                           op0=ALU.mult, op1=ALU.mult).then_inc(sem("t_ready"), 1)
                    dve.wait_ge(sem("t_ready"), t0 + j + 1)
                    if j:
                        lo(j - 1)
                lo(tiles - 1)

            def turn(dst, src, partner, lanes, table):
                chain.do(V.tensor_tensor(dst, src, rope[:, table, :], ALU.mult))
                chain.link(V.stream_shuffle(partner, src, lanes))
                chain.link(V.tensor_tensor(partner, partner, rope[:, table + 1, :], ALU.mult))
                return V.tensor_tensor(dst, dst, partner, ALU.add)

            def soft_steps(pre, steps, i, scale, keys, o_at, half_of, sink=None, extra=None):
                n = lambda k: i * steps + k

                def finish(s):
                    b = s % 2
                    dve.wait_ge(sem(pre + "_exp"), n(s + 1))
                    den = soft[:, 2, b:b + 1]
                    if sink:
                        dve.wait_ge(sem(pre + "_sink"), n(s + 1))
                        chain.link(V.tensor_tensor(soft[:, 4, b:b + 1], soft[:, 2, b:b + 1], soft[:, 3, b:b + 1], ALU.add))
                        den = soft[:, 4, b:b + 1]
                    chain.link(V.reciprocal(soft[:, 5, b:b + 1], den))
                    dve.wait_ge(sem(pre + "_pv"), n(s + 1))
                    half = 64 * half_of(s)
                    V.tensor_scalar(o_tok[:, s % 4, o_at(s)], psum[:, 6, half:half + 64], soft[:, 5, b:b + 1], None,
                                    ALU.mult).then_inc(sem(pre + "_o"), 1)

                for s in range(steps):
                    if s >= 2:
                        finish(s - 2)
                    dve.wait_ge(sem(pre + "_s"), n(s + 1))
                    src = psum[:, 2 * (s % 2):2 * (s % 2) + 2, :].rearrange("p a b -> p (a b)")
                    a = 256 if sink else 0
                    b = s % 2
                    chain.link(V.tensor_reduce(soft[:, 0, b:b + 1], src[:, a:a + keys], AX.X, ALU.max))
                    if sink:
                        ins = V.tensor_scalar(soft[:, 1, b:b + 1], soft[:, 0, b:b + 1], -scale, sink(s), ALU.mult, ALU.min)
                    else:
                        ins = V.tensor_scalar(soft[:, 1, b:b + 1], soft[:, 0, b:b + 1], -scale, None, ALU.mult)
                    ins.then_inc(sem(pre + "_max"), 1)
                    if extra:
                        extra(s)
                finish(steps - 2)
                finish(steps - 1)

            norm_diag(N_ATT)
            norm_row(N_ATT)
            modulated(0, KT, TOK, lambda j: res[:, j, :], lambda j: gain[:, 0, j:j + 1],
                      lambda j: (act_hi[:, j, :], act_lo[:, j, :]), a_hi, 8 * PREP["att"], a_ready, lambda j: mod[:, j, 0:1])
            norm_diag(N_CTX)
            norm_row(N_CTX)
            modulated(KT, KT, CTX, lambda j: ctx_x[:, j, :], lambda j: gain[:, 1, j:j + 1],
                      lambda j: (hid_hi[:, j, 0:CTX], hid_lo[:, j, 0:CTX]), h_hi, HID["ctx"], h_ready, lambda j: mod[:, j, 1:2])
            chain.do(V.tensor_copy(ident_b[:, :], ident[:, :]))
            chain.do(V.memset(ka[:, CTX:CTX + P], 0.0))
            chain.do(V.memset(ka[:, KEYS + P:KEYS + 2 * P], 0.0))
            chain.do(V.memset(va[:, 2:8:5, :], 0.0))
            dve.wait_ge(sem("rope_in"), 32)
            for i in range(12):
                g = At(G_IN2 + i)
                split(g + 2)
                evac_wait(g)
                ctx_ps = psum[:, 4 + i % 2, 0:CTX]
                if i < 2:
                    V.tensor_copy(ckv[:, i, 0:CTX], ctx_ps)
                    V.tensor_copy(ckv[:, i, CTX:KEYS], acc(g)).then_inc(tile_out, 1)
                elif i == 2:
                    V.tensor_copy(kr[:, 0:CTX], ctx_ps)
                    V.tensor_copy(turn_raw, acc(g)).then_inc(tile_out, 1)
                    dve.wait_ge(tile_out, g.n(1))
                    chain.link(turn(kr[:, CTX:KEYS], turn_raw, turn_sh, ROPE_B, 2))
                elif i == 3:
                    V.tensor_copy(ka[:, 0:CTX], ctx_ps)
                    V.tensor_copy(turn_raw, acc(g)).then_inc(tile_out, 1)
                    dve.wait_ge(tile_out, g.n(1))
                    chain.link(turn(ka[:, CTX + P:KEYS + P], turn_raw, turn_sh, ROPE_A, 0))
                elif i == 4:
                    V.tensor_copy(va_t[:, 0:CTX], ctx_ps)
                    V.tensor_copy(va_t[:, CTX:KEYS], acc(g)).then_inc(tile_out, 1)
                elif i < 8:
                    V.tensor_copy(cq[:, i - 5, :], acc(g)).then_inc(tile_out, 1)
                else:
                    V.tensor_copy(turn_raw, acc(g)).then_inc(tile_out, 1)
                    dve.wait_ge(tile_out, g.n(1))
                    chain.link(turn(qa[:, i - 8, :], turn_raw, turn_sh, ROPE_A, 0))
            norm_diag(N_CKV_C)
            norm_row(N_CKV_C)
            modulated(2 * KT, RANK_KV, CTX, lambda j: ckv[:, j, 0:CTX], lambda j: c("kv_norm", j),
                      lambda j: (latent_hi[:, j, 0:CTX], latent_lo[:, j, 0:CTX]), h_hi, HID["ckv_c"], h_ready)
            norm_diag(N_CKV)
            norm_row(N_CKV)
            modulated(2 * KT + 2, RANK_KV, TOK, lambda j: ckv[:, j, CTX:KEYS], lambda j: c("kv_norm", j),
                      lambda j: (latent_hi[:, j, CTX:KEYS], latent_lo[:, j, CTX:KEYS]), h_hi, HID["ckv"], h_ready)
            norm_diag(N_CQ)
            norm_row(N_CQ)
            modulated(2 * KT + 4, RANK_Q, TOK, lambda j: cq[:, j, :], lambda j: c("q_norm", j),
                      lambda j: (hid_hi[:, j, :], hid_lo[:, j, :]), h_hi, HID["cq"], h_ready)
            dve.wait_ge(h_ready, HID["cq"] + 3)
            for q in range(KEYS // P):
                if q < KEYS // P - 1:
                    dve.wait_ge(sem("vb_mm"), q + 1)
                else:
                    dve.wait_ge(mm_done, G_VUP + 1)
                ins = V.tensor_copy(vb[:, q, :], psum[:, q % BANKS, :])
                ins.then_inc(sem("vb_out") if q < KEYS // P - 1 else tile_out, 1)
            split(At(G_VUP + 2))
            dve.sem_inc(sem("win_o"), 1)
            with dve.Fori(0, 4) as i:
                dve.wait_ge(sem("win_o"), i * 8 + 1)
                V.tensor_copy(q_stage, qa.rearrange("p a b -> p (a b)")[:, bass.ds(i * TOK, TOK)]).then_inc(sem("q_staged"), 1)
                with chain.inside(i, 3 * 8):
                    soft_steps("win", 8, i, SCALE_A, WIN, lambda s: bass.ds(i * P + 64 * (s // 4), 64), lambda s: s // 4,
                               sink=lambda s: sink_neg[:, bass.ds(i + 4 * (s // 4), 1)])
            chain.after(4)
            for b in range(2):
                last = V.tensor_copy(kh[64:128, b, :], kr[64:128, :])
            last.then_inc(sem("kr_copied"), 1)
            dve.sem_inc(sem("mla_o"), 1)
            with dve.Fori(0, 2) as i:
                with chain.inside(i, 2 * 16 + 3 * 4):
                    def part(hh, k):
                        g = At(G_MLA + hh, i, 4)
                        if k < 2:
                            dve.wait_ge(sem("part_mm"), i * 8 + (2 * hh + k + 1))
                        else:
                            dve.wait_ge(mm_done, g.n(1))
                        if k == 0:
                            turn(qh[:, hh % 2, :], psum[:, 7, :], tmp[:, 0, :], ROPE_B, 2).then_inc(sem("part_out"), 1)
                        elif k == 1:
                            V.tensor_copy(kh[0:64, hh % 2, 0:TOK], psum[0:64, 7, :]).then_inc(sem("part_out"), 1)
                        else:
                            V.tensor_copy(kh[0:64, hh % 2, TOK:KEYS], psum[0:64, 7, 0:KEYS - TOK]).then_inc(tile_out, 1)
                            split(g + 2)

                    for k in range(3):
                        part(0, k)

                    def extra(s):
                        if s % 4 < 3 and s < 12:
                            part(s // 4 + 1, s % 4)
                    soft_steps("mla", 16, i, SCALE_B, KEYS, lambda s: bass.ds(i * 256 + 512 + 64 * (s // 4), 64),
                               lambda s: s // 4 % 2,
                               extra=extra)
            chain.after(2)
            for j in range(KT):
                dve.wait_ge(a_hi, 8 * PREP["out2"] + j + 1)
                V.tensor_tensor(act_lo[:, j, :], psum[:, j % BANKS, :], act_hi[:, j, :].bitcast(F32),
                                ALU.subtract).then_inc(a_ready, 1)
            for j in range(KT):
                g = At(G_OUT2 + j)
                split(g + 2)
                evac_wait(g)
                V.scalar_tensor_tensor(out=res[:, j, :], in0=acc(g), scalar=mod[:, 16 + j, 0:1], in1=res[:, j, :],
                                       op0=ALU.mult, op1=ALU.add).then_inc(tile_out, 1)
            norm_diag(N_FFN)
            norm_row(N_FFN)
            for j in range(KT):
                V.scalar_tensor_tensor(out=h2[:, j, :], in0=res[:, j, :], scalar=gain[:, 2, j:j + 1], in1=row[:, :],
                                       op0=ALU.mult, op1=ALU.mult).then_inc(sem("h2_gain"), 1)
            dve.wait_ge(sem("logits"), 1)
            logits = psum[:, 7, 0:NQ * NE].rearrange("p (a b) -> p a b", b=NE)
            wide = lambda v: v.unsqueeze(2).broadcast_to([P, NQ, NE])
            chain.link(V.tensor_reduce(e_small[:, 0, :], logits, AX.X, ALU.max))
            V.tensor_tensor(aff_p, logits, wide(e_small[:, 0, :]), ALU.subtract).then_inc(sem("aff_sub"), 1)
            dve.wait_ge(sem("aff_exp"), 1)
            chain.link(V.tensor_reduce(e_small[:, 0, :], aff_p, AX.X, ALU.add))
            chain.link(V.reciprocal(e_small[:, 1, :], e_small[:, 0, :]))
            V.tensor_tensor(aff, aff_p, wide(e_small[:, 1, :]), ALU.mult).then_inc(sem("aff_done"), 1)
            for m in range(8):
                dve.wait_ge(sem("tok_hi"), m + 1)
                V.tensor_tensor(act_lo[:, m, :], psum[:, m % BANKS, :], act_hi[:, m, :].bitcast(F32),
                                ALU.subtract).then_inc(sem("tok_lo"), 1)
            dve.wait_ge(sem("aff_turned"), 1)
            chain.link(V.tensor_copy(aff_t[0], psum[0:NE, 4, :]))
            for r in range(CAP // 8):
                chain.link(V.max(top8[:, :], aff_t[r % 2]))
                chain.link(V.match_replace(aff_t[(r + 1) % 2], top8[:, :], aff_t[r % 2], -1.0))
            V.tensor_scalar(aff_t[1], aff_t[0], 0.0, None, ALU.is_lt).then_inc(sem("chosen"), 1)
            dve.wait_ge(sem("msk_turned"), 1)
            V.tensor_copy(msk, psum[:, 5, 0:NQ * NE].rearrange("p (a b) -> p a b", b=NE)).then_inc(sem("msk_done"), 1)
            dve.wait_ge(sem("msk_done"), 1)
            dve.wait_ge(sem("counted"), 1)
            chain.link(V.tensor_tensor(aff_p, psum[:, 6, 0:NQ * NE].rearrange("p (a b) -> p a b", b=NE), msk, ALU.mult))
            chain.link(V.tensor_scalar(aff_p, aff_p, 1.0, None, ALU.subtract))
            for q in range(NQ):
                last = V.tensor_tensor(sel_s[:, 2 * q:2 * q + 2, :].rearrange("p a (e c) -> p (a e) c", c=CAP),
                                       iota.unsqueeze(1).broadcast_to([P, NE, CAP]),
                                       aff_p[:, q, :].unsqueeze(2).broadcast_to([P, NE, CAP]), ALU.is_equal)
            last.then_inc(sem("sel_done"), 1)
            dve.wait_ge(sem("val_mm"), 1)
            V.tensor_copy(val[0:64, :], psum[0:64, 7, 0:7 * 18 + 1:18])
            V.tensor_copy(val[64:128, :], psum[64:128, 7, 1:7 * 18 + 2:18]).then_inc(sem("val_done"), 1)
            dve.sem_inc(sem("moe_h"), 1)
            with dve.Fori(0, PAIRS) as i:
                for e in range(2):
                    dve.wait_ge(sem("moe_silu"), i * 2 + (e + 1))
                    V.tensor_tensor(h_e[:, e, :].rearrange("p (f c) -> p f c", c=CAP),
                                    gate_s[:, e, :].rearrange("p (f c) -> p f c", c=CAP), mine(2 * e + 1, e),
                                    ALU.mult).then_inc(sem("moe_h"), 1)
            for j in range(KT):
                dve.wait_ge(sem("scattered"), j + 1)
                V.scalar_tensor_tensor(out=res[:, j, :], in0=psum[:, j % BANKS, :], scalar=mod[:, 40 + j, 0:1],
                                       in1=res[:, j, :], op0=ALU.mult, op1=ALU.add).then_inc(sem("x_out"), 1)
            norm_diag(N_FINAL)
            norm_row(N_FINAL)
            dve.wait_ge(sem("x_out"), KT)
            for j in range(KT):
                V.scalar_tensor_tensor(out=res[:, j, :], in0=res[:, j, :], scalar=c("norm_final", j), in1=row[:, :],
                                       op0=ALU.mult, op1=ALU.mult).then_inc(sem("final"), 1)


def tiles_of(w, pad=SLOT):
    k, n = w.shape
    t = w.reshape(k // P, P, n // P, P).transpose(2, 1, 0, 3).reshape(n // P, P, k // P * P)
    return t


def columns(w, places):
    out = np.zeros((w.shape[0], P), w.dtype)
    for at, cols in places:
        out[:, at:at + len(cols)] = w[:, cols]
    return out


def layout(v):
    v = {k: np.asarray(a) for k, a in v.items()}
    f = np.float32

    def feat(a):
        return np.ascontiguousarray(a.reshape(-1, P).T)

    parts = []
    w0 = v["w_in_mlstm"][0]
    parts.append(tiles_of(columns(w0, [(0, range(3072, 3076)), (32, range(3076, 3080))])))
    parts.append(tiles_of(w0[:, :3072]))
    parts.append(tiles_of(v["w_out_mlstm"][0]))

    def mlp(l):
        up, down = v["w_mlp_up"][l], v["w_mlp_down"][l]
        for q in range(4):
            parts.append(tiles_of(up[:, q * D:(q + 1) * D]))
            parts.append(tiles_of(down[q * D:(q + 1) * D]))

    mlp(0)
    wc = tiles_of(v["w_in_conv"][0])
    parts.append(np.stack([wc[8:16], wc[16:24], wc[0:8]], 1).reshape(24, P, SLOT))
    parts.append(tiles_of(v["w_out_conv"][0]))
    mlp(1)
    w2 = v["w_in_2"][0]
    r = lambda a, n: list(range(a, a + n))
    for places in ([[(0, r(1152, 128))], [(0, r(1280, 128))], [(64, r(1408, 32))], [(0, r(512, 128))], [(0, r(640, 128))]]
                   + [[(0, r(768 + 128 * j, 128))] for j in range(3)]
                   + [[(0, r(64 * j, 64)), (64, r(64 * (j + 4), 64))] for j in range(4)]):
        parts.append(tiles_of(columns(w2, places)))
    kv = v["w_kv_up_2"][0].reshape(256, 8, 128)
    wv = kv[:, :, 64:].reshape(2, P, 512).transpose(1, 0, 2).reshape(1, P, SLOT)
    parts.append(wv)
    qu = v["w_q_up_2"][0].reshape(384, 8, 96)
    heads = np.zeros((8, P, SLOT), f)
    for h in range(8):
        heads[h, :, :384].reshape(P, 3, P)[:, :, :96] = qu[:, h].reshape(3, P, 96).transpose(1, 0, 2)
        heads[h, :, 384:640].reshape(P, 2, P)[:, :, :64] = kv[:, h, :64].reshape(2, P, 64).transpose(1, 0, 2)
    parts.append(heads)
    wo = v["w_out_2"][0]
    order = sum([r(64 * j, 64) + r(64 * (j + 4), 64) for j in range(4)], []) + r(512, 512)
    parts.append(tiles_of(wo[order]))
    wg, wu, wd = v["w_gate_2"][0], v["w_up_2"][0], v["w_down_2"][0]
    for p in range(PAIRS):
        for e in (2 * p, 2 * p + 1):
            parts += [tiles_of(wg[e]), tiles_of(wu[e])]
        for e in (2 * p, 2 * p + 1):
            parts.append(wd[e].reshape(FT, P, D))
    dense = np.concatenate(parts)
    stream = np.concatenate([dense[:G_AHEAD], tiles_of(v["w_mod_2"][0]), dense[G_AHEAD:]])
    assert stream.shape == (N_TILES, P, SLOT), stream.shape

    def pcol(a):
        out = np.zeros((P, 1), f)
        out[:len(a), 0] = a
        return out

    cols = np.concatenate([
        feat(v["norm_g"]), feat(v["g_hnorm"]), feat(v["w_conv"][0]), feat(v["b_mod_2"]), feat(v["norm_attn_2"]),
        feat(v["norm_ffn_2"]), feat(v["norm_final_2"]), feat(v["q_norm_2"]), feat(v["kv_norm_2"]),
        np.stack([feat(v["c_2"]), feat(v["c_ctx_2"])], 2).reshape(P, 2 * KT),
        np.broadcast_to(v["sink_2"], (P, 8)), pcol(v["b_gates_mlstm"][0, :4]), pcol(v["b_gates_mlstm"][0, 4:]),
        np.full((P, 1), EPS, f)], 1)

    pos = np.arange(TOK)
    def table(lanes, dim):
        half, nf = dim // 2, dim // 4
        inv = (np.float32(10000.0) ** (-np.arange(nf, dtype=f) / f(nf))).astype(f)
        cos, sin = np.ones((P, TOK), f), np.zeros((P, TOK), f)
        for p0 in lanes:
            for d in range(dim):
                where = (pos // 64 if d < half else pos % 64).astype(f)
                ang = where * inv[d % half % nf]
                cos[p0 + d] = np.cos(ang)
                sin[p0 + d] = np.sin(ang) * (-1 if d % half < nf else 1)
        return cos, sin
    rope = np.stack(table((0, 64), 64) + table((64,), 32), 1)
    t, s = np.arange(P)[:, None], np.arange(3 * P)[None] - P
    near = np.abs(t - s) <= P
    mask = np.stack([near & (s >= 0), near, near & (s < P)], 1)
    mask = np.where(mask, 0, -BIG).astype(mybir.dt.np(BF16))
    sel = np.zeros((HEADS, HEADS, P), f)
    for h in range(HEADS):
        sel[h, h] = 1
    return {
        "x": v["x"][0].T.reshape(KT, P, TOK).transpose(1, 0, 2), "ctx_in": v["ctx_2"][0].T.reshape(KT, P, CTX).transpose(1, 0, 2),
        "cols": cols, "ident_in": np.eye(P, dtype=f), "ones_in": np.ones((P, P), f), "sel_in": sel,
        "rope_in": rope, "mask_in": mask, "iota_in": np.broadcast_to(np.arange(CAP, dtype=f), (P, CAP)),
        "tri_in": np.triu(np.ones((P, P), f)), "router_in": v["w_router_2"][0].reshape(KT, P, NE).transpose(1, 0, 2),
        "stream": stream,
    }


def kernel(**inputs):
    import concourse.bacc as bacc
    from concourse.bass_utils import run_bass_kernel_spmd

    arrays = {k: np.ascontiguousarray(a) for k, a in layout(inputs).items()}
    nc = bacc.Bacc("TRN2", target_bir_lowering=False, num_devices=1)
    args = {k: nc.dram_tensor(k, a.shape, mybir.dt.from_np(a.dtype), kind="ExternalInput").ap() for k, a in arrays.items()}
    args["out"] = nc.dram_tensor("out", (P, KT, TOK), F32, kind="ExternalOutput").ap()
    build(nc, **args)
    got = run_bass_kernel_spmd(nc, [arrays], core_ids=[0]).results[0]["out"]
    return np.ascontiguousarray(np.asarray(got).transpose(1, 0, 2).reshape(D, TOK).T)[None]
```

```python
import contextlib

import numpy as np

import concourse.bass as bass
from concourse import mybir

F32 = mybir.dt.float32
F32R = mybir.dt.float32r
BF16 = mybir.dt.bfloat16
ALU = mybir.AluOpType
ACT = mybir.ActivationFunctionType
AX = mybir.AxisListType

P = 128
TOK = 512
NQ = TOK // P
CTX = 256
D = 1024
KT = D // P
HEADS = 4
VT = D // HEADS // P
EPS = 1e-6
GATE_CAP = 15.0
KSCALE = float(P) ** -0.5
RANK_Q, RANK_KV = 3, 2
KEYS = CTX + TOK
NE, CAP = 16, 64
PAIRS = NE // 2
FT = 4
BIG = 1e30

SLOT = KT * P
RING, SPLIT_RING, BANKS = 4, 2, 4

N_MOD = 48
G_GATES, G_QK, G_V, G_O = 0, 1, 9, 17
G_OUT0 = 25
G_MLP0 = 33
G_CONV = 97
G_OUT1 = 121
G_MLP1 = 129
G_IN2 = 193
G_VUP = 205
G_MLA = 206
G_OUT2 = 214
N_SPLIT = 222
N_MOE = 12 * NE
G_AHEAD = G_OUT0 + SPLIT_RING
T_MOD, T_MOE = G_AHEAD, N_MOD + N_SPLIT
N_TILES = T_MOE + N_MOE

COL = {}
_n = 0
for _name, _w in (("norm_g", 8 * KT), ("g_hnorm", KT), ("conv", 3 * KT), ("b_mod", 48), ("norm_attn", KT),
                  ("norm_ffn", KT), ("norm_final", KT), ("q_norm", RANK_Q), ("kv_norm", RANK_KV), ("c", 2 * KT),
                  ("sink", 8), ("b_i", 1), ("b_f", 1), ("eps", 1)):
    COL[_name] = _n
    _n += _w
NCOL = _n

NORMS = []


def _norm(tiles, width):
    base = NORMS[-1][0] + NORMS[-1][1] if NORMS else 0
    NORMS.append((base, tiles, width))
    return len(NORMS) - 1


N_PRE = {}
N_POST = {}
N_PRE["mix0"] = _norm(KT, TOK)
N_POST["mix0"] = _norm(KT, TOK)
N_PRE["mlp0"] = _norm(KT, TOK)
N_POST["mlp0"] = _norm(KT, TOK)
N_PRE["mix1"] = _norm(KT, TOK)
N_POST["mix1"] = _norm(KT, TOK)
N_PRE["mlp1"] = _norm(KT, TOK)
N_CTX = _norm(KT, CTX)
N_POST["mlp1"] = _norm(KT, TOK)
N_ATT = _norm(KT, TOK)
N_CKV_C = _norm(RANK_KV, CTX)
N_CKV = _norm(RANK_KV, TOK)
N_CQ = _norm(RANK_Q, TOK)
N_FFN = _norm(KT, TOK)
N_FINAL = _norm(KT, TOK)
IN2_NORMS = {5: (N_CKV_C, 0), 6: (N_CKV_C, 1), 7: (N_CKV, 0), 8: (N_CKV, 1), 10: (N_CQ, 0), 11: (N_CQ, 1)}
IN2_INV = (N_CTX, N_CKV_C, N_CKV, N_CQ)

PREP = {n: i for i, n in enumerate(("mix0", "out0", "mlp0", "mix1", "mlp1", "att", "out2"))}
HID = {"mlp0": 0, "mix1": 32, "mlp1": 40, "ctx": 72, "ckv_c": 80, "ckv": 82, "cq": 84}
ROPE_A = [(i + 16) % 32 for i in range(32)]
ROPE_B = [i ^ 8 for i in range(32)]
SCALE_A, SCALE_B = 64 ** -0.5, 96 ** -0.5
WIN = CTX + 3 * P
LAG = 4
SOFT = 4
MOE_RING = 12
MOE_STEP = 24


class At:

    def __init__(self, base, i=None, per=0):
        self.base, self.i, self.per = base, i, per

    def __add__(self, k):
        return At(self.base + k, self.i, self.per)

    def n(self, k=0):
        return self.base + k if self.i is None else self.i * self.per + (self.base + k)

    def place(self):
        return self.base + (N_MOD if self.base >= G_AHEAD else 0)

    def rounds(self):
        r = self.place() // RING + 1
        return r if self.i is None else self.i * (self.per // RING) + r


class Chain:

    def __init__(self, eng, sem):
        self.eng, self.sem, self.n, self.i, self.per = eng, sem, 0, None, 0

    def do(self, ins):
        ins.then_inc(self.sem, 1)
        self.n += 1
        return ins

    def sync(self):
        if self.i is None:
            if self.n:
                self.eng.wait_ge(self.sem, self.n)
        else:
            self.eng.wait_ge(self.sem, self.i * self.per + self.n)

    def link(self, ins):
        self.do(ins)
        self.sync()

    @contextlib.contextmanager
    def fori(self, count, per):
        start = self.n
        with self.eng.Fori(0, count) as i:
            self.i, self.per = i, per
            yield i
            assert self.n - start == per, f"{self.n - start} steps an iteration"
        self.i, self.per, self.n = None, 0, start + count * per

    @contextlib.contextmanager
    def inside(self, i, per):
        self.i, self.per, self.start = i, per, self.n
        yield
        assert self.n - self.start == per, f"{self.n - self.start} steps an iteration"

    def after(self, count):
        self.n, self.i = self.start + count * self.per, None


def build(nc, x, ctx_in, cols, ident_in, ones_in, sel_in, rope_in, mask_in, iota_in, tri_in, router_in, stream,
          out):
    with contextlib.ExitStack() as keep:
        def sb(name, shape, dt=F32):
            return keep.enter_context(nc.sbuf_tensor(name, shape, dt))

        res = sb("residual", [P, KT, TOK])
        raw = sb("raw_tiles", [P, RING, SLOT])
        split_all = sb("split_parts", [P, 2 * SPLIT_RING * SLOT + 4 * KT * TOK], F32R)

        def split_view(at, a, b):
            return split_all[:, at:at + a * b].rearrange("p (a b) -> p a b", b=b)

        w_hi, w_lo = (split_view(i * SPLIT_RING * SLOT, SPLIT_RING, SLOT) for i in range(2))
        act_hi, act_lo, hid_hi, hid_lo = (split_view(2 * SPLIT_RING * SLOT + i * KT * TOK, KT, TOK) for i in range(4))
        ye_hi, ye_lo = (split_view(i * PAIRS * D, PAIRS, D) for i in range(2))
        ident = sb("ident", [P, P])
        ones = sb("ones", [P, P])
        sel = sb("sel", [HEADS, HEADS, P])
        col = sb("columns", [P, NCOL])
        sum_sel = sb("sum_selectors", [P, NQ, NQ])
        row = sb("norm_row", [P, TOK])
        inv = sb("norm_inv", [NQ, 2, P])
        sq = sb("squares", [P, 2, TOK])
        ssum = sb("square_sum", [P, TOK])
        diag = ssum.rearrange("p (a b) -> p a b", b=P)
        tmp = sb("tmp", [P, 2, TOK])
        silu_c = sb("silu_c", [P, KT, 2])
        mod = sb("mod", [P, N_MOD, 2])
        gain = sb("gains", [P, 3, KT])
        ARENA = 19500
        arena = sb("arena", [P, ARENA])

        psum = keep.enter_context(nc.psum_tensor("banks", [P, 8, 512], F32))
        row_ps = psum[:, 6, :]

        def view(at, *dims):
            n = int(np.prod(dims))
            assert at + n <= ARENA, (at, dims)
            v = arena[:, at:at + n]
            if len(dims) == 2:
                return v.rearrange("p (a b) -> p a b", b=dims[1])
            if len(dims) == 3:
                return v.rearrange("p (a b c) -> p a b c", b=dims[1], c=dims[2])
            return v

        qT, kT = view(0, HEADS, TOK), view(2048, HEADS, TOK)
        v_tok, o_sig, vT = view(4096, NQ, D), view(8192, KT, TOK), view(12288, KT, TOK)
        dec, wk, q_in, inter_s = (view(12288 + 512 * i, NQ, P) for i in range(4))
        num, num2 = view(14336, VT, TOK), view(15360, VT, TOK)
        rows_at = [16384 + 512 * i for i in range(6)]
        grow = [arena[0:HEADS, a:a + 512].rearrange("p (c l) -> p c l", l=P) for a in rows_at]
        state = view(16384, 3, 2 * P + 1)
        gcol = sb("gate_cols", [P, 2, NQ, HEADS])
        hsm = sb("head_small", [P, 6, NQ])
        gsm = sb("gate_small", [HEADS, 8])
        y = view(0, KT, TOK)
        addend = view(9000, 4, TOK)
        halo = view(4096, 2, TOK + 2)
        cbuf = view(5200, 4, TOK)
        sqt = view(7400, 2, TOK)

        rope = view(0, 4, TOK)
        mask = view(2048, 3 * 3 * P // 2).bitcast(BF16).rearrange("p (a b) -> p a b", b=3 * P)
        ident_b = sb("ident_bf16", [P, P], BF16)
        qa, ka, va = view(3200, 4, TOK), view(5248, CTX + TOK + 2 * P), view(6272, 8, P)
        cq, ckv, kr = view(7296, RANK_Q, TOK), view(8832, RANK_KV, KEYS), view(10368, KEYS)
        o_tok = view(11136, NQ, D)
        ctx_x = view(15232, KT, CTX)
        ctx_h = view(11136, KT, CTX)
        ctx_hi, ctx_lo = hid_hi[:, :, 0:CTX], hid_lo[:, :, 0:CTX]
        turn_raw, turn_sh, va_t = view(17280, TOK), view(17792, TOK), view(18304, KEYS)
        prob, prob_t, q_stage = view(15232, 2, KEYS), view(16768, 2, KEYS), view(18304, 2, TOK)
        vb, qh, kh = view(7296, 6, TOK), view(2048, 2, TOK), view(3072, 2, KEYS)
        soft = sb("softmax_small", [P, 6, SOFT])
        sink_neg = sb("sink_neg", [P, 8])
        xs, h2 = view(0, KT, NE * CAP), view(8192, KT, TOK)
        gate_s, h_e = view(16384, 2, FT * CAP), view(16896, 2, FT * CAP)
        aff_t = [arena[0:NE, 17408 + 512 * i:17920 + 512 * i] for i in range(2)]
        aff, aff_p, msk = view(18432, NQ, NE), view(18496, NQ, NE), view(18560, NQ, NE)
        val, e_small, iota, tri = view(18624, PAIRS), view(18640, 2, NQ), view(18656, CAP), view(18720, P)
        router = view(18848, KT, NE)
        logits_t = aff_t[1]
        tri_b, ones_b = (view(19000 + 64 * i, P // 2).bitcast(BF16) for i in range(2))
        val_parts = tmp.rearrange("p a b -> p (a b)")[:, 0:PAIRS * 2 * NE]
        msk_b = view(19128, NQ * NE // 2).bitcast(BF16).rearrange("p (a b) -> p a b", b=NE)
        aff_split = sb("aff_split", [P, NQ, 2 * NE], F32R)
        more = [view(at, SLOT) for at in range(12288, 16384, SLOT)] + [view(at, SLOT) for at in range(8192, 12288, SLOT)]
        top8 = sb("top8", [NE, 8])
        sel_t, sel_s = hid_lo, hid_hi
        latent_hi = hid_hi.rearrange("p a b -> p (a b)")[:, 3 * TOK:3 * TOK + 2 * KEYS].rearrange("p (a b) -> p a b", b=KEYS)
        latent_lo = hid_lo.rearrange("p a b -> p (a b)")[:, 3 * TOK:3 * TOK + 2 * KEYS].rearrange("p (a b) -> p a b", b=KEYS)

        def addend_of(j):
            return addend[:, j % 4, :]

        def mine(bank, e):
            return psum[:, bank, :].rearrange("p (f e c) -> p f e c", e=2, c=CAP)[:, :, e, :]

        sems = {}

        def sem(name):
            if name not in sems:
                sems[name] = keep.enter_context(nc.semaphore(name))
            return sems[name]

        raw_in = [sem(f"raw_in_{s}") for s in range(RING)]
        more_in = [sem(f"more_in_{s}") for s in range(MOE_RING - RING)]

        def part_bank(hh, k):
            return 7 if hh else (7, 4, 5)[k]

        def moe_slot(s):
            if s < RING:
                return raw[:, (T_MOE + s) % RING, :], raw_in[(T_MOE + s) % RING]
            return more[s - RING], more_in[s - RING]

        mod_done, moe_done = sem("mod_done"), sem("moe_done")
        hi_done, lo_done, mm_done, tile_out = sem("hi_done"), sem("lo_done"), sem("mm_done"), sem("tile_out")
        sq_done, sq_added, msq_done, std_done = sem("sq_done"), sem("sq_added"), sem("msq_done"), sem("std_done")
        inv_done, bc_done = sem("inv_done"), sem("bc_done")
        a_hi, a_ready, h_hi, h_ready = sem("a_hi"), sem("a_ready"), sem("h_hi"), sem("h_ready")
        y_ready, x_ready = sem("y_ready"), sem("x_ready")
        const_in, x_in = sem("const_in"), [sem(f"x_in_{i}") for i in range(2)]
        out_in = [sem(f"out_{i}") for i in range(4)]

        def c(name, j=0):
            return col[:, COL[name] + j:COL[name] + j + 1]

        def normg(layer, which, j):
            return c("norm_g", (4 * layer + which) * KT + j)

        block = keep.enter_context(nc.Block())

        @block.sync
        def _(sp):
            n_const = 0
            for dst, src in ((col[:], cols), (ident[:], ident_in), (ones[:], ones_in), (sel[:], sel_in)):
                sp.dma_start(dst, src).then_inc(const_in, 16)
                n_const += 1
            for h in range(2):
                sp.dma_start(res[:, 4 * h:4 * h + 4, :], x[:, 4 * h:4 * h + 4, :]).then_inc(x_in[h], 16)

            def load(t, slot):
                sp.dma_start(raw[:, slot, :], stream[t]).then_inc(raw_in[slot], 16)

            for t in range(RING):
                load(t, t % RING)
            with sp.Fori(0, G_AHEAD // RING - 1) as i:
                for s in range(RING):
                    sp.wait_ge(lo_done, i * RING + (s + 1))
                    load(i * RING + (RING + s), s)
            for t in range(G_AHEAD // RING * RING, G_AHEAD + RING):
                sp.wait_ge(lo_done, t - RING + 1)
                load(t, t % RING)
            with sp.Fori(0, N_MOD // RING - 1) as i:
                for s in range(RING):
                    sp.wait_ge(mod_done, i * RING + (s + 1))
                    load(i * RING + (T_MOD + RING + s), (T_MOD + s) % RING)
            for s in range(RING):
                sp.wait_ge(mod_done, N_MOD - RING + s + 1)
                load(T_MOD + N_MOD + s, (T_MOD + s) % RING)
            rest = (N_SPLIT - G_AHEAD - RING) // RING
            with sp.Fori(0, rest) as i:
                for s in range(RING):
                    sp.wait_ge(lo_done, i * RING + (G_AHEAD + s + 1))
                    load(i * RING + (T_MOD + N_MOD + RING + s), (T_MOD + s) % RING)
            for g in range(G_AHEAD + RING * (rest + 1), N_SPLIT):
                sp.wait_ge(lo_done, g - RING + 1)
                load(N_MOD + g, (N_MOD + g) % RING)
            def load_moe(t, s):
                at, arrived = moe_slot(s)
                sp.dma_start(at, stream[T_MOE + t]).then_inc(arrived, 16)

            sp.wait_ge(sem("mix_turned"), KT)
            for s in range(RING, 2 * RING):
                load_moe(s, s)
            for s in range(RING):
                sp.wait_ge(lo_done, N_SPLIT - RING + s + 1)
                load_moe(s, s)
            sp.wait_ge(sem("tok_turned"), 8)
            for s in range(2 * RING, MOE_RING):
                load_moe(s, s)
            with sp.Fori(0, N_MOE // MOE_RING - 1) as i:
                for s in range(MOE_RING):
                    sp.wait_ge(moe_done, i * MOE_RING + (s + 1))
                    load_moe(i * MOE_RING + (MOE_RING + s), s)

            for h in range(4):
                sp.wait_ge(sem("final"), 2 * h + 2)
                sp.dma_start(out[:, 2 * h:2 * h + 2, :], res[:, 2 * h:2 * h + 2, :]).then_inc(out_in[h], 16)
            for h in range(4):
                sp.wait_ge(out_in[h], 16)

        @block.gpsimd
        def _(pool):
            def sums(n):
                base, tiles, width = NORMS[n]
                for j in range(tiles - 1):
                    pool.wait_ge(sq_done, base + j + 1)
                    if j == 0:
                        if n:
                            pool.wait_ge(msq_done, n)
                        nc.gpsimd.tensor_copy(ssum[:, :width], sq[:, (base + j) % 2, :width]).then_inc(sq_added, 1)
                    else:
                        pool.wait_ge(sq_added, base - n + j)
                        nc.gpsimd.tensor_tensor(ssum[:, :width], ssum[:, :width], sq[:, (base + j) % 2, :width],
                                                ALU.add).then_inc(sq_added, 1)

            sums(N_PRE["mix0"])
            for h in range(HEADS):
                pool.wait_ge(sem("dec_exp"), h + 1)
                nc.gpsimd.affine_select(out=dec, in_=dec, compare_op=ALU.is_ge, fill=0.0, base=0,
                                        pattern=[[0, NQ], [1, P]], channel_multiplier=-1).then_inc(sem("dec_masked"), 1)
            for k, name in enumerate(("mix0", "mlp0", "mix1", "mlp1")):
                if k == 3:
                    sums(N_CTX)
                sums(N_POST[name])
                if k == 3:
                    for j in range(KT):
                        pool.wait_ge(h_hi, HID["ctx"] + j + 1)
                        nc.gpsimd.tensor_tensor(ctx_lo[:, j, :], ctx_h[:, j, :], ctx_hi[:, j, :].bitcast(F32),
                                                ALU.subtract).then_inc(h_ready, 1)
                for j in range(KT if k < 3 else 0):
                    pool.wait_ge(y_ready, 8 * k + j + 1)
                    nc.gpsimd.tensor_tensor(res[:, j, :], res[:, j, :], addend_of(j), ALU.add).then_inc(x_ready, 1)
                sums(N_PRE[("mlp0", "mix1", "mlp1")[k]] if k < 3 else N_ATT)

            for n in (N_CKV_C, N_CKV, N_CQ):
                sums(n)
            sums(N_FFN)
            sums(N_FINAL)

        @block.tensor
        def _(pe):
            chain = Chain(pe, sem("pe_chain"))

            def norm_sum(n):
                base, tiles, width = NORMS[n]
                nq = width // P
                pe.wait_ge(sq_added, base - n + tiles - 1)
                if n:
                    pe.wait_ge(std_done, n)
                for last, sums_ in enumerate((ssum, sq[:, (base + tiles - 1) % 2, :])):
                    if last:
                        pe.wait_ge(sq_done, base + tiles)
                    for q in range(nq):
                        mm = pe.matmul(psum[0:NQ, 7, 0:P], sum_sel[:, q, :], sums_[:, q * P:(q + 1) * P],
                                       start=(not last and q == 0), stop=(last == 1 and q == nq - 1))
                mm.then_inc(msq_done, 1)

            def norm_bcast(n):
                pe.wait_ge(inv_done, n + 1)
                for q in range(NORMS[n][2] // P):
                    mm = pe.matmul(row_ps[:, q * P:(q + 1) * P], sel[:, q, :], inv[:, 1, :], start=True, stop=True)
                mm.then_inc(bc_done, 1)

            def product(out_ap, slot, terms, between=None):
                for k, (a, b, hi, lo, wait) in enumerate(terms):
                    if wait:
                        pe.wait_ge(*wait)
                    if between and k == KT // 2:
                        between()
                    for m, (w, v) in enumerate(((w_hi, hi), (w_lo, hi), (w_hi, lo))):
                        mm = pe.matmul(out_ap, w[:, slot, a:b], v, start=(k == 0 and m == 0),
                                       stop=(k == len(terms) - 1 and m == 2))
                return mm

            def gemm(g, hi, lo, ready=None, done=0, between=None):
                pe.wait_ge(lo_done, g.n(1))
                if g.base - done >= BANKS:
                    pe.wait_ge(tile_out, g.n(1 - done - BANKS))
                terms = [(k * P, (k + 1) * P, hi[:, k, :], lo[:, k, :], ready and (ready[0], ready[1] + k))
                         for k in range(KT)]
                product(psum[:, (g.base - done) % BANKS, :], g.base % SPLIT_RING, terms, between).then_inc(mm_done, 1)

            def gemm_pair(g, hi, lo, ready):
                pe.wait_ge(lo_done, g.n(1))
                if g.base:
                    pe.wait_ge(tile_out, g.n(2 - BANKS))
                for step in range(KT + LAG):
                    for j, k in ((0, step), (1, step - LAG)):
                        if not 0 <= k < KT:
                            continue
                        if j == 0:
                            pe.wait_ge(ready[0], ready[1] + k)
                        elif k == 0:
                            pe.wait_ge(lo_done, g.n(2))
                        s = (g + j).base % SPLIT_RING
                        for m, (w, v) in enumerate(((w_hi, hi), (w_lo, hi), (w_hi, lo))):
                            mm = pe.matmul(psum[:, (g + j).base % BANKS, :], w[:, s, k * P:(k + 1) * P], v[:, k, :],
                                           start=(k == 0 and m == 0), stop=(k == KT - 1 and m == 2))
                        if k == KT - 1:
                            mm.then_inc(mm_done, 1)

            pe.wait_ge(const_in, 64)
            n_mod = 0

            def modulation(count):
                nonlocal n_mod
                for n in range(n_mod, n_mod + count):
                    t = T_MOD + n
                    pe.wait_ge(raw_in[t % RING], 16 * (t // RING + 1))
                    for k in range(KT):
                        mm = pe.matmul(psum[:, 3, 2 * n:2 * n + P], raw[:, t % RING, k * P:(k + 1) * P],
                                       silu_c[:, k, :].unsqueeze(1).broadcast_to([P, P // 2, 2]),
                                       start=(k == 0), stop=(k == KT - 1))
                    mm.then_inc(mod_done, 1)
                n_mod += count

            def a_wait(prep):
                return (a_ready, 8 * PREP[prep] + 1)

            gemm_pair(At(0), act_hi, act_lo, a_wait("mix0"))
            for j in range(2, 5):
                gemm(At(j), act_hi, act_lo, between=(lambda: norm_bcast(N_PRE["mix0"])) if j == 3 else None)
                if j == 2:
                    norm_sum(N_PRE["mix0"])
            with pe.Fori(0, 3) as i:
                for j in range(4):
                    gemm(At(5 + j, i, 4), act_hi, act_lo)
            for j in range(8):
                gemm(At(G_O + j), act_hi, act_lo)
                if j >= 2:
                    pe.wait_ge(sem("v_tok_done"), j - 1)
                for q in range(NQ):
                    mm = pe.transpose(psum[:, 4 + j % 2, q * P:(q + 1) * P], vT[:, j, q * P:(q + 1) * P], ident[:, :])
                mm.then_inc(sem("v_turned"), 1)
            pe.wait_ge(sem("inter_done"), 1)
            for q in range(NQ):
                pe.transpose(psum[:, 7, 16 + 4 * q:20 + 4 * q], grow[4][:, q, :], ident[0:4, 0:4])
                mm = pe.transpose(psum[:, 7, 32 + 4 * q:36 + 4 * q], grow[5][:, q, :], ident[0:4, 0:4])
            mm.then_inc(sem("gate_turned"), 1)
            for h in range(HEADS):
                if h:
                    pe.wait_ge(a_ready, 8 + VT * h)
                if h == 0:
                    pe.wait_ge(sem("gate_cols_done"), 1)
                    pe.wait_ge(sem("v_tok_done"), 8)
                    pe.wait_ge(tile_out, 25)
                mm = pe.matmul(psum[:, 6, :], sel[:, h, :], grow[2].rearrange("p c l -> p (c l)"), start=True, stop=True)
                mm.then_inc(sem("u_bc"), 1)
                mm = pe.matmul(psum[:, 7, :], sel[:, h, :], grow[3].rearrange("p c l -> p (c l)"), start=True, stop=True)
                mm.then_inc(sem("i_bc"), 1)
                for q in range(NQ):
                    mm = pe.matmul(psum[:, 4, q * P:(q + 1) * P], kT[:, h, q * P:(q + 1) * P],
                                   qT[:, h, q * P:(q + 1) * P], start=True, stop=True)
                mm.then_inc(sem("scores"), 1)
                for q in range(NQ):
                    mm = pe.transpose(psum[:, 0, q * P:(q + 1) * P], kT[:, h, q * P:(q + 1) * P], ident[:, :])
                mm.then_inc(sem("k_turned"), 1)
                if h == 0:
                    pe.wait_ge(sem("silu_done"), 1)
                modulation(3)
                pe.wait_ge(sem("wk_done"), h + 1)
                for q in range(NQ - 1):
                    if q:
                        modulation(1)
                        pe.wait_ge(sem("state_done"), 3 * h + q)
                    pe.matmul(psum[:, 5, 0:2 * P], wk[:, q, :], v_tok[:, q, h * 2 * P:(h + 1) * 2 * P],
                              start=True, stop=True)
                    pe.matmul(psum[:, 5, 2 * P:2 * P + 1], wk[:, q, :], ones[:, 0:1],
                              start=True, stop=True).then_inc(sem("kv_done"), 1)
                modulation(1)
                pe.wait_ge(sem("p_done"), h + 1)
                pe.wait_ge(sem("state_done"), 3 * h + 3)
                for q in range(NQ):
                    for t in range(VT):
                        at = (h * VT + t) * P
                        pe.matmul(psum[:, 1 + t, q * P:(q + 1) * P], v_tok[:, q, at:at + P], dec[:, q, :],
                                  start=True, stop=(q == 0))
                        if q:
                            pe.matmul(psum[:, 1 + t, q * P:(q + 1) * P], state[:, q - 1, t * P:(t + 1) * P],
                                      q_in[:, q, :], start=False, stop=True)
                    mm = pe.matmul(psum[:, 7, q:q + 1], dec[:, q, :], ones[:, 0:1], start=True, stop=(q == 0))
                    if q:
                        mm = pe.matmul(psum[:, 7, q:q + 1], q_in[:, q, :], state[:, q - 1, 2 * P:2 * P + 1],
                                       start=False, stop=True)
                mm.then_inc(sem("num_done"), 1)
                modulation(2)
                pe.wait_ge(sem("num_added"), h + 1)
                for q in range(NQ):
                    mm = pe.matmul(psum[:, 6, 8 + q:9 + q], num2[:, 0, q * P:(q + 1) * P], ones[:, 0:1],
                                   start=True, stop=True)
                mm.then_inc(sem("num_msq"), 1)
                modulation(2)
                pe.wait_ge(sem("head_diag"), h + 1)
                pe.matmul(psum[:, 0, :], ones[:, :], diag[:, :, :], start=True, stop=True).then_inc(sem("head_bc"), 1)
                modulation(2)

            def out_proj(g0, hi, lo, ready, n):
                for j in range(8):
                    gemm(At(g0 + j), hi, lo, ready if j == 0 else None)
                norm_sum(n)
                norm_bcast(n)

            def mlp_pe(g0, name, layer):
                hb = HID[name]

                def quarter(g, first, ready, after=None, ctx=False):
                    if first:
                        gemm_pair(g, act_hi, act_lo, first)
                    for j in range(2 if first else 0, 8):
                        gemm(g + j, act_hi, act_lo, between=(lambda: norm_bcast(after)) if after and j == 3 else None)
                        if after and j == 2:
                            norm_sum(after)
                    for j in range(8):
                        gemm(g + (8 + j), hid_hi, hid_lo, ready if j == 0 else None)
                        if ctx and j >= 6:
                            (norm_sum, norm_bcast)[j - 6](N_CTX)

                quarter(At(g0), a_wait(name), (h_ready, hb + 1), N_PRE[name], ctx=layer == 1)
                with pe.Fori(0, 2) as i:
                    quarter(At(g0 + 16, i, 16), None, (h_ready, i * 8 + (hb + 9)))
                quarter(At(g0 + 48), None, (h_ready, hb + 25))
                norm_sum(N_POST[name])
                norm_bcast(N_POST[name])

            out_proj(G_OUT0, act_hi, act_lo, a_wait("out0"), N_POST["mix0"])
            mlp_pe(G_MLP0, "mlp0", 0)
            gemm_pair(At(G_CONV), act_hi, act_lo, a_wait("mix1"))
            for j in range(2, 4):
                gemm(At(G_CONV + j), act_hi, act_lo, between=(lambda: norm_bcast(N_PRE["mix1"])) if j == 3 else None)
                if j == 2:
                    norm_sum(N_PRE["mix1"])
            with pe.Fori(0, 5) as i:
                for j in range(4):
                    gemm(At(G_CONV + 4 + j, i, 4), act_hi, act_lo)
            out_proj(G_OUT1, hid_hi, hid_lo, (h_ready, HID["mix1"] + 1), N_POST["mix1"])
            mlp_pe(G_MLP1, "mlp1", 1)

            def ctx_product(i):
                g = G_IN2 + i
                pe.wait_ge(lo_done, g + 1)
                if i >= 2:
                    pe.wait_ge(tile_out, g - 1)
                return product(psum[:, 4 + i % 2, 0:CTX], g % SPLIT_RING,
                               [(k * P, k * P + P, ctx_hi[:, k, :], ctx_lo[:, k, :],
                                 (h_ready, HID["ctx"] + k + 1) if i == 0 else None) for k in range(KT)])

            for i in range(2):
                ctx_product(i)
            norm_sum(N_ATT)
            norm_bcast(N_ATT)
            gemm_pair(At(G_IN2), act_hi, act_lo, a_wait("att"))
            for i in range(2, 12):
                if i in IN2_NORMS:
                    n, step = IN2_NORMS[i]
                    (norm_sum, norm_bcast)[step](n)
                if i < 5:
                    ctx_product(i)
                if i == 11:
                    pe.wait_ge(tile_out, G_IN2 + 5)
                    for q in range(KEYS // P):
                        mm = pe.transpose(psum[:, 4 + q // 4, (q % 4) * P:(q % 4 + 1) * P], va_t[:, q * P:(q + 1) * P], ident[:, :])
                    mm.then_inc(sem("va_turned"), 1)
                gemm(At(G_IN2 + i), act_hi, act_lo)
            g = G_VUP
            pe.wait_ge(lo_done, g + 1)
            pe.wait_ge(h_ready, HID["cq"])
            for q in range(KEYS // P):
                if q >= BANKS:
                    pe.wait_ge(sem("vb_out"), q - BANKS + 1)
                else:
                    pe.wait_ge(tile_out, g - BANKS + q + 1)
                for k in range(RANK_KV):
                    for m, (w, v) in enumerate(((w_hi, latent_hi), (w_lo, latent_hi), (w_hi, latent_lo))):
                        mm = pe.matmul(psum[:, (g + q) % BANKS, :], v[:, k, q * P:(q + 1) * P],
                                       w[:, g % SPLIT_RING, k * TOK:(k + 1) * TOK],
                                       start=(k == 0 and m == 0), stop=(k == 1 and m == 2))
                mm.then_inc(mm_done if q == KEYS // P - 1 else sem("vb_mm"), 1)

            def attend(pre, steps, i, scores, tiles, value, parts=()):
                n = lambda k: i * steps + k

                def turn(s):
                    pe.wait_ge(sem(pre + "_exp"), n(s + 1))
                    pe.wait_ge(sem(pre + "_pt"), n(s + 1))
                    for t in range(tiles):
                        mm = pe.transpose(psum[:, 4 + t // 4, (t % 4) * P:(t % 4 + 1) * P],
                                          prob[:, s % 2, t * P:(t + 1) * P], ident[:, :])
                    mm.then_inc(sem(pre + "_turned"), 1)

                def values(s):
                    pe.wait_ge(sem(pre + "_pt"), n(s + 2))
                    pe.wait_ge(sem(pre + "_o"), n(s + 1))
                    for t in range(tiles):
                        mm = pe.matmul(psum[:, 6, 0:P], prob_t[:, s % 2, t * P:(t + 1) * P], value(s, t),
                                       start=(t == 0), stop=(t == tiles - 1))
                    mm.then_inc(sem(pre + "_pv"), 1)

                for s in range(steps):
                    if s >= 2:
                        pe.wait_ge(sem(pre + "_exp"), n(s - 1))
                    scores(s).then_inc(sem(pre + "_s"), 1)
                    for p in (parts(s) if parts else ()):
                        p()
                    if s >= 1:
                        turn(s - 1)
                    if s >= 2:
                        values(s - 2)
                turn(steps - 1)
                values(steps - 2)
                values(steps - 1)

            pe.wait_ge(sem("va_done"), 1)
            pe.wait_ge(sem("rope_in"), 32)
            with pe.Fori(0, 2) as i:
                pe.wait_ge(sem("q_staged"), i + 1)

                def win_scores(s):
                    lane, q, b = 64 * (s // 4 % 2), s % 4, 2 * (s % 2)
                    lhs = q_stage[lane:lane + 64, s // 8, q * P:(q + 1) * P]
                    pe.matmul(psum[:, b, 256:512], lhs, ka[lane:lane + 64, 0:CTX],
                              start=True, stop=True)
                    pe.matmul(psum[:, b + 1, 0:3 * P], lhs,
                              ka[lane:lane + 64, CTX + q * P:CTX + (q + 3) * P], start=True, stop=False)
                    kind = 0 if q == 0 else 2 if q == NQ - 1 else 1
                    return pe.matmul(psum[:, b + 1, 0:3 * P], ident_b[:, :], mask[:, kind, :], start=False, stop=True)

                def win_value(s, t):
                    return va[:, t if t < 2 else t + s % 4, :]

                attend("win", 16, i, win_scores, WIN // P, win_value)
            pe.wait_ge(tile_out, G_VUP + 1)
            pe.wait_ge(sem("win_o"), 33)
            pe.wait_ge(sem("kr_copied"), 1)
            with pe.Fori(0, 2) as i:
                def part(hh, k):
                    g = At(G_MLA + hh, i, 4)
                    s = g.base % SPLIT_RING
                    bank = part_bank(hh, k)
                    if k == 0:
                        pe.wait_ge(lo_done, g.n(1))
                        pe.wait_ge(tile_out, g.n())
                    elif hh:
                        pe.wait_ge(sem("part_out"), i * 8 + (2 * hh + k))
                    if k == 0:
                        terms = [(m * P, m * P + P, hid_hi[:, m, :], hid_lo[:, m, :], None) for m in range(RANK_Q)]
                        product(psum[:, bank, :], s, terms).then_inc(sem("part_mm"), 1)
                    else:
                        a, b = ((0, TOK), (TOK, KEYS))[k - 1]
                        terms = [((3 + m) * P, (4 + m) * P, latent_hi[:, m, a:b], latent_lo[:, m, a:b], None)
                                 for m in range(RANK_KV)]
                        product(psum[:, bank, 0:b - a], s, terms).then_inc(mm_done if k == 2 else sem("part_mm"), 1)

                for k in range(3):
                    part(0, k)

                def mla_scores(s):
                    hh, q, b = s // 4, s % 4, 2 * (s % 2)
                    if q == 0:
                        pe.wait_ge(tile_out, At(G_MLA + hh, i, 4).n(1))
                    lhs = qh[:, hh % 2, q * P:(q + 1) * P]
                    pe.matmul(psum[:, b, :], lhs, kh[:, hh % 2, 0:TOK], start=True, stop=True)
                    return pe.matmul(psum[:, b + 1, 0:KEYS - TOK], lhs, kh[:, hh % 2, TOK:KEYS], start=True, stop=True)

                def mla_value(s, t):
                    return vb[:, t, bass.ds(i * 256 + P * (s // 8), P)]

                def mla_parts(s):
                    hh, q = s // 4 + 1, s % 4
                    return [lambda: part(hh, q)] if q < 3 and hh < 4 else []

                attend("mla", 16, i, mla_scores, KEYS // P, mla_value, mla_parts)
            pe.wait_ge(sem("mla_o"), 33)
            for j in range(KT):
                if j >= BANKS:
                    pe.wait_ge(a_ready, 8 * PREP["out2"] + j - BANKS + 1)
                for q in range(NQ):
                    mm = pe.transpose(psum[:, 4 + j % BANKS, q * P:(q + 1) * P], o_tok[:, q, j * P:(j + 1) * P], ident[:, :])
                mm.then_inc(sem("mix_turned"), 1)
            gemm_pair(At(G_OUT2), act_hi, act_lo, a_wait("out2"))
            for j in range(2, KT):
                gemm(At(G_OUT2 + j), act_hi, act_lo)
            norm_sum(N_FFN)
            norm_bcast(N_FFN)
            pe.wait_ge(sem("moe_in"), 48)
            for k in range(KT):
                pe.wait_ge(sem("h2_done"), k + 1)
                mm = pe.matmul(psum[0:NE, 7, :], router[:, k, :], h2[:, k, :], start=(k == 0), stop=(k == KT - 1))
            mm.then_inc(sem("logits_mm"), 1)

            def tokens(first, last):
                for m in range(first, last):
                    if m >= BANKS:
                        pe.wait_ge(sem("tok_lo"), m - BANKS + 1)
                    q, half = m // 2, m % 2
                    for k in range(4):
                        mm = pe.transpose(psum[:, m % BANKS, k * P:(k + 1) * P], h2[:, 4 * half + k, q * P:(q + 1) * P],
                                          ident[:, :])
                    mm.then_inc(sem("tok_turned"), 1)

            tokens(0, 2)
            pe.wait_ge(sem("logits_copied"), 1)
            for q in range(NQ):
                mm = pe.transpose(psum[:, 5, q * NE:(q + 1) * NE], logits_t[:, q * P:(q + 1) * P], ident[0:NE, 0:NE])
            mm.then_inc(sem("logits"), 1)
            tokens(2, 4)
            pe.wait_ge(sem("aff_done"), 1)
            for q in range(NQ):
                mm = pe.transpose(psum[0:NE, 4, q * P:(q + 1) * P], aff[:, q, :], ident[:, :])
            mm.then_inc(sem("aff_turned"), 1)
            tokens(4, 8)
            pe.wait_ge(sem("chosen"), 1)
            for q in range(NQ):
                mm = pe.transpose(psum[:, 5, q * NE:(q + 1) * NE], aff_t[1][:, q * P:(q + 1) * P], ident[0:NE, 0:NE])
            mm.then_inc(sem("msk_turned"), 1)
            pe.wait_ge(sem("msk_done"), 1)
            for q in range(NQ):
                for b in range(q + 1):
                    mm = pe.matmul(psum[:, 6, q * NE:(q + 1) * NE], tri_b if b == q else ones_b, msk_b[:, b, :],
                                   start=(b == 0), stop=(b == q))
            mm.then_inc(sem("counted"), 1)
            pe.wait_ge(sem("tok_lo"), 8)
            for m in range(16):
                d, half = m // 2, m % 2
                if m >= BANKS:
                    pe.wait_ge(sem("xs_done"), m - BANKS + 1)
                for q in range(NQ):
                    if m == 0:
                        pe.wait_ge(sem("sel_done"), q + 1)
                    f = 2 * q + d // 4
                    for k, v in enumerate((act_hi, act_lo)):
                        mm = pe.matmul(psum[:, m % BANKS, :], v[:, f, (d % 4) * P:(d % 4 + 1) * P], sel_s[:, 2 * q + half, :],
                                       start=(q == 0 and k == 0), stop=(q == NQ - 1 and k == 1))
                mm.then_inc(sem("gathered"), 1)
            pe.wait_ge(sem("aff_lo"), 1)
            for p in range(PAIRS):
                if p >= 2:
                    pe.wait_ge(sem("sel_t_done"), p - 1)
                parts = [sel_s[:, 2 * q + p // 4, (p % 4) * P:(p % 4 + 1) * P] for q in range(NQ)]
                for q in range(NQ):
                    mm = pe.transpose(psum[:, 4 + p % 2, q * P:(q + 1) * P], parts[q].bitcast(F32), ident[:, :])
                mm.then_inc(sem("sel_turned"), 1)
                for q in range(NQ):
                    mm = pe.matmul(psum[:, 7, p * 2 * NE:(p + 1) * 2 * NE], parts[q], aff_split[:, q, :],
                                   start=(q == 0), stop=(q == NQ - 1))
            mm.then_inc(sem("val_mm"), 1)
            pe.wait_ge(sem("xs_done"), 16)
            pe.wait_ge(sem("sel_t_done"), PAIRS)

            def arrived(i, t):
                s = t % MOE_RING
                at, sem_in = moe_slot(s)
                before = (T_MOE + s) // RING if s < RING else 0
                pe.wait_ge(sem_in, i * (16 * MOE_STEP // MOE_RING) + 16 * (before + t // MOE_RING + 1))
                return at

            with pe.Fori(0, PAIRS) as i:
                pe.wait_ge(sem("moe_h"), i * 2 + 1)
                for t in range(16):
                    e, kind, f = t // 8, t % 8 // 4, t % 4
                    w = arrived(i, t)
                    for k in range(KT):
                        mm = pe.matmul(psum[:, 2 * e + kind, f * P:(f + 1) * P], w[:, k * P:(k + 1) * P],
                                       xs[:, k, bass.ds(i * P, P)], start=(k == 0), stop=(k == KT - 1))
                    mm.then_inc(moe_done, 1)
                pe.wait_ge(sem("moe_y"), i * 2 + 1)
                for t in range(16, 24):
                    e, f = (t - 16) // FT, t % FT
                    w = arrived(i, t)
                    if f == 0:
                        pe.wait_ge(sem("moe_h"), i * 2 + (e + 2))
                    for half in range(2):
                        mm = pe.matmul(psum[e * CAP:(e + 1) * CAP, 4 + half, :], h_e[:, e, f * CAP:(f + 1) * CAP],
                                       w[:, half * 512:(half + 1) * 512], start=(f == 0), stop=(f == FT - 1))
                    mm.then_inc(moe_done, 1)
            pe.wait_ge(sem("moe_y"), 2 * PAIRS + 1)
            for j in range(KT):
                if j >= BANKS:
                    pe.wait_ge(sem("x_out"), j - BANKS + 1)
                for p in range(PAIRS):
                    for k, v in enumerate((ye_hi, ye_lo)):
                        mm = pe.matmul(psum[:, j % BANKS, :], v[:, p, j * P:(j + 1) * P], sel_t[:, p, :],
                                       start=(p == 0 and k == 0), stop=(p == PAIRS - 1 and k == 1))
                mm.then_inc(sem("scattered"), 1)
            norm_sum(N_FINAL)
            norm_bcast(N_FINAL)

        @block.scalar
        def _(act):
            chain = Chain(act, sem("act_chain"))

            def split(g):
                if g.base >= N_SPLIT:
                    return
                slot = g.place() % RING
                act.wait_ge(raw_in[slot], g.rounds() * 16)
                if g.base >= SPLIT_RING:
                    act.wait_ge(mm_done, g.n(1 - SPLIT_RING))
                nc.scalar.copy(w_hi[:, g.base % SPLIT_RING, :], raw[:, slot, :]).then_inc(hi_done, 1)

            def square(n, j, src):
                base, _, width = NORMS[n]
                if base + j >= 2:
                    if j == 1:
                        act.wait_ge(msq_done, n)
                    else:
                        act.wait_ge(sq_added, base - n + max(j - 1, 0))
                nc.scalar.activation(sq[:, (base + j) % 2, :width], src, ACT.Square).then_inc(sq_done, 1)

            def root(n, feats):
                act.wait_ge(msq_done, n + 1)
                if n:
                    act.wait_ge(inv_done, n)
                nc.scalar.activation(inv[:, 0, :], psum[0:NQ, 7, 0:P], ACT.Sqrt, bias=c("eps")[0:NQ],
                                     scale=1.0 / feats).then_inc(std_done, 1)

            act.wait_ge(const_in, 64)
            nc.scalar.activation(silu_c.rearrange("p a b -> p (a b)"), col[:, COL["c"]:COL["c"] + 2 * KT],
                                 ACT.Silu).then_inc(sem("silu_done"), 1)
            for j in range(KT):
                act.wait_ge(x_in[j // 4], 16)
                nc.scalar.activation(act_hi[:, j, :], res[:, j, :], ACT.Copy, scale=normg(0, 0, j)).then_inc(a_hi, 1)
                if j in (3, 7):
                    split(At(j // 4))
            for j in range(KT):
                if j in (4, 6):
                    split(At(j // 2))
                square(N_PRE["mix0"], j, res[:, j, :])
            root(N_PRE["mix0"], D)
            split(At(4))
            act.wait_ge(tile_out, 1)
            for k in range(2):
                nc.scalar.activation(grow[k], grow[k], ACT.Tanh, bias=gsm[:, k:k + 1],
                                     scale=1.0 / GATE_CAP).then_inc(sem("gate_tanh"), 1)
            act.wait_ge(sem("gate_tanh"), 2)
            chain.link(nc.scalar.activation(grow[2], grow[1], ACT.Exp, scale=-GATE_CAP))
            nc.scalar.activation(grow[1], grow[2], ACT.Ln, bias=1.0).then_inc(sem("gate_ln"), 1)
            for j in range(3, 5):
                split(At(j + 2))
            with act.Fori(0, 3) as i:
                for j in range(4):
                    split(At(7 + j, i, 4))
            act.wait_ge(sem("gate_u"), 1)
            for q in range(NQ):
                last = nc.scalar.activation(grow[3][:, q, :], grow[2][:, q, :], ACT.Exp, bias=gsm[:, 2 + q:3 + q], scale=-1.0)
            last.then_inc(sem("inter_done"), 1)
            for j in range(8):
                split(At(G_O + j + 2))
                act.wait_ge(sem("v_turned"), j + 1)
                nc.scalar.activation(v_tok[:, :, j * P:(j + 1) * P],
                                     psum[:, 4 + j % 2, :].rearrange("p (a b) -> p a b", b=P), ACT.Copy)\
                    .then_inc(sem("v_tok_done"), 1)
                act.wait_ge(tile_out, G_O + j + 1)
                nc.scalar.activation(o_sig[:, j, :], o_sig[:, j, :], ACT.Sigmoid).then_inc(sem("o_done"), 1)
            act.wait_ge(sem("gate_cols_done"), 1)
            nc.scalar.activation(gcol[:, 1], gcol[:, 1], ACT.Exp, scale=-1.0).then_inc(sem("floor_done"), 1)
            for h in range(HEADS):
                act.wait_ge(sem("gap_done"), h + 1)
                nc.scalar.activation(dec, dec, ACT.Exp, scale=-1.0).then_inc(sem("dec_exp"), 1)
                act.wait_ge(sem("num_copied"), h + 1)
                nc.scalar.activation(num2, num, ACT.Square).then_inc(sem("num_sq"), 1)
                act.wait_ge(sem("head_var"), h + 1)
                nc.scalar.activation(hsm[:, 3, :], hsm[:, 2, :], ACT.Sqrt).then_inc(sem("head_root"), 1)
                for t in range(VT):
                    act.wait_ge(sem("h_full"), VT * h + t + 1)
                    nc.scalar.copy(act_hi[:, VT * h + t, :], tmp[:, t, :]).then_inc(a_hi, 1)

            def rounded(dst, width, base, done, t0, tiles, shift=None):
                for j in range(tiles):
                    act.wait_ge(sem("t_ready"), t0 + j + 1)
                    src = tmp[:, j % 2, :width]
                    if shift is None:
                        ins = nc.scalar.copy(dst(j), src)
                    else:
                        ins = nc.scalar.activation(dst(j), src, ACT.Identity, bias=shift(j))
                    ins.then_inc(done, 1)

            def post_all(g0, name):
                for j in range(KT):
                    if j < KT - 1:
                        split(At(g0 + j + 2))
                    act.wait_ge(tile_out, g0 + j + 1)
                    square(N_POST[name], j, y[:, j, :])
                split(At(g0 + KT + 1))

            def prep(name, nxt, layer, which, g0):
                root(N_POST[name], D)
                if name == "mlp1":
                    for j in range(KT):
                        act.wait_ge(sem("ctx_done"), j + 1)
                        if j == 0:
                            act.wait_ge(mm_done, g0)
                        nc.scalar.copy(ctx_hi[:, j, :], ctx_h[:, j, :]).then_inc(h_hi, 1)
                for j in range(KT):
                    act.wait_ge(x_ready, 8 * ("mix0", "mlp0", "mix1", "mlp1").index(name) + j + 1)
                    if nxt:
                        nc.scalar.activation(act_hi[:, j, :], res[:, j, :], ACT.Copy,
                                             scale=normg(layer, which, j)).then_inc(a_hi, 1)
                    else:
                        square(N_ATT, j, res[:, j, :])
                if nxt:
                    for j in range(KT):
                        if j in (4, 6):
                            split(At(g0 + j // 2))
                        square(N_PRE[nxt], j, res[:, j, :])

            def mlp_act(g0, name):
                def up(g, j, nroot=None):
                    if nroot is None or j >= 3:
                        split(g + (j + 2))
                    if nroot is not None and j == 0:
                        root(nroot, D)
                        split(g + 4)
                    act.wait_ge(tile_out, g.n(j + 1))
                    chain.do(nc.scalar.activation(sqt[:, j % 2, :], tmp[:, j % 2, :], ACT.Square))
                    chain.sync()
                    nc.scalar.copy(hid_hi[:, j, :], sqt[:, j % 2, :]).then_inc(h_hi, 1)

                for j in range(8):
                    up(At(g0), j, N_PRE[name])
                for j in range(8):
                    split(At(g0 + 8 + j + 2))
                    if name == "mlp1" and j < 4:
                        for k in (2 * j, 2 * j + 1):
                            square(N_CTX, k, ctx_x[:, k, :])
                    if name == "mlp1" and j == 6:
                        root(N_CTX, D)
                with chain.fori(2, 8) as i:
                    g = At(g0 + 16, i, 16)
                    for j in range(8):
                        up(g, j)
                    for j in range(8):
                        split(g + (8 + j + 2))
                for j in range(8):
                    up(At(g0 + 48), j)
                post_all(g0 + 56, name)

            post_all(G_OUT0, "mix0")
            prep("mix0", "mlp0", 0, 2, G_MLP0)
            mlp_act(G_MLP0, "mlp0")
            prep("mlp0", "mix1", 1, 0, G_CONV)
            root(N_PRE["mix1"], D)

            def conv_hi(f, k):
                act.wait_ge(sem("conv_full"), f)
                nc.scalar.copy(hid_hi[:, k, :], cbuf[:, 3, :]).then_inc(h_hi, 1)

            split(At(G_CONV + 4))
            conv_hi(1, 0)
            for j in range(1, 8):
                for s in range(3):
                    split(At(G_CONV + 3 * j + s + 2))
                conv_hi(j + 1, j)
            post_all(G_OUT1, "mix1")
            prep("mix1", "mlp1", 1, 2, G_MLP1)
            act.dma_start(ctx_x, ctx_in).then_inc(sem("ctx_in"), 16)
            act.wait_ge(sem("ctx_in"), 16)
            mlp_act(G_MLP1, "mlp1")
            prep("mlp1", None, 0, 0, G_IN2)

            def softmax(pre, steps, i, scale, keys, tiles, sink=None, begin=None):
                n = lambda k: i * steps + k

                def move(s):
                    act.wait_ge(sem(pre + "_turned"), n(s + 1))
                    if s >= 2:
                        act.wait_ge(sem(pre + "_pv"), n(s - 1))
                    src = psum[:, 4:6, :].rearrange("p a b -> p (a b)")[:, 0:tiles * P]
                    nc.scalar.copy(prob_t[:, s % 2, 0:tiles * P], src).then_inc(sem(pre + "_pt"), 1)

                for s in range(steps):
                    act.wait_ge(sem(pre + "_max"), n(s + 1))
                    if s >= 2:
                        act.wait_ge(sem(pre + "_turned"), n(s - 1))
                    src = psum[:, 2 * (s % 2):2 * (s % 2) + 2, :].rearrange("p a b -> p (a b)")
                    a, b = (256 if sink else 0), s % SOFT
                    nc.scalar.activation(prob[:, s % 2, 0:keys], src[:, a:a + keys], ACT.Exp, bias=soft[:, 1, b:b + 1],
                                         scale=scale, accum_out=soft[:, 2, b:b + 1]).then_inc(sem(pre + "_exp"), 1)
                    if sink:
                        nc.scalar.activation(soft[:, 3, b:b + 1], sink(s), ACT.Exp, bias=soft[:, 1, b:b + 1]).then_inc(sem(pre + "_sink"), 1)
                    if s >= 1:
                        move(s - 1)
                    if begin:
                        begin(s)
                move(steps - 1)

            act.dma_start(rope, rope_in).then_inc(sem("rope_in"), 16)
            act.dma_start(mask, mask_in).then_inc(sem("rope_in"), 16)
            root(N_ATT, D)
            rounded(lambda j: act_hi[:, j, :], TOK, None, a_hi, 0, KT, lambda j: mod[:, j, 0:1])
            for i in range(12):
                split(At(G_IN2 + i + 2))
                if i == 2:
                    act.wait_ge(tile_out, G_IN2 + RANK_KV)
                    for j in range(RANK_KV):
                        square(N_CKV_C, j, ckv[:, j, 0:CTX])
                if i == 4:
                    root(N_CKV_C, RANK_KV * P)
                if i == 5:
                    rounded(lambda j: latent_hi[:, j, 0:CTX], CTX, None, h_hi, KT, RANK_KV)
                    for j in range(RANK_KV):
                        square(N_CKV, j, ckv[:, j, CTX:KEYS])
                if i == 6:
                    root(N_CKV, RANK_KV * P)
                if i == 7:
                    rounded(lambda j: latent_hi[:, j, CTX:KEYS], TOK, None, h_hi, KT + 2, RANK_KV)
                if i == 8:
                    act.wait_ge(tile_out, G_IN2 + 8)
                    for j in range(RANK_Q):
                        square(N_CQ, j, cq[:, j, :])
                if i == 9:
                    root(N_CQ, RANK_Q * P)
                if i == 10:
                    rounded(lambda j: hid_hi[:, j, :], TOK, None, h_hi, KT + 4, RANK_Q)
            act.wait_ge(sem("va_turned"), 1)
            nc.scalar.copy(va[:, 0:2, :], psum[:, 4, 0:256].rearrange("p (a b) -> p a b", b=P))
            nc.scalar.copy(va[:, 3:5, :], psum[:, 4, 256:512].rearrange("p (a b) -> p a b", b=P))
            nc.scalar.copy(va[:, 5:7, :], psum[:, 5, 0:256].rearrange("p (a b) -> p a b", b=P)).then_inc(sem("va_done"), 1)
            act.wait_ge(h_ready, HID["cq"] + RANK_Q)
            for q in range(KEYS // P):
                if q < KEYS // P - 1:
                    act.wait_ge(sem("vb_mm"), q + 1)
                else:
                    act.wait_ge(mm_done, G_VUP + 1)
                ins = nc.scalar.copy(vb[:, q, :], psum[:, (G_VUP + q) % BANKS, :])
                ins.then_inc(sem("vb_out") if q < KEYS // P - 1 else tile_out, 1)
            split(At(G_VUP + 2))
            act.sem_inc(sem("win_pt"), 1)
            with act.Fori(0, 2) as i:
                softmax("win", 16, i, SCALE_A, WIN, WIN // P,
                        sink=lambda s: col[:, bass.ds(i * 2 + (COL["sink"] + s // 8 + 4 * (s // 4 % 2)), 1)])
            act.sem_inc(sem("mla_pt"), 1)
            with act.Fori(0, 2) as i:
                split(At(G_MLA + 2, i, 4))

                def begin(s):
                    if s % 4 == 2 and s < 12:
                        split(At(G_MLA + s // 4 + 3, i, 4))
                softmax("mla", 16, i, SCALE_B, KEYS, KEYS // P, begin=begin)
            for j in range(KT):
                act.wait_ge(sem("mix_turned"), j + 1)
                nc.scalar.copy(act_hi[:, j, :], psum[:, 4 + j % BANKS, :]).then_inc(a_hi, 1)
            for j in range(KT):
                split(At(G_OUT2 + j + 2))
                act.wait_ge(tile_out, G_OUT2 + j + 1)
                square(N_FFN, j, res[:, j, :])
            act.dma_start(router, router_in).then_inc(sem("moe_in"), 16)
            act.dma_start(iota, iota_in).then_inc(sem("moe_in"), 16)
            act.dma_start(tri, tri_in).then_inc(sem("moe_in"), 16)
            root(N_FFN, D)
            for j in range(KT):
                act.wait_ge(sem("h2_gain"), j + 1)
                nc.scalar.activation(h2[:, j, :], h2[:, j, :], ACT.Identity, bias=mod[:, 24 + j, 0:1]).then_inc(sem("h2_done"), 1)
            act.wait_ge(sem("logits_mm"), 1)
            nc.scalar.copy(logits_t, psum[0:NE, 7, :]).then_inc(sem("logits_copied"), 1)
            def tok_hi(first, last):
                for m in range(first, last):
                    act.wait_ge(sem("tok_turned"), m + 1)
                    nc.scalar.copy(act_hi[:, m, :], psum[:, m % BANKS, :]).then_inc(sem("tok_hi"), 1)

            tok_hi(0, 2)
            act.wait_ge(sem("aff_sub"), 1)
            nc.scalar.activation(aff_p, aff_p, ACT.Exp).then_inc(sem("aff_exp"), 1)
            tok_hi(2, 4)
            act.wait_ge(sem("aff_done"), 1)
            nc.scalar.copy(aff_split[:, :, 0:NE], aff).then_inc(sem("aff_hi"), 1)
            tok_hi(4, 8)
            for m in range(16):
                d, half = m // 2, m % 2
                act.wait_ge(sem("gathered"), m + 1)
                nc.scalar.copy(xs[:, d, half * 512:(half + 1) * 512], psum[:, m % BANKS, :]).then_inc(sem("xs_done"), 1)
            for p in range(PAIRS):
                act.wait_ge(sem("sel_turned"), p + 1)
                nc.scalar.copy(sel_t[:, p, :], psum[:, 4 + p % 2, :]).then_inc(sem("sel_t_done"), 1)
            act.wait_ge(sem("val_done"), 1)
            with act.Fori(0, PAIRS) as i:
                for e in range(2):
                    act.wait_ge(moe_done, i * MOE_STEP + 8 * (e + 1))
                    nc.scalar.activation(gate_s[:, e, :].rearrange("p (f c) -> p f c", c=CAP), mine(2 * e, e), ACT.Silu).then_inc(sem("moe_silu"), 1)
                act.wait_ge(moe_done, i * MOE_STEP + MOE_STEP)
                for half in range(2):
                    nc.scalar.activation(ye_hi.rearrange("p a b -> p (a b)")[:, bass.ds(i * D + half * 512, 512)],
                                         psum[:, 4 + half, :], ACT.Copy,
                                         scale=val[:, bass.ds(i, 1)]).then_inc(sem("moe_y_hi"), 1)
            for j in range(KT):
                act.wait_ge(sem("x_out"), j + 1)
                square(N_FINAL, j, res[:, j, :])
            root(N_FINAL, D)

        @block.vector
        def _(dve):
            chain = Chain(dve, sem("dve_chain"))
            V = nc.vector

            def split(g):
                if g.base >= N_SPLIT:
                    return
                s = g.base % SPLIT_RING
                dve.wait_ge(hi_done, g.n(1))
                V.tensor_tensor(w_lo[:, s, :], raw[:, g.place() % RING, :], w_hi[:, s, :].bitcast(F32),
                                ALU.subtract).then_inc(lo_done, 1)

            def norm_inv(n):
                dve.wait_ge(std_done, n + 1)
                if n:
                    dve.wait_ge(bc_done, n)
                V.reciprocal(inv[:, 1, :], inv[:, 0, :]).then_inc(inv_done, 1)

            def norm_row(n, copy=False, meanwhile=None):
                if n not in IN2_INV:
                    norm_inv(n)
                if meanwhile:
                    split(meanwhile)
                dve.wait_ge(bc_done, n + 1)
                if copy:
                    chain.link(V.tensor_copy(row[:, :], row_ps))

            def acc(g, done=0):
                return psum[:, (g.base - done) % BANKS, :]

            def evac_wait(g):
                dve.wait_ge(mm_done, g.n(1))

            dve.wait_ge(const_in, 64)
            chain.link(V.memset(gsm[:, 2:8], 0.0))
            chain.link(V.memset(sum_sel[:, :, :], 0.0))
            for q in range(NQ):
                chain.link(V.memset(sum_sel[:, q, q:q + 1], 1.0))
            for k, name in enumerate(("b_i", "b_f")):
                chain.link(V.tensor_scalar(gsm[:, k:k + 1], c(name)[0:HEADS], 1.0 / GATE_CAP, None, ALU.mult))
            for j in range(KT):
                dve.wait_ge(a_hi, j + 1)
                V.scalar_tensor_tensor(out=act_lo[:, j, :], in0=res[:, j, :], scalar=normg(0, 0, j),
                                       in1=act_hi[:, j, :].bitcast(F32), op0=ALU.mult,
                                       op1=ALU.subtract).then_inc(a_ready, 1)
                if j in (3, 7):
                    split(At(j // 4))
            split(At(2))
            split(At(3))
            norm_row(0, copy=True, meanwhile=At(4))
            evac_wait(At(0))
            chain.do(V.tensor_tensor(grow[0].rearrange("p c l -> p (c l)"), psum[0:4, 0, :], row[0:4, :], ALU.mult))
            V.tensor_tensor(grow[1].rearrange("p c l -> p (c l)"), psum[32:36, 0, :], row[32:36, :],
                            ALU.mult).then_inc(tile_out, 1)

            def evac_qk(g, dst, scale):
                if g.base >= 3:
                    split(g + 2)
                evac_wait(g)
                if scale is None:
                    V.tensor_tensor(dst, acc(g), row[:, :], ALU.mult).then_inc(tile_out, 1)
                else:
                    V.scalar_tensor_tensor(out=dst, in0=acc(g), scalar=scale, in1=row[:, :], op0=ALU.mult,
                                           op1=ALU.mult).then_inc(tile_out, 1)

            for j in range(4):
                evac_qk(At(1 + j), qT[:, j, :], None)
            for j in range(4):
                evac_qk(At(5 + j), kT[:, j, :], KSCALE)
            dve.wait_ge(sem("gate_ln"), 1)

            def scan(src, a, b, op):
                s = 1
                while s < P:
                    chain.do(V.tensor_copy(a[:, :, 0:s], src[:, :, 0:s]))
                    chain.link(V.tensor_tensor(a[:, :, s:P], src[:, :, s:P], src[:, :, 0:P - s], op))
                    src, a, b = a, b, a
                    s *= 2
                return src

            def evac_v(j):
                g = At(G_V + j)
                split(g + 2)
                evac_wait(g)
                V.tensor_tensor(vT[:, j, :], acc(g), row[:, :], ALU.mult).then_inc(tile_out, 1)

            nb = scan(grow[1], grow[3], grow[2], ALU.add)
            at = [r for r in (grow[1], grow[2], grow[3]) if r is not nb][0]
            assert nb is grow[3]
            chain.link(V.scalar_tensor_tensor(out=grow[4], in0=grow[0], scalar=GATE_CAP, in1=nb,
                                              op0=ALU.mult, op1=ALU.add))
            evac_v(0)
            pm = scan(grow[4], grow[0], grow[1], ALU.max)
            assert pm is grow[0]
            evac_v(1)
            for q in range(NQ):
                m = gsm[:, 2 + q:3 + q]
                chain.link(V.tensor_scalar(grow[2][:, q, :], pm[:, q, :], m, None, ALU.max))
                if q < NQ - 1:
                    chain.link(V.tensor_tensor(gsm[:, 3 + q:4 + q], grow[2][:, q, P - 1:P], nb[:, q, P - 1:P],
                                               ALU.subtract))
            V.tensor_tensor(grow[5], grow[2], nb, ALU.subtract).then_inc(sem("gate_u"), 1)
            for j in range(2, 8):
                evac_v(j)
            for j in range(8):
                g = At(G_O + j)
                split(g + 2)
                evac_wait(g)
                V.tensor_tensor(o_sig[:, j, :], acc(g), row[:, :], ALU.mult).then_inc(tile_out, 1)
            dve.wait_ge(sem("gate_turned"), 1)
            V.tensor_copy(gcol.rearrange("p a q h -> p (a q h)"), psum[:, 7, 16:48]).then_inc(sem("gate_cols_done"), 1)
            dve.wait_ge(sem("gate_cols_done"), 1)

            for h in range(HEADS):
                dve.wait_ge(sem("u_bc"), h + 1)
                for q in range(NQ):
                    last = V.tensor_scalar(dec[:, q, :], psum[:, 6, q * P:(q + 1) * P], gcol[:, 0, q, h:h + 1],
                                           0.0, ALU.subtract, ALU.max)
                last.then_inc(sem("gap_done"), 1)
                dve.wait_ge(sem("i_bc"), h + 1)
                i_bc = psum[:, 7, :].rearrange("p (a b) -> p a b", b=P)
                chain.do(V.tensor_copy(inter_s, i_bc))
                chain.do(V.tensor_tensor(q_in, qT[:, h, :].rearrange("p (a b) -> p a b", b=P), i_bc, ALU.mult))
                dve.wait_ge(sem("dec_masked"), h + 1)
                dve.wait_ge(sem("k_turned"), h + 1)
                for q in range(NQ - 1):
                    last = V.tensor_scalar(wk[:, q, :], psum[:, 0, q * P:(q + 1) * P], dec[:, q, P - 1:P], None,
                                           ALU.mult)
                last.then_inc(sem("wk_done"), 1)
                dve.wait_ge(sem("wk_done"), h + 1)
                dve.wait_ge(sem("scores"), h + 1)
                V.tensor_tensor(dec, psum[:, 4, :].rearrange("p (a b) -> p a b", b=P), dec,
                                ALU.mult).then_inc(sem("p_done"), 1)
                chain.sync()
                for q in range(NQ - 1):
                    dve.wait_ge(sem("kv_done"), 3 * h + q + 1)
                    if q == 0:
                        V.tensor_copy(state[:, 0, :], psum[:, 5, :2 * P + 1]).then_inc(sem("state_done"), 1)
                    else:
                        dve.wait_ge(sem("state_done"), 3 * h + q)
                        V.scalar_tensor_tensor(out=state[:, q, :], in0=state[:, q - 1, :],
                                               scalar=inter_s[:, q, P - 1:P], in1=psum[:, 5, :2 * P + 1],
                                               op0=ALU.mult, op1=ALU.add).then_inc(sem("state_done"), 1)
                dve.wait_ge(sem("num_done"), h + 1)
                V.tensor_copy(num, psum[:, 1:1 + VT, :]).then_inc(sem("num_copied"), 1)
                if h == 0:
                    dve.wait_ge(sem("floor_done"), 1)
                chain.link(V.scalar_tensor_tensor(out=hsm[:, 0, :], in0=psum[:, 7, 0:NQ], scalar=-1.0,
                                                  in1=gcol[:, 1, :, h], op0=ALU.mult, op1=ALU.max))
                chain.link(V.tensor_tensor(hsm[:, 0, :], psum[:, 7, 0:NQ], hsm[:, 0, :], ALU.max))
                chain.link(V.scalar_tensor_tensor(out=hsm[:, 1, :], in0=hsm[:, 0, :], scalar=EPS, in1=hsm[:, 0, :],
                                                  op0=ALU.mult, op1=ALU.mult))
                dve.wait_ge(sem("num_sq"), h + 1)
                V.tensor_tensor(num2[:, 0, :], num2[:, 0, :], num2[:, 1, :], ALU.add).then_inc(sem("num_added"), 1)
                dve.wait_ge(sem("num_msq"), h + 1)
                chain.link(V.scalar_tensor_tensor(out=hsm[:, 2, :], in0=psum[:, 6, 8:8 + NQ],
                                                  scalar=1.0 / (VT * P), in1=hsm[:, 1, :],
                                                  op0=ALU.mult, op1=ALU.add))
                V.tensor_scalar(hsm[:, 2, :], hsm[:, 2, :], 1e35, None, ALU.min).then_inc(sem("head_var"), 1)
                dve.wait_ge(sem("head_root"), h + 1)
                chain.link(V.reciprocal(hsm[:, 4, :], hsm[:, 3, :]))
                V.tensor_tensor(diag[:, :, :], ident[:, :].unsqueeze(1).broadcast_to([P, NQ, P]),
                                hsm[:, 4, :].unsqueeze(2).broadcast_to([P, NQ, P]), ALU.mult)\
                    .then_inc(sem("head_diag"), 1)
                dve.wait_ge(sem("head_bc"), h + 1)
                dve.wait_ge(sem("num_copied"), h + 1)
                for t in range(VT):
                    chain.do(V.tensor_tensor(tmp[:, t, :], num[:, t, :], psum[:, 0, :], ALU.mult))
                chain.sync()
                for t in range(VT):
                    V.scalar_tensor_tensor(out=tmp[:, t, :], in0=tmp[:, t, :], scalar=c("g_hnorm", VT * h + t),
                                           in1=o_sig[:, VT * h + t, :], op0=ALU.mult,
                                           op1=ALU.mult).then_inc(sem("h_full"), 1)
                for t in range(VT):
                    dve.wait_ge(a_hi, 8 + VT * h + t + 1)
                    V.tensor_tensor(act_lo[:, VT * h + t, :], tmp[:, t, :],
                                    act_hi[:, VT * h + t, :].bitcast(F32), ALU.subtract).then_inc(a_ready, 1)

            dve.wait_ge(mod_done, N_MOD)
            chain.link(V.tensor_tensor(mod[:, :, :], psum[:, 3, 0:2 * N_MOD].rearrange("p (a b) -> p a b", b=2),
                                       col[:, COL["b_mod"]:COL["b_mod"] + N_MOD].unsqueeze(2).broadcast_to([P, N_MOD, 2]),
                                       ALU.add))
            for k, (first, which, name) in enumerate(((8, 0, "norm_attn"), (8, 1, "norm_attn"), (32, 0, "norm_ffn"))):
                chain.link(V.scalar_tensor_tensor(out=gain[:, k, :], in0=mod[:, first:first + 8, which], scalar=1.0,
                                                  in1=col[:, COL[name]:COL[name] + KT], op0=ALU.add, op1=ALU.mult))
            chain.link(V.tensor_scalar(sink_neg[:, :], col[:, COL["sink"]:COL["sink"] + 8], -1.0, None, ALU.mult))

            def prep(name, nxt, layer, which, glayer, gwhich, g0):
                norm_row(N_POST[name])
                xb = 8 * ("mix0", "mlp0", "mix1", "mlp1").index(name)

                def lo(j):
                    dve.wait_ge(a_hi, 8 * PREP[nxt] + j + 1)
                    V.scalar_tensor_tensor(out=act_lo[:, j, :], in0=res[:, j, :], scalar=normg(layer, which, j),
                                           in1=act_hi[:, j, :].bitcast(F32), op0=ALU.mult,
                                           op1=ALU.subtract).then_inc(a_ready, 1)

                for j in range(KT):
                    if not nxt:
                        if j == 3:
                            split(At(g0 + 1))
                        chain.link(V.scalar_tensor_tensor(out=addend_of(j), in0=y[:, j, :], scalar=normg(glayer, gwhich, j),
                                                          in1=row_ps, op0=ALU.mult, op1=ALU.mult))
                        V.tensor_tensor(res[:, j, :], res[:, j, :], addend_of(j), ALU.add).then_inc(x_ready, 1)
                        continue
                    if j >= 4:
                        dve.wait_ge(x_ready, xb + j - 3)
                    V.scalar_tensor_tensor(out=addend_of(j), in0=y[:, j, :], scalar=normg(glayer, gwhich, j),
                                           in1=row_ps, op0=ALU.mult, op1=ALU.mult).then_inc(y_ready, 1)
                    if j == 3:
                        split(At(g0 + 1))
                    if nxt and j >= 2:
                        lo(j - 2)
                if nxt:
                    lo(KT - 2)
                    lo(KT - 1)
                    split(At(g0 + 2))
                    split(At(g0 + 3))

            def evac_y(g, j, add=False, last=False):
                if not (last and j == KT - 1):
                    split(g + 2)
                evac_wait(g)
                if add:
                    V.tensor_tensor(y[:, j, :], y[:, j, :], acc(g), ALU.add).then_inc(tile_out, 1)
                else:
                    V.tensor_copy(y[:, j, :], acc(g)).then_inc(tile_out, 1)

            def modulated(t0, tiles, width, src, g, dst, done_hi, base, ready, shift=None):
                def lo(j):
                    dve.wait_ge(done_hi, base + j + 1)
                    hi, lo_ = dst(j)
                    if shift is None:
                        V.tensor_tensor(lo_, tmp[:, j % 2, :width], hi.bitcast(F32), ALU.subtract).then_inc(ready, 1)
                    else:
                        V.scalar_tensor_tensor(out=lo_, in0=tmp[:, j % 2, :width], scalar=shift(j), in1=hi.bitcast(F32),
                                               op0=ALU.add, op1=ALU.subtract).then_inc(ready, 1)

                for j in range(tiles):
                    if j >= 2:
                        dve.wait_ge(ready, base + j - 1)
                    V.scalar_tensor_tensor(out=tmp[:, j % 2, :width], in0=src(j), scalar=g(j), in1=row_ps[:, :width],
                                           op0=ALU.mult, op1=ALU.mult).then_inc(sem("t_ready"), 1)
                    if j:
                        lo(j - 1)
                lo(tiles - 1)

            def mlp_dve(g0, name):
                hb = HID[name]

                def lo(g, j, i, r):
                    n = hb + j + 1 + r
                    dve.wait_ge(h_hi, n if i is None else i * 8 + n)
                    V.tensor_tensor(hid_lo[:, j, :], sqt[:, j % 2, :], hid_hi[:, j, :].bitcast(F32),
                                    ALU.subtract).then_inc(h_ready, 1)

                def quarter(g, r, i=None, pre=None, add=True, last=False, ctx=False):
                    for j in range(8):
                        gj = g + j
                        if pre is None or j >= 3:
                            split(gj + 2)
                        if pre is not None and j == 0:
                            norm_row(pre, copy=True, meanwhile=g + 4)
                        evac_wait(gj)
                        V.scalar_tensor_tensor(out=tmp[:, j % 2, :], in0=acc(gj), scalar=0.0, in1=row[:, :],
                                               op0=ALU.max, op1=ALU.mult).then_inc(tile_out, 1)
                        if j:
                            lo(g, j - 1, i, r)
                    lo(g, 7, i, r)
                    for j in range(8):
                        if ctx and last:
                            if j == 0:
                                norm_row(N_CTX)
                            chain.link(V.scalar_tensor_tensor(out=ctx_h[:, j, :], in0=ctx_x[:, j, :], scalar=gain[:, 1, j:j + 1],
                                                              in1=row_ps[:, :CTX], op0=ALU.mult, op1=ALU.mult))
                            V.tensor_scalar(ctx_h[:, j, :], ctx_h[:, j, :], mod[:, j, 1:2], None,
                                            ALU.add).then_inc(sem("ctx_done"), 1)
                        evac_y(g + (8 + j), j, add, last)
                        if ctx and j == 6 and not last:
                            norm_inv(N_CTX)

                ctx = name == "mlp1"
                quarter(At(g0), 0, pre=N_PRE[name], add=False, ctx=ctx)
                with dve.Fori(0, 2) as i:
                    quarter(At(g0 + 16, i, 16), 8, i)
                quarter(At(g0 + 48), 24, last=True, ctx=ctx)

            for j in range(8):
                evac_y(At(G_OUT0 + j), j, last=True)
            prep("mix0", "mlp0", 0, 2, 0, 1, G_MLP0)
            mlp_dve(G_MLP0, "mlp0")
            prep("mlp0", "mix1", 1, 0, 0, 3, G_CONV)
            chain.link(V.memset(halo[:, :, 0:2], 0.0))
            for j in range(8):
                g = At(G_CONV + 3 * j)
                if j:
                    split(g + 2)
                else:
                    norm_row(N_PRE["mix1"], copy=True, meanwhile=g + 4)
                evac_wait(g)
                V.tensor_tensor(cbuf[:, 0, :], acc(g), row[:, :], ALU.mult).then_inc(tile_out, 1)
                g = g + 1
                if j:
                    split(g + 2)
                evac_wait(g)
                V.tensor_tensor(cbuf[:, 1, :], acc(g), row[:, :], ALU.mult).then_inc(tile_out, 1)
                dve.wait_ge(tile_out, g.n(1))
                u = halo[:, j % 2, :]
                chain.link(V.tensor_tensor(u[:, 2:], cbuf[:, 0, :], cbuf[:, 1, :], ALU.mult))
                chain.link(V.tensor_scalar(cbuf[:, 2, :], u[:, 2:], c("conv", 2 * KT + j), None, ALU.mult))
                for k in (1, 0):
                    chain.link(V.scalar_tensor_tensor(out=cbuf[:, 2, :], in0=u[:, k:k + TOK], scalar=c("conv", k * KT + j),
                                                      in1=cbuf[:, 2, :], op0=ALU.mult, op1=ALU.add))
                g = g + 1
                if j:
                    split(g + 2)
                evac_wait(g)
                V.tensor_tensor(cbuf[:, 1, :], acc(g), row[:, :], ALU.mult).then_inc(tile_out, 1)
                dve.wait_ge(tile_out, g.n(1))
                V.tensor_tensor(cbuf[:, 3, :], cbuf[:, 2, :], cbuf[:, 1, :], ALU.mult).then_inc(sem("conv_full"), 1)
                dve.wait_ge(h_hi, HID["mix1"] + j + 1)
                V.tensor_tensor(hid_lo[:, j, :], cbuf[:, 3, :], hid_hi[:, j, :].bitcast(F32),
                                ALU.subtract).then_inc(h_ready, 1)
            for j in range(8):
                evac_y(At(G_OUT1 + j), j, last=True)
            prep("mix1", "mlp1", 1, 2, 1, 1, G_MLP1)
            mlp_dve(G_MLP1, "mlp1")
            prep("mlp1", None, 0, 0, 1, 3, G_IN2)

            def turn(dst, src, partner, lanes, table):
                chain.do(V.tensor_tensor(dst, src, rope[:, table, :], ALU.mult))
                chain.link(V.stream_shuffle(partner, src, lanes))
                chain.link(V.tensor_tensor(partner, partner, rope[:, table + 1, :], ALU.mult))
                return V.tensor_tensor(dst, dst, partner, ALU.add)

            def soft_steps(pre, steps, i, scale, keys, o_at, half_of, sink=None, extra=None):
                n = lambda k: i * steps + k

                def finish(s):
                    b = s % SOFT
                    dve.wait_ge(sem(pre + "_exp"), n(s + 1))
                    den = soft[:, 2, b:b + 1]
                    if sink:
                        dve.wait_ge(sem(pre + "_sink"), n(s + 1))
                        chain.link(V.tensor_tensor(soft[:, 4, b:b + 1], soft[:, 2, b:b + 1], soft[:, 3, b:b + 1], ALU.add))
                        den = soft[:, 4, b:b + 1]
                    chain.link(V.reciprocal(soft[:, 5, b:b + 1], den))
                    dve.wait_ge(sem(pre + "_pv"), n(s + 1))
                    half = 64 * half_of(s)
                    V.tensor_scalar(o_tok[:, s % 4, o_at(s)], psum[:, 6, half:half + 64], soft[:, 5, b:b + 1], None,
                                    ALU.mult).then_inc(sem(pre + "_o"), 1)

                for s in range(steps):
                    dve.wait_ge(sem(pre + "_s"), n(s + 1))
                    src = psum[:, 2 * (s % 2):2 * (s % 2) + 2, :].rearrange("p a b -> p (a b)")
                    a, b = (256 if sink else 0), s % SOFT
                    chain.link(V.tensor_reduce(soft[:, 0, b:b + 1], src[:, a:a + keys], AX.X, ALU.max))
                    if sink:
                        ins = V.tensor_scalar(soft[:, 1, b:b + 1], soft[:, 0, b:b + 1], -scale, sink(s), ALU.mult, ALU.min)
                    else:
                        ins = V.tensor_scalar(soft[:, 1, b:b + 1], soft[:, 0, b:b + 1], -scale, None, ALU.mult)
                    ins.then_inc(sem(pre + "_max"), 1)
                    if extra:
                        extra(s)
                    if s >= 2:
                        finish(s - 2)
                finish(steps - 2)
                finish(steps - 1)

            norm_row(N_ATT)
            modulated(0, KT, TOK, lambda j: res[:, j, :], lambda j: gain[:, 0, j:j + 1],
                      lambda j: (act_hi[:, j, :], act_lo[:, j, :]), a_hi, 8 * PREP["att"], a_ready, lambda j: mod[:, j, 0:1])
            chain.do(V.tensor_copy(ident_b[:, :], ident[:, :]))
            chain.do(V.memset(ka[:, CTX:CTX + P], 0.0))
            chain.do(V.memset(ka[:, KEYS + P:KEYS + 2 * P], 0.0))
            chain.do(V.memset(va[:, 2:8:5, :], 0.0))
            dve.wait_ge(sem("rope_in"), 32)
            for i in range(12):
                g = At(G_IN2 + i)
                split(g + 2)
                evac_wait(g)
                ctx_ps = psum[:, 4 + i % 2, 0:CTX]
                if i < 2:
                    V.tensor_copy(ckv[:, i, 0:CTX], ctx_ps)
                    V.tensor_copy(ckv[:, i, CTX:KEYS], acc(g)).then_inc(tile_out, 1)
                elif i == 2:
                    V.tensor_copy(kr[:, 0:CTX], ctx_ps)
                    V.tensor_copy(turn_raw, acc(g)).then_inc(tile_out, 1)
                    dve.wait_ge(tile_out, g.n(1))
                    chain.link(turn(kr[:, CTX:KEYS], turn_raw, turn_sh, ROPE_B, 2))
                elif i == 3:
                    V.tensor_copy(ka[:, 0:CTX], ctx_ps)
                    V.tensor_copy(turn_raw, acc(g)).then_inc(tile_out, 1)
                    dve.wait_ge(tile_out, g.n(1))
                    chain.link(turn(ka[:, CTX + P:KEYS + P], turn_raw, turn_sh, ROPE_A, 0))
                elif i == 4:
                    V.tensor_copy(va_t[:, 0:CTX], ctx_ps)
                    V.tensor_copy(va_t[:, CTX:KEYS], acc(g)).then_inc(tile_out, 1)
                elif i < 8:
                    V.tensor_copy(cq[:, i - 5, :], acc(g)).then_inc(tile_out, 1)
                else:
                    V.tensor_copy(turn_raw, acc(g)).then_inc(tile_out, 1)
                    dve.wait_ge(tile_out, g.n(1))
                    chain.link(turn(qa[:, i - 8, :], turn_raw, turn_sh, ROPE_A, 0))
                for n, at in ((N_CKV_C, 4), (N_CKV, 6), (N_CQ, 9)):
                    if i == at:
                        norm_inv(n)
                if i == 5:
                    norm_row(N_CKV_C)
                    modulated(KT, RANK_KV, CTX, lambda j: ckv[:, j, 0:CTX], lambda j: c("kv_norm", j),
                              lambda j: (latent_hi[:, j, 0:CTX], latent_lo[:, j, 0:CTX]), h_hi, HID["ckv_c"], h_ready)
                if i == 7:
                    norm_row(N_CKV)
                    modulated(KT + 2, RANK_KV, TOK, lambda j: ckv[:, j, CTX:KEYS], lambda j: c("kv_norm", j),
                              lambda j: (latent_hi[:, j, CTX:KEYS], latent_lo[:, j, CTX:KEYS]), h_hi, HID["ckv"], h_ready)
                if i == 10:
                    norm_row(N_CQ)
                    modulated(KT + 4, RANK_Q, TOK, lambda j: cq[:, j, :], lambda j: c("q_norm", j),
                              lambda j: (hid_hi[:, j, :], hid_lo[:, j, :]), h_hi, HID["cq"], h_ready)
            split(At(G_VUP + 2))
            dve.sem_inc(sem("win_o"), 1)
            with dve.Fori(0, 2) as i:
                dve.wait_ge(sem("win_o"), i * 16 + 1)
                V.tensor_copy(q_stage.rearrange("p a b -> p (a b)"),
                              qa.rearrange("p a b -> p (a b)")[:, bass.ds(i * 2 * TOK, 2 * TOK)]).then_inc(sem("q_staged"), 1)
                with chain.inside(i, 3 * 16):
                    soft_steps("win", 16, i, SCALE_A, WIN, lambda s: bass.ds(i * 2 * P + 64 * (s // 4), 64),
                               lambda s: s // 4 % 2,
                               sink=lambda s: sink_neg[:, bass.ds(i * 2 + (s // 8 + 4 * (s // 4 % 2)), 1)])
            chain.after(2)
            for b in range(2):
                last = V.tensor_copy(kh[64:128, b, :], kr[64:128, :])
            last.then_inc(sem("kr_copied"), 1)
            dve.sem_inc(sem("mla_o"), 1)
            with dve.Fori(0, 2) as i:
                with chain.inside(i, 2 * 16 + 3 * 4):
                    def part(hh, k):
                        g = At(G_MLA + hh, i, 4)
                        bank = part_bank(hh, k)
                        if k < 2:
                            dve.wait_ge(sem("part_mm"), i * 8 + (2 * hh + k + 1))
                        else:
                            dve.wait_ge(mm_done, g.n(1))
                        if k == 0:
                            turn(qh[:, hh % 2, :], psum[:, bank, :], tmp[:, 0, :], ROPE_B, 2).then_inc(sem("part_out"), 1)
                        elif k == 1:
                            V.tensor_copy(kh[0:64, hh % 2, 0:TOK], psum[0:64, bank, :]).then_inc(sem("part_out"), 1)
                        else:
                            V.tensor_copy(kh[0:64, hh % 2, TOK:KEYS], psum[0:64, bank, 0:KEYS - TOK]).then_inc(tile_out, 1)
                            split(g + 2)

                    for k in range(3):
                        part(0, k)

                    def extra(s):
                        if s % 4 < 3 and s < 12:
                            part(s // 4 + 1, s % 4)
                    soft_steps("mla", 16, i, SCALE_B, KEYS, lambda s: bass.ds(i * 256 + 512 + 64 * (s // 4), 64),
                               lambda s: s // 4 % 2,
                               extra=extra)
            chain.after(2)
            for j in range(KT):
                dve.wait_ge(a_hi, 8 * PREP["out2"] + j + 1)
                V.tensor_tensor(act_lo[:, j, :], psum[:, 4 + j % BANKS, :], act_hi[:, j, :].bitcast(F32),
                                ALU.subtract).then_inc(a_ready, 1)
            for j in range(KT):
                g = At(G_OUT2 + j)
                split(g + 2)
                evac_wait(g)
                V.scalar_tensor_tensor(out=res[:, j, :], in0=acc(g), scalar=mod[:, 16 + j, 0:1], in1=res[:, j, :],
                                       op0=ALU.mult, op1=ALU.add).then_inc(tile_out, 1)
            norm_row(N_FFN)
            for j in range(KT):
                V.scalar_tensor_tensor(out=h2[:, j, :], in0=res[:, j, :], scalar=gain[:, 2, j:j + 1], in1=row_ps,
                                       op0=ALU.mult, op1=ALU.mult).then_inc(sem("h2_gain"), 1)
            dve.wait_ge(sem("moe_in"), 48)
            chain.do(V.tensor_copy(tri_b, tri))
            chain.do(V.tensor_copy(ones_b, ones[:, :]))
            def tok_lo(first, last):
                for m in range(first, last):
                    dve.wait_ge(sem("tok_hi"), m + 1)
                    V.tensor_tensor(act_lo[:, m, :], psum[:, m % BANKS, :], act_hi[:, m, :].bitcast(F32),
                                    ALU.subtract).then_inc(sem("tok_lo"), 1)

            dve.wait_ge(sem("logits"), 1)
            logits = psum[:, 5, 0:NQ * NE].rearrange("p (a b) -> p a b", b=NE)
            wide = lambda v: v.unsqueeze(2).broadcast_to([P, NQ, NE])
            chain.link(V.tensor_reduce(e_small[:, 0, :], logits, AX.X, ALU.max))
            V.tensor_tensor(aff_p, logits, wide(e_small[:, 0, :]), ALU.subtract).then_inc(sem("aff_sub"), 1)
            tok_lo(0, 2)
            dve.wait_ge(sem("aff_exp"), 1)
            chain.link(V.tensor_reduce(e_small[:, 0, :], aff_p, AX.X, ALU.add))
            chain.link(V.reciprocal(e_small[:, 1, :], e_small[:, 0, :]))
            V.tensor_tensor(aff, aff_p, wide(e_small[:, 1, :]), ALU.mult).then_inc(sem("aff_done"), 1)
            tok_lo(2, 4)

            dve.wait_ge(sem("aff_turned"), 1)
            chain.link(V.tensor_copy(aff_t[0], psum[0:NE, 4, :]))
            for r in range(CAP // 8):
                chain.link(V.max(top8[:, :], aff_t[r % 2]))
                chain.link(V.match_replace(aff_t[(r + 1) % 2], top8[:, :], aff_t[r % 2], -1.0))
            V.tensor_scalar(aff_t[1], aff_t[0], 0.0, None, ALU.is_lt).then_inc(sem("chosen"), 1)
            tok_lo(4, 5)
            dve.wait_ge(sem("msk_turned"), 1)
            chain.do(V.tensor_copy(msk_b, psum[:, 5, 0:NQ * NE].rearrange("p (a b) -> p a b", b=NE)))
            V.tensor_copy(msk, psum[:, 5, 0:NQ * NE].rearrange("p (a b) -> p a b", b=NE)).then_inc(sem("msk_done"), 1)
            dve.wait_ge(sem("msk_done"), 1)
            tok_lo(5, 8)
            dve.wait_ge(sem("counted"), 1)
            chain.link(V.tensor_tensor(aff_p, psum[:, 6, 0:NQ * NE].rearrange("p (a b) -> p a b", b=NE), msk, ALU.mult))
            chain.link(V.tensor_scalar(aff_p, aff_p, 1.0, None, ALU.subtract))
            for q in range(NQ):
                V.tensor_tensor(sel_s[:, 2 * q:2 * q + 2, :].rearrange("p a (e c) -> p (a e) c", c=CAP),
                                       iota.unsqueeze(1).broadcast_to([P, NE, CAP]),
                                aff_p[:, q, :].unsqueeze(2).broadcast_to([P, NE, CAP]),
                                ALU.is_equal).then_inc(sem("sel_done"), 1)
            dve.wait_ge(sem("aff_hi"), 1)
            V.tensor_tensor(aff_split[:, :, NE:], aff, aff_split[:, :, 0:NE].bitcast(F32),
                            ALU.subtract).then_inc(sem("aff_lo"), 1)
            dve.wait_ge(sem("val_mm"), 1)
            chain.link(V.tensor_copy(val_parts, psum[:, 7, 0:PAIRS * 2 * NE]))
            for e in range(2):
                rows = slice(e * CAP, (e + 1) * CAP)
                end = (PAIRS - 1) * (2 * NE + 2) + e + 1
                last = V.tensor_tensor(val[rows, :], val_parts[rows, e:end:2 * NE + 2],
                                       val_parts[rows, NE + e:NE + end:2 * NE + 2], ALU.add)
            last.then_inc(sem("val_done"), 1)
            dve.sem_inc(sem("moe_h"), 1)
            dve.sem_inc(sem("moe_y"), 1)
            with dve.Fori(0, PAIRS) as i:
                for e in range(2):
                    dve.wait_ge(sem("moe_silu"), i * 2 + (e + 1))
                    V.tensor_tensor(h_e[:, e, :].rearrange("p (f c) -> p f c", c=CAP),
                                    gate_s[:, e, :].rearrange("p (f c) -> p f c", c=CAP), mine(2 * e + 1, e),
                                    ALU.mult).then_inc(sem("moe_h"), 1)
                for half in range(2):
                    dve.wait_ge(sem("moe_y_hi"), i * 2 + (half + 1))
                    at = bass.ds(i * D + half * 512, 512)
                    V.scalar_tensor_tensor(out=ye_lo.rearrange("p a b -> p (a b)")[:, at], in0=psum[:, 4 + half, :],
                                           scalar=val[:, bass.ds(i, 1)],
                                           in1=ye_hi.rearrange("p a b -> p (a b)")[:, at].bitcast(F32),
                                           op0=ALU.mult, op1=ALU.subtract).then_inc(sem("moe_y"), 1)
            for j in range(KT):
                dve.wait_ge(sem("scattered"), j + 1)
                V.scalar_tensor_tensor(out=res[:, j, :], in0=psum[:, j % BANKS, :], scalar=mod[:, 40 + j, 0:1],
                                       in1=res[:, j, :], op0=ALU.mult, op1=ALU.add).then_inc(sem("x_out"), 1)
            norm_row(N_FINAL)
            dve.wait_ge(sem("x_out"), KT)
            for j in range(KT):
                V.scalar_tensor_tensor(out=res[:, j, :], in0=res[:, j, :], scalar=c("norm_final", j), in1=row_ps,
                                       op0=ALU.mult, op1=ALU.mult).then_inc(sem("final"), 1)


def tiles_of(w, pad=SLOT):
    k, n = w.shape
    t = w.reshape(k // P, P, n // P, P).transpose(2, 1, 0, 3).reshape(n // P, P, k // P * P)
    return t


def columns(w, places):
    out = np.zeros((w.shape[0], P), w.dtype)
    for at, cols in places:
        out[:, at:at + len(cols)] = w[:, cols]
    return out


def layout(v):
    v = {k: np.asarray(a) for k, a in v.items()}
    f = np.float32

    def feat(a):
        return np.ascontiguousarray(a.reshape(-1, P).T)

    parts = []
    w0 = v["w_in_mlstm"][0]
    parts.append(tiles_of(columns(w0, [(0, range(3072, 3076)), (32, range(3076, 3080))])))
    parts.append(tiles_of(w0[:, :3072]))
    parts.append(tiles_of(v["w_out_mlstm"][0]))

    def mlp(l):
        up, down = v["w_mlp_up"][l], v["w_mlp_down"][l]
        for q in range(4):
            parts.append(tiles_of(up[:, q * D:(q + 1) * D]))
            parts.append(tiles_of(down[q * D:(q + 1) * D]))

    mlp(0)
    wc = tiles_of(v["w_in_conv"][0])
    parts.append(np.stack([wc[8:16], wc[16:24], wc[0:8]], 1).reshape(24, P, SLOT))
    parts.append(tiles_of(v["w_out_conv"][0]))
    mlp(1)
    w2 = v["w_in_2"][0]
    r = lambda a, n: list(range(a, a + n))
    for places in ([[(0, r(1152, 128))], [(0, r(1280, 128))], [(64, r(1408, 32))], [(0, r(512, 128))], [(0, r(640, 128))]]
                   + [[(0, r(768 + 128 * j, 128))] for j in range(3)]
                   + [[(0, r(64 * j, 64)), (64, r(64 * (j + 4), 64))] for j in range(4)]):
        parts.append(tiles_of(columns(w2, places)))
    kv = v["w_kv_up_2"][0].reshape(256, 8, 128)
    wv = kv[:, :, 64:].reshape(2, P, 512).transpose(1, 0, 2).reshape(1, P, SLOT)
    parts.append(wv)
    qu = v["w_q_up_2"][0].reshape(384, 8, 96)
    heads = np.zeros((8, P, SLOT), f)
    for h in range(8):
        heads[h, :, :384].reshape(P, 3, P)[:, :, :96] = qu[:, h].reshape(3, P, 96).transpose(1, 0, 2)
        heads[h, :, 384:640].reshape(P, 2, P)[:, :, :64] = kv[:, h, :64].reshape(2, P, 64).transpose(1, 0, 2)
    parts.append(heads)
    wo = v["w_out_2"][0]
    order = sum([r(64 * j, 64) + r(64 * (j + 4), 64) for j in range(4)], []) + r(512, 512)
    parts.append(tiles_of(wo[order]))
    wg, wu, wd = v["w_gate_2"][0], v["w_up_2"][0], v["w_down_2"][0]
    for p in range(PAIRS):
        for e in (2 * p, 2 * p + 1):
            parts += [tiles_of(wg[e]), tiles_of(wu[e])]
        for e in (2 * p, 2 * p + 1):
            parts.append(wd[e].reshape(FT, P, D))
    dense = np.concatenate(parts)
    stream = np.concatenate([dense[:G_AHEAD], tiles_of(v["w_mod_2"][0]), dense[G_AHEAD:]])
    assert stream.shape == (N_TILES, P, SLOT), stream.shape

    def pcol(a):
        out = np.zeros((P, 1), f)
        out[:len(a), 0] = a
        return out

    cols = np.concatenate([
        feat(v["norm_g"]), feat(v["g_hnorm"]), feat(v["w_conv"][0]), feat(v["b_mod_2"]), feat(v["norm_attn_2"]),
        feat(v["norm_ffn_2"]), feat(v["norm_final_2"]), feat(v["q_norm_2"]), feat(v["kv_norm_2"]),
        np.stack([feat(v["c_2"]), feat(v["c_ctx_2"])], 2).reshape(P, 2 * KT),
        np.broadcast_to(v["sink_2"], (P, 8)), pcol(v["b_gates_mlstm"][0, :4]), pcol(v["b_gates_mlstm"][0, 4:]),
        np.full((P, 1), EPS, f)], 1)

    pos = np.arange(TOK)
    def table(lanes, dim):
        half, nf = dim // 2, dim // 4
        inv = (np.float32(10000.0) ** (-np.arange(nf, dtype=f) / f(nf))).astype(f)
        cos, sin = np.ones((P, TOK), f), np.zeros((P, TOK), f)
        for p0 in lanes:
            for d in range(dim):
                where = (pos // 64 if d < half else pos % 64).astype(f)
                ang = where * inv[d % half % nf]
                cos[p0 + d] = np.cos(ang)
                sin[p0 + d] = np.sin(ang) * (-1 if d % half < nf else 1)
        return cos, sin
    rope = np.stack(table((0, 64), 64) + table((64,), 32), 1)
    t, s = np.arange(P)[:, None], np.arange(3 * P)[None] - P
    near = np.abs(t - s) <= P
    mask = np.stack([near & (s >= 0), near, near & (s < P)], 1)
    mask = np.where(mask, 0, -BIG).astype(mybir.dt.np(BF16))
    sel = np.zeros((HEADS, HEADS, P), f)
    for h in range(HEADS):
        sel[h, h] = 1
    return {
        "x": v["x"][0].T.reshape(KT, P, TOK).transpose(1, 0, 2), "ctx_in": v["ctx_2"][0].T.reshape(KT, P, CTX).transpose(1, 0, 2),
        "cols": cols, "ident_in": np.eye(P, dtype=f), "ones_in": np.ones((P, P), f), "sel_in": sel,
        "rope_in": rope, "mask_in": mask, "iota_in": np.broadcast_to(np.arange(CAP, dtype=f), (P, CAP)),
        "tri_in": np.triu(np.ones((P, P), f)), "router_in": v["w_router_2"][0].reshape(KT, P, NE).transpose(1, 0, 2),
        "stream": stream,
    }


def kernel(**inputs):
    import concourse.bacc as bacc
    from concourse.bass_utils import run_bass_kernel_spmd

    arrays = {k: np.ascontiguousarray(a) for k, a in layout(inputs).items()}
    nc = bacc.Bacc("TRN2", target_bir_lowering=False, num_devices=1)
    args = {k: nc.dram_tensor(k, a.shape, mybir.dt.from_np(a.dtype), kind="ExternalInput").ap() for k, a in arrays.items()}
    args["out"] = nc.dram_tensor("out", (P, KT, TOK), F32, kind="ExternalOutput").ap()
    build(nc, **args)
    got = run_bass_kernel_spmd(nc, [arrays], core_ids=[0]).results[0]["out"]
    return np.ascontiguousarray(np.asarray(got).transpose(1, 0, 2).reshape(D, TOK).T)[None]
```
